# Optimizing a Trainium2 kernel written in Bass

```python
import numpy as np
import jax
import jax.numpy as jnp
from jax import lax

D_MODEL = 1024
BATCH = 1
SEQ = 128
DEPTH = 2
DEC_BATCH = 1
DEC_SEQ = 512
PAST_LEN = 128

GRID_W = 64
HEAD_DIM = 64
MLA_HEADS = 6
MLA_Q_LORA = 256
MLA_KV_LORA = 128
MLA_NOPE = 64
MLA_ROPE = 32
MLA_V = 64
NA_HEADS = 4
NA_WIN_ROWS = 8
NA_WIN_COLS = 16
GQA_HEADS = 6
GQA_KV_HEADS = 2
MIX_W = MLA_HEADS * MLA_V + NA_HEADS * HEAD_DIM + GQA_HEADS * HEAD_DIM
D_FF = -(-8 * D_MODEL // (3 * 256)) * 256
ROPE_THETA = 10000.0
Q_BLOCK = 128
EPS = 1e-6
NEG_INF = -1e30
OFF_CKV = MLA_Q_LORA
OFF_KROPE = OFF_CKV + MLA_KV_LORA
OFF_NA = OFF_KROPE + MLA_ROPE
OFF_GQA = OFF_NA + 3 * NA_HEADS * HEAD_DIM
OFF_GK = OFF_GQA + GQA_HEADS * HEAD_DIM
OFF_GV = OFF_GK + GQA_KV_HEADS * HEAD_DIM
IN_COLS = OFF_GV + GQA_KV_HEADS * HEAD_DIM

kernel_name = 'hybrid_mla_natten_gqa_diffusion_step'

def rms_norm(x, g):
    xf = x.astype(jnp.float32)
    y = xf * lax.rsqrt(jnp.mean(xf * xf, axis=-1, keepdims=True) + EPS)
    return (y * g.astype(jnp.float32)).astype(x.dtype)

def adaln(cond, w_ada, b_ada):
    m = jax.nn.silu(cond) @ w_ada + b_ada
    return jnp.split(m[:, None, :], 6, axis=-1)

def modulate(x, g, shift, scale):
    return rms_norm(x, g) * (1 + scale) + shift

def swiglu(h, w_gate, w_up, w_down):
    return (jax.nn.silu(h @ w_gate) * (h @ w_up)) @ w_down

def axial_rope_tables(n_tokens, rot_dim):
    t = jnp.arange(n_tokens)
    row = (t // GRID_W).astype(jnp.float32)
    col = (t % GRID_W).astype(jnp.float32)
    axis_dim = rot_dim // 2
    inv_freq = ROPE_THETA ** (-jnp.arange(0, axis_dim, 2, dtype=jnp.float32) / axis_dim)
    ang_r = row[:, None] * inv_freq
    ang_c = col[:, None] * inv_freq
    ang = jnp.concatenate([ang_r, ang_r, ang_c, ang_c], axis=-1)
    return jnp.cos(ang), jnp.sin(ang)

def apply_rope(x, cos, sin):
    x1, x2, x3, x4 = jnp.split(x, 4, axis=-1)
    rot = jnp.concatenate([-x2, x1, -x4, x3], axis=-1)
    if x.ndim == 4:
        cos, sin = cos[:, None, :], sin[:, None, :]
    return (x * cos + rot * sin).astype(x.dtype)

def blocked_attention(q, k, v):
    b, s, h, dk = q.shape
    g = k.shape[2]
    rep = h // g
    nb = s // Q_BLOCK
    qb = q.reshape(b, nb, Q_BLOCK, g, rep, dk).transpose(1, 0, 2, 3, 4, 5)
    scale = dk ** -0.5

    def one_block(qblk):
        sc = jnp.einsum('bqgrd,btgd->bgrqt', qblk, k).astype(jnp.float32) * scale
        p = jax.nn.softmax(sc, axis=-1).astype(v.dtype)
        return jnp.einsum('bgrqt,btgd->bqgrd', p, v)

    o = lax.map(one_block, qb)
    return o.transpose(1, 0, 2, 3, 4, 5).reshape(b, s, h, v.shape[-1])

def mixer_inputs(h, w_in, mla_q_norm_g, mla_kv_norm_g, w_q_up, gqa_q_norm_g, gqa_k_norm_g):
    b, s, _ = h.shape
    z = h @ w_in
    c_q = rms_norm(z[..., :OFF_CKV], mla_q_norm_g)
    c_kv = rms_norm(z[..., OFF_CKV:OFF_KROPE], mla_kv_norm_g)
    k_rope = z[..., OFF_KROPE:OFF_NA]
    q_mla = (c_q @ w_q_up).reshape(b, s, MLA_HEADS, MLA_NOPE + MLA_ROPE)
    na = z[..., OFF_NA:OFF_GQA].reshape(b, s, 3, NA_HEADS, HEAD_DIM)
    gq = rms_norm(z[..., OFF_GQA:OFF_GK].reshape(b, s, GQA_HEADS, HEAD_DIM), gqa_q_norm_g)
    gk = rms_norm(z[..., OFF_GK:OFF_GV].reshape(b, s, GQA_KV_HEADS, HEAD_DIM), gqa_k_norm_g)
    gv = z[..., OFF_GV:].reshape(b, s, GQA_KV_HEADS, HEAD_DIM)
    return q_mla, c_kv, k_rope, na[:, :, 0], na[:, :, 1], na[:, :, 2], gq, gk, gv

def mla_keys_values(c_kv, k_rope, w_kv_up):
    b, t, _ = c_kv.shape
    kv = (c_kv @ w_kv_up).reshape(b, t, MLA_HEADS, MLA_NOPE + MLA_V)
    k_pe = jnp.broadcast_to(k_rope[:, :, None, :], (b, t, MLA_HEADS, MLA_ROPE))
    return jnp.concatenate([kv[..., :MLA_NOPE], k_pe], axis=-1), kv[..., MLA_NOPE:]

def na_tables(rows):
    kr = min(NA_WIN_ROWS, rows)
    kc = NA_WIN_COLS
    kbw = 2 * kc
    ncb = GRID_W // kc
    r = np.arange(rows)
    key_rows = np.clip(r - kr // 2, 0, rows - kr)[:, None] + np.arange(kr)
    blk_start = np.clip(np.arange(ncb) * kc - kc // 2, 0, GRID_W - kbw)
    key_cols = blk_start[:, None] + np.arange(kbw)
    q_cols = np.arange(ncb)[:, None] * kc + np.arange(kc)
    win_start = np.clip(q_cols - kc // 2, 0, GRID_W - kc)
    idx = (key_rows[:, None, :, None] * GRID_W + key_cols[None, :, None, :]).reshape(-1)
    inside = (key_cols[:, None, :] >= win_start[..., None]) & (key_cols[:, None, :] < win_start[..., None] + kc)
    mask = np.broadcast_to(inside[:, :, None, :], (ncb, kc, kr, kbw)).reshape(ncb, kc, kr * kbw)
    drow = key_rows - r[:, None] + NA_WIN_ROWS - 1
    dcol = np.clip(key_cols[:, None, :] - q_cols[..., None], 1 - kc, kc - 1) + kc - 1
    return idx, mask, drow, dcol, kr

def neighbourhood_attention(q, k, v, k_ctx, v_ctx, rpb):
    b, s, h, d = q.shape
    rows = s // GRID_W
    ncb = GRID_W // NA_WIN_COLS
    idx, mask, drow, dcol, kr = na_tables(rows)
    kb = kr * 2 * NA_WIN_COLS
    qg = q.reshape(b, rows, ncb, NA_WIN_COLS, h, d)
    kg = jnp.take(k, idx, axis=1).reshape(b, rows, ncb, kb, h, d)
    vg = jnp.take(v, idx, axis=1).reshape(b, rows, ncb, kb, h, d)
    bias = rpb[:, drow[:, None, None, :, None], dcol[None, :, :, None, :]]
    bias = bias.reshape(h, rows, ncb, NA_WIN_COLS, kb).astype(jnp.float32)
    scale = d ** -0.5
    s_loc = jnp.einsum('brnqhd,brnkhd->bhrnqk', qg, kg).astype(jnp.float32) * scale + bias[None]
    s_loc = jnp.where(mask[None, None, None], s_loc, NEG_INF)
    s_ctx = jnp.einsum('brnqhd,bthd->bhrnqt', qg, k_ctx).astype(jnp.float32) * scale
    p = jax.nn.softmax(jnp.concatenate([s_loc, s_ctx], axis=-1), axis=-1).astype(v.dtype)
    o = (jnp.einsum('bhrnqk,brnkhd->brnqhd', p[..., :kb], vg)
         + jnp.einsum('bhrnqt,bthd->brnqhd', p[..., kb:], v_ctx))
    return o.reshape(b, s, h, d)

def mix_out(o_mla, o_na, o_gqa, w_out):
    b, s = o_mla.shape[:2]
    o = jnp.concatenate([o_mla.reshape(b, s, -1), o_na.reshape(b, s, -1), o_gqa.reshape(b, s, -1)], axis=-1)
    return o @ w_out

def setup_inputs(seed: int = 0) -> dict:
    key = jax.random.key(seed)
    ks = jax.random.split(key, 32)
    f32 = jnp.float32

    def nrm(k, shape, scale=1.0):
        return jax.random.normal(k, shape, f32) * scale

    def gain(k, shape):
        return 1.0 + 0.02 * jax.random.normal(k, shape, f32)

    return {
        'x_prompt': nrm(ks[0], (BATCH, SEQ, D_MODEL)),
        'x_sample': nrm(ks[1], (DEC_BATCH, DEC_SEQ, D_MODEL)),
        'cache_mla_ckv': nrm(ks[2], (DEC_BATCH, DEPTH, PAST_LEN, MLA_KV_LORA)),
        'cache_mla_krope': nrm(ks[3], (DEC_BATCH, DEPTH, PAST_LEN, MLA_ROPE)),
        'cache_na_k': nrm(ks[4], (DEC_BATCH, DEPTH, PAST_LEN, NA_HEADS, HEAD_DIM)),
        'cache_na_v': nrm(ks[5], (DEC_BATCH, DEPTH, PAST_LEN, NA_HEADS, HEAD_DIM)),
        'cache_gqa_k': nrm(ks[6], (DEC_BATCH, DEPTH, PAST_LEN, GQA_KV_HEADS, HEAD_DIM)),
        'cache_gqa_v': nrm(ks[7], (DEC_BATCH, DEPTH, PAST_LEN, GQA_KV_HEADS, HEAD_DIM)),
        'c': nrm(ks[8], (DEC_BATCH, D_MODEL)),
        'c_ctx': nrm(ks[9], (D_MODEL,)),
        'w_ada': nrm(ks[10], (DEPTH, D_MODEL, 6 * D_MODEL), D_MODEL ** -0.5),
        'b_ada': nrm(ks[11], (DEPTH, 6 * D_MODEL), 0.02),
        'norm_mix_g': gain(ks[12], (DEPTH, D_MODEL)),
        'norm_ffn_g': gain(ks[13], (DEPTH, D_MODEL)),
        'w_in': nrm(ks[14], (DEPTH, D_MODEL, IN_COLS), D_MODEL ** -0.5),
        'mla_q_norm_g': gain(ks[15], (DEPTH, MLA_Q_LORA)),
        'mla_kv_norm_g': gain(ks[16], (DEPTH, MLA_KV_LORA)),
        'w_q_up': nrm(ks[17], (DEPTH, MLA_Q_LORA, MLA_HEADS * (MLA_NOPE + MLA_ROPE)), MLA_Q_LORA ** -0.5),
        'w_kv_up': nrm(ks[18], (DEPTH, MLA_KV_LORA, MLA_HEADS * (MLA_NOPE + MLA_V)), MLA_KV_LORA ** -0.5),
        'na_rpb': nrm(ks[19], (DEPTH, NA_HEADS, 2 * NA_WIN_ROWS - 1, 2 * NA_WIN_COLS - 1), 0.1),
        'gqa_q_norm_g': gain(ks[20], (DEPTH, HEAD_DIM)),
        'gqa_k_norm_g': gain(ks[21], (DEPTH, HEAD_DIM)),
        'w_out': nrm(ks[22], (DEPTH, MIX_W, D_MODEL), MIX_W ** -0.5),
        'w_gate': nrm(ks[23], (DEPTH, D_MODEL, D_FF), D_MODEL ** -0.5),
        'w_up': nrm(ks[24], (DEPTH, D_MODEL, D_FF), D_MODEL ** -0.5),
        'w_down': nrm(ks[25], (DEPTH, D_FF, D_MODEL), D_FF ** -0.5),
        'final_norm_g': gain(ks[26], (D_MODEL,)),
    }

def reference(x_prompt, x_sample, cache_mla_ckv, cache_mla_krope, cache_na_k, cache_na_v,
              cache_gqa_k, cache_gqa_v, c, c_ctx, w_ada, b_ada, norm_mix_g, norm_ffn_g, w_in,
              mla_q_norm_g, mla_kv_norm_g, w_q_up, w_kv_up, na_rpb, gqa_q_norm_g, gqa_k_norm_g,
              w_out, w_gate, w_up, w_down, final_norm_g):
    xp = x_prompt
    ckv_l, krope_l, nak_l, nav_l, gk_l, gv_l = [], [], [], [], [], []
    for l in range(DEPTH):
        sh_a, sc_a, g_a, sh_f, sc_f, g_f = adaln(c_ctx[None, :], w_ada[l], b_ada[l])
        h = modulate(xp, norm_mix_g[l], sh_a, sc_a)
        q_mla, c_kv, k_rope, na_q, na_k, na_v, gq, gk, gv = mixer_inputs(
            h, w_in[l], mla_q_norm_g[l], mla_kv_norm_g[l], w_q_up[l], gqa_q_norm_g[l], gqa_k_norm_g[l])
        k_m, v_m = mla_keys_values(c_kv, k_rope, w_kv_up[l])
        o_mla = blocked_attention(q_mla, k_m, v_m)
        o_na = blocked_attention(na_q, na_k, na_v)
        o_gqa = blocked_attention(gq, gk, gv)
        xp = xp + g_a * mix_out(o_mla, o_na, o_gqa, w_out[l])
        xp = xp + g_f * swiglu(modulate(xp, norm_ffn_g[l], sh_f, sc_f), w_gate[l], w_up[l], w_down[l])
        ckv_l.append(c_kv)
        krope_l.append(k_rope)
        nak_l.append(na_k)
        nav_l.append(na_v)
        gk_l.append(gk)
        gv_l.append(gv)
    y_prompt = rms_norm(xp, final_norm_g)
    new_mla_ckv = jnp.stack(ckv_l, axis=1)
    new_mla_krope = jnp.stack(krope_l, axis=1)
    new_na_k = jnp.stack(nak_l, axis=1)
    new_na_v = jnp.stack(nav_l, axis=1)
    new_gqa_k = jnp.stack(gk_l, axis=1)
    new_gqa_v = jnp.stack(gv_l, axis=1)

    xs = x_sample
    s_lat = xs.shape[1]
    cos_m, sin_m = axial_rope_tables(s_lat, MLA_ROPE)
    cos_g, sin_g = axial_rope_tables(s_lat, HEAD_DIM)
    for l in range(DEPTH):
        sh_a, sc_a, g_a, sh_f, sc_f, g_f = adaln(c, w_ada[l], b_ada[l])
        h = modulate(xs, norm_mix_g[l], sh_a, sc_a)
        q_mla, c_kv, k_rope, na_q, na_k, na_v, gq, gk, gv = mixer_inputs(
            h, w_in[l], mla_q_norm_g[l], mla_kv_norm_g[l], w_q_up[l], gqa_q_norm_g[l], gqa_k_norm_g[l])
        q_mla = jnp.concatenate([q_mla[..., :MLA_NOPE], apply_rope(q_mla[..., MLA_NOPE:], cos_m, sin_m)], axis=-1)
        k_lat, v_lat = mla_keys_values(c_kv, apply_rope(k_rope, cos_m, sin_m), w_kv_up[l])
        k_ctx, v_ctx = mla_keys_values(cache_mla_ckv[:, l], cache_mla_krope[:, l], w_kv_up[l])
        o_mla = blocked_attention(q_mla, jnp.concatenate([k_lat, k_ctx], axis=1),
                                  jnp.concatenate([v_lat, v_ctx], axis=1))
        o_na = neighbourhood_attention(na_q, na_k, na_v, cache_na_k[:, l], cache_na_v[:, l], na_rpb[l])
        o_gqa = blocked_attention(apply_rope(gq, cos_g, sin_g),
                                  jnp.concatenate([apply_rope(gk, cos_g, sin_g), cache_gqa_k[:, l]], axis=1),
                                  jnp.concatenate([gv, cache_gqa_v[:, l]], axis=1))
        xs = xs + g_a * mix_out(o_mla, o_na, o_gqa, w_out[l])
        xs = xs + g_f * swiglu(modulate(xs, norm_ffn_g[l], sh_f, sc_f), w_gate[l], w_up[l], w_down[l])
    y_sample = rms_norm(xs, final_norm_g)

    return (y_prompt, y_sample, new_mla_ckv, new_mla_krope, new_na_k, new_na_v, new_gqa_k, new_gqa_v)


_drawn_inputs = setup_inputs


def setup_inputs(seed=0):
    import zlib

    import numpy as np

    out = dict(_drawn_inputs(seed))
    spreads = {}
    factors = {'cache_mla_ckv': 3.242,
     'cache_mla_krope': 5.783,
     'cache_gqa_k': 3.787,
     'cache_gqa_v': 3.157,
     'norm_mix_g': 3.172,
     'norm_ffn_g': 3.075,
     'mla_q_norm_g': 8.0,
     'na_rpb': 8.0,
     'gqa_q_norm_g': 8.0,
     'gqa_k_norm_g': 2.819,
     'final_norm_g': 7.551,
     'cache_na_k': 8.0,
     'cache_na_v': 8.0}
    for name, (base, spread) in spreads.items():
        noise = np.random.default_rng([zlib.crc32(name.encode()), seed]).standard_normal(out[name].shape)
        drawn = base * np.exp(spread * noise) if base else spread * noise
        out[name] = jnp.asarray(drawn.astype(out[name].dtype))
    for name, factor in factors.items():
        out[name] = (out[name] * factor).astype(out[name].dtype)
    return out
```

```python
from contextlib import ExitStack

import concourse.bass as bass
from concourse import mybir

F32 = mybir.dt.float32
F32R = mybir.dt.float32r
ALU = mybir.AluOpType
ACT = mybir.ActivationFunctionType
AX = mybir.AxisListType

P = 128
DM = 1024
KD = DM // P
LAT, CTX, T = 512, 128, 640
HALF = T // 2
NT = T // P
DEPTH = 2
EPS = 1e-6
GRID_W, ROWS = 64, 8

OFF_CKV, OFF_KR, OFF_NA = 256, 384, 416
NA_Q, NA_K, NA_V = OFF_NA, OFF_NA + 256, OFF_NA + 512
OFF_G = OFF_NA + 768
G_K = OFF_G + 384
G_V = OFF_G + 512
IN_COLS = G_V + 128
IC = 8
ICW = IN_COLS // IC
QW = 576
FF = 2816
FB = FF // 256
NADA = 48
ADA1 = 16
ADA_RING = 2
KEYS = 768
WIN = 713
MLA_SCALE = 96.0 ** -0.5
HD_SCALE = 0.125

HEADS = [("na", h) for h in range(4)] + [("mla", h) for h in range(6)] + [("gqa", h) for h in range(6)]
PAIR_TILE = [3, 4, 0, 1, 2, 5, 6, 7]
NH = len(HEADS)
NP = NH // 2
UNITS = 5 * NH
TS = 5 * NH + NP
NA_M = [(0, 1), (0, 2), (1, 3), (2, 3)]
NA_OFF = [0, 256, 640, 1024]
NA_COLS = 1280


def na_range(m):
    if m == 4:
        return 0, 3
    ns = [n for n in range(4) if NA_M[n][0] <= m <= NA_M[n][1]]
    return ns[0], ns[-1]


def prep_steps(g):
    kind, h = HEADS[g]
    if kind == "mla":
        s = [("Qa", g), ("Qb", g), ("Ka", g), ("Kb", g)]
        if h < 2:
            s.append(("Kpe", g))
        return s
    return [("Ka", g), ("Qa", g), ("Qb", g)]


def schedule():
    def prep(g):
        kind, h = HEADS[g]
        out = [("C", g)] + [("M",) + s for s in prep_steps(g)]
        if g % 2 == 0:
            if kind == "mla":
                out += [("M", "Va", g), ("M", "Vb", g)]
            else:
                out.append(("V", g))
        if kind == "na":
            out.append(("BM", g))
        return out

    order = list(prep(0))
    ada = ADA1
    pending_out = None
    for g in range(NH + 1):
        units = [("S", g, i) for i in range(5)] if g < NH else []
        trans = [("T", g - 1, m) for m in range(5)] if g > 0 else []
        if g > 0 and (g - 1) % 2 == 1:
            trans.append(("TP", (g - 1) // 2))
        extra = list(prep(g + 1)) if g + 1 < NH else []
        for _ in range(2):
            if g < NH and ada < NADA:
                extra.append(("ADA", ada))
                ada += 1
        if 2 <= g < 7:
            extra.append(("GZ", g - 2))
        n = max(len(units), len(trans), 1)
        per = -(-len(extra) // n)
        for j in range(n):
            if j < len(units):
                order.append(units[j])
            if j == 0 and pending_out is not None:
                order.append(("OUT", pending_out))
                pending_out = None
            if j < len(trans):
                order.append(trans[j])
            order += extra[:per]
            extra = extra[per:]
        order += extra
        if g > 0 and (g - 1) % 2 == 1:
            pending_out = (g - 1) // 2
    order.append(("OUT", pending_out))
    return order


SCHED = schedule()
MISC = [s[1:] for s in SCHED if s[0] == "M"]
MISC_AT = {s: n for n, s in enumerate(MISC)}
NM = len(MISC)
T_AT = {s: n for n, s in enumerate([s for s in SCHED if s[0] in ("T", "TP")])}
S_AT = {s: n for n, s in enumerate([s for s in SCHED if s[0] == "S"])}
NV = 5


def kind_of_pair(pair):
    return HEADS[2 * pair][0]


def v_at(pair):
    return pair if pair < 2 else pair - 3


def last_t_of(g):
    return T_AT[("T", g, 4)]


def build(nc, a, out):
    ctx = ExitStack()
    with ctx:
        def sem(name):
            return ctx.enter_context(nc.semaphore(name))

        def sb(name, shape, dt=F32, scope=ctx):
            return scope.enter_context(nc.sbuf_tensor(name, shape, dt))

        x = sb("x", [P, KD, T])
        ada_w = sb("ada_w", [P, ADA_RING, KD, P])
        mod = sb("mod", [P, NADA, 2])
        coef = sb("coef", [P, 2, KD, 2])
        rstd = sb("rstd", [P, T])
        cond = sb("cond", [P, KD, 2])
        silu_c = sb("silu_c", [P, KD, 2])
        b_ada = sb("b_ada", [P, DEPTH, NADA])
        norm_g = sb("norm_g", [P, DEPTH, 2, KD])
        fin_g = sb("fin_g", [P, KD])
        qn_g = sb("qn_g", [P, DEPTH, 2])
        kv_g = sb("kv_g", [P, P])
        g8 = sb("g8", [P, 512])
        rope = sb("rope", [P, 4, 2, 96])
        mask = sb("mask", [P, NA_COLS // ROWS])
        ident = sb("ident", [P, P])
        ones = sb("ones", [P, P])
        stat = sb("stat", [P, NT, 10])
        kc_na = sb("kc_na", [P, 4, P])
        kc_g = sb("kc_g", [P, 2, P])
        kc_mla = sb("kc_mla", [P, P])
        kc_pe = sb("kc_pe", [P, P])
        vc_na = sb("vc_na", [P, 256])
        vc_g = sb("vc_g", [P, P])
        negmax = sb("negmax", [P, UNITS])
        rsum = sb("rsum", [P, UNITS])
        rinv = sb("rinv", [P, UNITS])

        s1 = ExitStack()
        bias_h = sb("bias_h", [P, NA_COLS], F32, s1)
        win = sb("win", [P, 2, WIN + 7], F32, s1)
        pad = sb("pad_h", [P, KD * 2 * T - NA_COLS - 2 * (WIN + 7) - 6 * T], F32, s1)
        ckvT = sb("ckvT", [P, 2, KEYS], F32R, s1)
        wkv = sb("wkv", [P, 2, KEYS], F32R, s1)
        s1.close()
        hT = sb("hT", [P, KD, 2, T], F32R)

        s2 = ExitStack()
        sq = sb("sq", [P, 2, T], F32, s2)
        tn = sb("tn", [P, 2, T], F32, s2)
        hf = sb("hf", [P, T], F32, s2)
        s2.close()
        s3 = ExitStack()
        act = sb("act", [P, 2, 2, T], F32R, s3)
        sl = sb("sl", [P, 2, HALF], F32, s3)
        mm = sb("mm", [P, 2, HALF], F32, s3)
        wo_raw = sb("wo_raw", [P, 2, KD, P], F32, s3)
        wo = sb("wo", [P, 2, 2, KD, P], F32R, s3)
        dw_raw = sb("dw_raw", [P, 2, DM], F32, s3)
        s3.close()
        z = sb("z", [P, NT, IN_COLS])
        qm = sb("qm", [P, NT, QW])
        sb("z_end", [P, 32])

        s4 = ExitStack()
        wi_raw = sb("wi_raw", [P, 2, KD, ICW], F32, s4)
        wi = sb("wi", [P, 2, 2, KD, ICW], F32R, s4)
        cqT = sb("cqT", [P, 2, 2, T], F32R, s4)
        wq_raw = sb("wq_raw", [P, 2, QW], F32, s4)
        wq = sb("wq", [P, 2, 2, QW], F32R, s4)
        s4.close()
        s5 = ExitStack()
        gw_raw = sb("gw_raw", [P, 2, KD, 256], F32, s5)
        gw = sb("gw", [P, 2, 2, KD, 256], F32R, s5)
        dw = sb("dw", [P, 2, 2, DM], F32R, s5)
        s5.close()
        probs = sb("probs", [P, 2, 4, T])
        probs_p = sb("probs_p", [P, 2, P])
        pT = sb("pT", [P, 2, 2, 512], F32R)
        Q = sb("Q", [P, 2, 2, T], F32R)
        K = sb("K", [P, 2, 2, KEYS], F32R)
        V = sb("V", [P, 2, 2, 6, 192], F32R)
        ztmp = sb("ztmp", [P, 512])
        wkv_raw = sb("wkv_raw", [P, KEYS])

        ps = ctx.enter_context(nc.psum_tensor("ps", [P, 8, 512], F32))

        const_in = sem("const_in")
        x_in = sem("x_in")
        small_in = sem("small_in")
        ones_set = sem("ones_set")
        silu_done = sem("silu_done")
        ada_in = [sem(f"ada_in{i}") for i in range(ADA_RING)]
        ada_ps = sem("ada_ps")
        ada_done = sem("ada_done")
        coef_done = sem("coef_done")
        sq_ready = sem("sq_ready")
        ss_done = sem("ss_done")
        ms_ready = sem("ms_ready")
        rms_ready = sem("rms_ready")
        rstd_ready = sem("rstd_ready")
        tn_ready = sem("tn_ready")
        hf_ready = sem("hf_ready")
        h_hi = sem("h_hi")
        h_ready = sem("h_ready")
        wi_in = [sem(f"wi_in{i}") for i in range(2)]
        wi_hi = sem("wi_hi")
        wi_ready = sem("wi_ready")
        z_ps = sem("z_ps")
        z_done = sem("z_done")
        wqk_in = sem("wqk_in")
        wqk_hi = sem("wqk_hi")
        wq_ready = sem("wq_ready")
        wkv_ready = sem("wkv_ready")
        cstat = sem("cstat")
        cstat_ms = sem("cstat_ms")
        cstat_rms = sem("cstat_rms")
        c_norm = sem("c_norm")
        cT_ps = sem("cT_ps")
        cT_hi = sem("cT_hi")
        cT_ready = sem("cT_ready")
        gsq = sem("gsq")
        gstat = sem("gstat")
        qm_ps = sem("qm_ps")
        qm_done = sem("qm_done")
        q_roped = sem("q_roped")
        g_norm = sem("g_norm")
        g_roped = sem("g_roped")
        kv_out = sem("kv_out")
        norm_out = sem("norm_out")
        vz_done = sem("vz_done")
        win_in = [sem(f"win_in{i}") for i in range(2)]
        bias_ready = sem("bias_ready")
        misc_ps = sem("misc_ps")
        misc_hi = sem("misc_hi")
        misc_done = sem("misc_done")
        kc_hi = sem("kc_hi")
        v_hi = sem("v_hi")
        v_ready = sem("v_ready")
        s_ready = sem("s_ready")
        biased = sem("biased")
        max_ready = sem("max_ready")
        exp_done = sem("exp_done")
        rinv_ready = sem("rinv_ready")
        p_ready = sem("p_ready")
        pT_ps = sem("pT_ps")
        pT_hi = sem("pT_hi")
        pT_ready = sem("pT_ready")
        pv_done = sem("pv_done")
        o_hi = sem("o_hi")
        o_ready = sem("o_ready")
        wo_in = [sem(f"wo_in{i}") for i in range(2)]
        wo_hi = sem("wo_hi")
        wo_ready = sem("wo_ready")
        y_ps = sem("y_ps")
        x_done = sem("x_done")
        gw_in = sem("gw_in")
        dw_in = sem("dw_in")
        gw_hi = sem("gw_hi")
        gw_ready = sem("gw_ready")
        dw_hi = sem("dw_hi")
        dw_ready = sem("dw_ready")
        gu_ps = sem("gu_ps")
        sl_ready = sem("sl_ready")
        mm_ready = sem("mm_ready")
        act_hi = sem("act_hi")
        act_ready = sem("act_ready")
        dve_own = sem("dve_own")
        pool_own = sem("pool_own")
        act_own = sem("act_own")
        y_ready = sem("y_ready")
        passed_pe = sem("passed_pe")
        passed_sc = sem("passed_sc")
        passed_po = sem("passed_po")
        y_out = sem("y_out")

        XD = KD + FB * KD

        def settled(eng, passed):
            eng.sem_inc(passed, 1)

        block = ctx.enter_context(nc.Block())

        def v_slots(pair, q, t0, n):
            v = V[:, pair % 2, q, t0:t0 + n, :]
            return bass.AP(tensor=v.tensor, offset=v.offset, ap=[list(v.ap[0]), [192, n], [128, 2], [1, 64]])

        def v_sources(g, q):
            kind, h = HEADS[g]
            pair = g // 2
            res = []
            for slot in range(2):
                c0 = NA_V + 64 * (h + slot) if kind == "na" else G_V + 64 * ((h + slot) // 3)
                cc = 64 * (h + slot) if kind == "na" else 64 * ((h + slot) // 3)
                cache = vc_na if kind == "na" else vc_g
                d0 = 128 * slot
                res.append((V[:, pair % 2, q, 0:NT, d0:d0 + 64], z[:, 0:NT, c0:c0 + 64], V[:, pair % 2, 0, 0:NT, d0:d0 + 64]))
                res.append((V[:, pair % 2, q, 5, d0:d0 + 64], cache[:, cc:cc + 64], V[:, pair % 2, 0, 5, d0:d0 + 64]))
            return res

        def recip_later(ve, l, u):
            if u < 0:
                return
            ve.wait_ge(exp_done, l * UNITS + u + 1)
            ve.reciprocal(rinv[:, u:u + 1], rsum[:, u:u + 1]).then_inc(rinv_ready, 1)

        def norm_unit(po, l, u):
            g, i = u // 5, u % 5
            kind = HEADS[g][0]
            if i == 4:
                t = probs_p[:, g % 2, :]
            elif kind == "na":
                t = probs[:, g % 2, i, 0:(NA_M[i][1] - NA_M[i][0] + 2) * P]
            else:
                t = probs[:, g % 2, i, :]
            po.wait_ge(rinv_ready, l * UNITS + u + 1)
            settled(po, passed_po)
            po.tensor_scalar(t, t, rinv[:, u:u + 1], None, ALU.mult).then_inc(p_ready, 1)

        @block.sync
        def _(sp):
            for dst, src in ((cond, a["cond"]), (b_ada, a["b_ada"]), (norm_g, a["norm_g"]), (fin_g, a["fin_g"]),
                             (qn_g, a["qn_g"]), (rope, a["rope"]), (mask, a["mask"]), (ident, a["ident"])):
                sp.dma_start(dst[:], src).then_inc(const_in, 16)
            for k in range(KD):
                sp.dma_start(x[:, k, :], a["x"][k * P:(k + 1) * P, :]).then_inc(x_in, 16)

            def ada_load(l, t):
                if t >= ADA_RING:
                    sp.wait_ge(ada_ps, l * NADA + t - ADA_RING + 1)
                else:
                    sp.wait_ge(ada_ps, l * NADA)
                sp.dma_start(ada_w[:, t % ADA_RING], a["w_ada"][l, :, t * P:(t + 1) * P]
                             .rearrange("(k p) n -> p k n", p=P)).then_inc(ada_in[t % ADA_RING], 16)

            with sp.Fori(0, DEPTH) as l:
                for t in range(ADA1):
                    ada_load(l, t)
                    if t == 1:
                        sp.wait_ge(x_done, l * XD)
                        sp.dma_start(kv_g[:], a["kv_g"][bass.ts(l, 1), :].to_broadcast([P, P])).then_inc(small_in, 16)
                        sp.dma_start(g8[:], a["g8"][bass.ts(l, 1), :].to_broadcast([P, 512])).then_inc(small_in, 16)
                        for r in range(2):
                            sp.dma_start(kc_na[64 * r:64 * r + 64], a["na_kT"][l]).then_inc(small_in, 16)
                            sp.dma_start(kc_g[64 * r:64 * r + 64], a["g_kT"][l]).then_inc(small_in, 16)
                        sp.dma_start(kc_mla[:], a["ckvT"][l]).then_inc(small_in, 16)
                        sp.dma_start(kc_pe[64:96, :], a["krT"][l]).then_inc(small_in, 16)
                        sp.dma_start(vc_na[:], a["na_v"][l]).then_inc(small_in, 16)
                        sp.dma_start(vc_g[:], a["g_v"][l]).then_inc(small_in, 16)
                for c in range(IC):
                    if c >= 2:
                        sp.wait_ge(wi_ready, l * IC + c - 1)
                    sp.dma_start(wi_raw[:, c % 2], a["w_in"][l, :, c * ICW:(c + 1) * ICW]
                                 .rearrange("(k p) n -> p k n", p=P)).then_inc(wi_in[c % 2], 16)
                sp.dma_start(wq_raw[:], a["w_q_up"][l].rearrange("(k p) n -> p k n", p=P)).then_inc(wqk_in, 16)
                sp.dma_start(wkv_raw[:], a["w_kv_up"][l]).then_inc(wqk_in, 16)
                tile = NT - 1
                sp.wait_ge(z_done, l * IC * NT + IC * NT)
                for name, c0, w in (("o_kr", OFF_KR, 32), ("o_nak", NA_K, 256), ("o_nav", NA_V, 256), ("o_gv", G_V, P)):
                    sp.dma_start(out[name][l], z[:, tile, c0:c0 + w]).then_inc(kv_out, 16)
                sp.wait_ge(c_norm, l * NT + NT)
                sp.dma_start(out["o_ckv"][l], z[:, tile, OFF_CKV:OFF_KR]).then_inc(norm_out, 16)
                for s in SCHED:
                    if s[0] == "ADA":
                        ada_load(l, s[1])
                    if s[0] == "GZ" and s[1] == NT - 1:
                        sp.wait_ge(g_norm, l * NT + NT)
                        sp.dma_start(out["o_gk"][l], z[:, tile, G_K:G_V]).then_inc(norm_out, 16)
                sp.wait_ge(misc_done, l * NM + NM)
                sp.wait_ge(v_ready, l * NV + NV)
                sp.wait_ge(kv_out, l * 64 + 64)
                sp.wait_ge(norm_out, l * 32 + 32)
                for o in range(KD):
                    if o >= 2:
                        sp.wait_ge(wo_ready, l * KD + o - 1)
                    sp.dma_start(wo_raw[:, o % 2], a["w_out"][l, :, o * P:(o + 1) * P]
                                 .rearrange("(k p) n -> p k n", p=P)).then_inc(wo_in[o % 2], 16)
                    if o == 1:
                        sp.wait_ge(o_ready, l * NP + NP)
                        sp.dma_start(gw_raw[:, 0], a["w_gate"][l, :, 0:256].rearrange("(k p) n -> p k n", p=P)).then_inc(gw_in, 16)
                        sp.dma_start(gw_raw[:, 1], a["w_up"][l, :, 0:256].rearrange("(k p) n -> p k n", p=P)).then_inc(gw_in, 16)
                        sp.dma_start(dw_raw[:], a["w_down"][l, 0:256, :].rearrange("(j p) n -> p j n", p=P)).then_inc(dw_in, 16)
                with sp.Fori(1, FB) as b:
                    sp.wait_ge(gw_ready, l * FB + b)
                    sp.dma_start(gw_raw[:, 0], a["w_gate"][l, :, bass.ts(b, 256)].rearrange("(k p) n -> p k n", p=P)).then_inc(gw_in, 16)
                    sp.dma_start(gw_raw[:, 1], a["w_up"][l, :, bass.ts(b, 256)].rearrange("(k p) n -> p k n", p=P)).then_inc(gw_in, 16)
                    sp.wait_ge(dw_ready, l * FB + b)
                    sp.dma_start(dw_raw[:], a["w_down"][l, bass.ts(b, 256), :].rearrange("(j p) n -> p j n", p=P)).then_inc(dw_in, 16)
            for k in range(KD):
                sp.wait_ge(y_ready, k + 1)
                sp.dma_start(out["o_y"][k * P:(k + 1) * P, :], x[:, k]).then_inc(y_out, 16)
            sp.wait_ge(y_out, 16 * KD)
            sp.wait_ge(kv_out, DEPTH * 64)
            sp.wait_ge(norm_out, DEPTH * 32)

        @block.tensor
        def _(pe):
            prev7 = [None]

            def split_mm(dst, lh, ll, rh, rl, start, stop):
                pe.matmul(dst, lh, rh, start=start, stop=False, skip_group_check=True)
                pe.matmul(dst, lh, rl, start=False, stop=False, skip_group_check=True)
                return pe.matmul(dst, ll, rh, start=False, stop=stop, skip_group_check=True)

            def ada_tile(l, t, bank):
                pe.wait_ge(ada_in[t % ADA_RING], 16 * (l * (NADA // ADA_RING) + t // ADA_RING + 1))
                for k in range(KD):
                    m = pe.matmul(ps[:, bank, 0:2], ada_w[:, t % ADA_RING, k, :], silu_c[:, k, :],
                                  start=k == 0, stop=k == KD - 1)
                m.then_inc(ada_ps, 1)

            def sum_squares(base, k):
                pe.wait_ge(sq_ready, base + k + 1)
                for j in range(2):
                    m = pe.matmul(ps[:, j, 0:HALF], ones[:], sq[:, k % 2, j * HALF:(j + 1) * HALF],
                                  start=k == 0, stop=k == KD - 1, skip_group_check=True)
                m.then_inc(ss_done, 1)

            pe.wait_ge(silu_done, 1)
            pe.wait_ge(ones_set, 1)
            pe.wait_ge(const_in, 16 * 8)
            with pe.Fori(0, DEPTH) as l:
                for t in range(ADA1):
                    if t >= 2:
                        pe.wait_ge(ada_done, l * NADA + t - 1)
                    else:
                        pe.wait_ge(x_done, l * XD)
                    ada_tile(l, t, 6 + t % 2)
                for k in range(KD):
                    sum_squares(l * 2 * KD, k)
                for c in range(IC):
                    pe.wait_ge(wi_ready, l * IC + c + 1)
                    for t in range(NT):
                        n = c * NT + t
                        if c == 0 and t == 0:
                            for k in range(KD):
                                pe.wait_ge(h_ready, l * 2 * KD + k + 1)
                                m = split_mm(ps[:, 0, 0:ICW], hT[:, k, 0, 0:P], hT[:, k, 1, 0:P],
                                             wi[:, 0, 0, k, :], wi[:, 0, 1, k, :], k == 0, k == KD - 1)
                            m.then_inc(z_ps, 1)
                            continue
                        if n >= 6:
                            pe.wait_ge(z_done, l * IC * NT + n - 5)
                        for k in range(KD):
                            m = split_mm(ps[:, n % 6, 0:ICW], hT[:, k, 0, t * P:(t + 1) * P], hT[:, k, 1, t * P:(t + 1) * P],
                                         wi[:, c % 2, 0, k, :], wi[:, c % 2, 1, k, :], k == 0, k == KD - 1)
                        m.then_inc(z_ps, 1)
                pe.wait_ge(z_done, l * IC * NT + IC * NT)
                pe.wait_ge(c_norm, l * NT + NT)
                for e in range(3):
                    for t in range(4):
                        m = pe.transpose(ps[:, e, t * P:(t + 1) * P], z[:, t, e * P:(e + 1) * P], ident[:])
                    m.then_inc(cT_ps, 1)
                for e in range(3):
                    m = pe.transpose(ps[:, 3, e * P:(e + 1) * P], z[:, 4, e * P:(e + 1) * P], ident[:])
                m.then_inc(cT_ps, 1)
                pe.wait_ge(cT_ready, l * 4 + 4)
                pe.wait_ge(wq_ready, l + 1)
                for n in range(2 * NT):
                    t, j = n // 2, n % 2
                    if n >= 3:
                        pe.wait_ge(qm_done, l * 2 * NT + n - 2)
                    for e in range(2):
                        m = split_mm(ps[:, 4 + n % 3, 0:288], cqT[:, e, 0, t * P:(t + 1) * P], cqT[:, e, 1, t * P:(t + 1) * P],
                                     wq[:, e, 0, j * 288:(j + 1) * 288], wq[:, e, 1, j * 288:(j + 1) * 288], e == 0, e == 1)
                    m.then_inc(qm_ps, 1)
                pe.wait_ge(qm_done, l * 2 * NT + 2 * NT)
                pending = []

                def flush():
                    if pending:
                        pending.pop()()

                prev7[0] = (ada_done, NADA, ADA1)

                def take7():
                    s, per, n = prev7[0]
                    pe.wait_ge(s, l * per + n)

                for s in SCHED:
                    if s[0] == "S":
                        _, g, i = s
                        kind = HEADS[g][0]
                        u, gb = S_AT[s], g % 2
                        if i == 0:
                            pe.wait_ge(misc_done, l * NM + MISC_AT[prep_steps(g)[-1]] + 1)
                        if u >= 2:
                            pe.wait_ge(exp_done, l * UNITS + u - 1)
                        bk = 2 * (u % 2)
                        qs = slice(i * P, (i + 1) * P)
                        if i == 4:
                            parts = [(bk, 0, P, 640)]
                        elif kind == "na":
                            m0, m1 = NA_M[i]
                            w = (m1 - m0 + 1) * P
                            parts = [(bk, 0, w, m0 * P), (bk, w, P, LAT)]
                        else:
                            parts = [(bk, 0, HALF, 0), (bk + 1, 0, HALF, HALF)]
                        for n, (bank, c0, w, k0) in enumerate(parts):
                            dst = ps[:, bank, c0:c0 + w]
                            first = c0 == 0
                            if kind == "mla":
                                m = split_mm(dst, Q[0:96, gb, 0, qs], Q[0:96, gb, 1, qs], K[0:96, gb, 0, k0:k0 + w],
                                             K[0:96, gb, 1, k0:k0 + w], first, True)
                            else:
                                pe.matmul(dst, Q[:, gb, 0, qs], K[:, gb, 0, k0:k0 + w], start=first, stop=False,
                                          skip_group_check=True)
                                m = pe.matmul(dst, Q[:, gb, 0, qs], K[:, gb, 1, k0:k0 + w], start=False, stop=True,
                                              skip_group_check=True)
                        m.then_inc(s_ready, 1)
                        flush()
                    elif s[0] == "T":
                        _, g, mt = s
                        kind = HEADS[g][0]
                        n = T_AT[s]
                        if mt == 0:
                            pe.wait_ge(p_ready, l * UNITS + 5 * g + 4)
                        if n >= 2:
                            pe.wait_ge(pT_ready, l * TS + n - 1)
                        a0, a1 = na_range(mt) if kind == "na" else (0, 3)
                        for i in range(a0, a1 + 1):
                            if kind == "na":
                                m0, m1 = NA_M[i]
                                pos = (m1 - m0 + 1 if mt == 4 else mt - m0) * P
                            else:
                                pos = mt * P
                            m = pe.transpose(ps[:, 4 + n % 2, i * P:(i + 1) * P], probs[:, g % 2, i, pos:pos + P], ident[:])
                        m.then_inc(pT_ps, 1)
                        flush()

                        def pv(g=g, mt=mt, n=n, a0=a0, a1=a1):
                            pair, slot = g // 2, g % 2
                            if slot == 0 and mt == 0:
                                if kind_of_pair(pair) == "mla":
                                    pe.wait_ge(misc_done, l * NM + MISC_AT[("Vb", 2 * pair)] + 1)
                                else:
                                    pe.wait_ge(v_ready, l * NV + v_at(pair) + 1)
                                if pair > 0:
                                    pe.wait_ge(o_ready, l * NP + pair)
                            pe.wait_ge(pT_ready, l * TS + n + 1)
                            vt = 5 if mt == 4 else mt
                            cols = slice(a0 * P, (a1 + 1) * P)
                            lh, ll = (V[:, pair % 2, q, vt, 64 * slot:64 * slot + P] for q in range(2))
                            m = split_mm(ps[:, 6, cols], lh, ll, pT[:, n % 2, 0, cols], pT[:, n % 2, 1, cols],
                                         slot == 0 and mt == 0, False)
                            m.then_inc(pv_done, 1)
                        pending.append(pv)
                    elif s[0] == "TP":
                        pair = s[1]
                        n = T_AT[s]
                        pe.wait_ge(p_ready, l * UNITS + 10 * pair + 10)
                        pe.wait_ge(pT_ready, l * TS + n - 1)
                        for slot in range(2):
                            m = pe.transpose(ps[:, 4 + n % 2, slot * P:(slot + 1) * P], probs_p[:, slot, :], ident[:])
                        m.then_inc(pT_ps, 1)
                        flush()

                        def pvp(pair=pair, n=n):
                            pe.wait_ge(pT_ready, l * TS + n + 1)
                            take7()
                            for slot in range(2):
                                lh, ll = (V[:, pair % 2, q, 4, 64 * slot:64 * slot + P] for q in range(2))
                                cols = slice(slot * P, (slot + 1) * P)
                                m = split_mm(ps[:, 7, 0:P], lh, ll, pT[:, n % 2, 0, cols], pT[:, n % 2, 1, cols],
                                             slot == 0, slot == 1)
                            m.then_inc(pv_done, 1)
                            prev7[0] = (o_ready, NP, pair + 1)
                        pending.append(pvp)
                    elif s[0] == "OUT":
                        flush()
                    elif s[0] == "ADA":
                        take7()
                        ada_tile(l, s[1], 7)
                        prev7[0] = (ada_done, NADA, s[1] + 1)
                    elif s[0] == "M":
                        what, g = s[1:]
                        kind, h = HEADS[g]
                        take7()
                        settled(pe, passed_pe)
                        if what in ("Qa", "Qb"):
                            if kind == "mla" and g == 4 and what == "Qa":
                                pe.wait_ge(q_roped, l + 1)
                            if kind == "gqa" and what == "Qa" and h == 0:
                                pe.wait_ge(g_roped, l * 4 + 4)
                                settled(pe, passed_pe)
                        if what == "Qa" or (what == "Ka" and kind != "mla") or what == "Qb":
                            ts_ = range(4) if what != "Qb" else [4]
                            for t in ts_:
                                o0 = (t % 4) * P
                                if kind == "mla":
                                    m = pe.transpose(ps[0:96, 7, o0:o0 + P], qm[:, t, h * 96:(h + 1) * 96], ident[:])
                                    if what == "Qb" and h < 2:
                                        m = pe.transpose(ps[0:96, 7, P:2 * P], z[:, t, OFF_KR - 64:OFF_NA], ident[:])
                                else:
                                    qc = (NA_Q if kind == "na" else OFF_G) + 64 * h
                                    kc = NA_K + 64 * h if kind == "na" else G_K + 64 * (h // 3)
                                    c0 = kc if what == "Ka" else qc
                                    if kind == "gqa" and what == "Ka" and h == 0 and t == 0:
                                        pe.wait_ge(g_roped, l * 4 + 4)
                                        pe.wait_ge(g_norm, l * NT + NT)
                                        settled(pe, passed_pe)
                                    m = pe.transpose(ps[0:64, 7, o0:o0 + P], z[:, t, c0:c0 + 64], ident[:])
                                    if what == "Qb":
                                        m = pe.transpose(ps[0:64, 7, P:2 * P], z[:, t, kc:kc + 64], ident[:])
                        elif what in ("Ka", "Kb"):
                            c0, c1 = (0, LAT) if what == "Ka" else (LAT, KEYS)
                            if g == 4:
                                pe.wait_ge(wkv_ready, l + 1)
                            m = split_mm(ps[0:64, 7, 0:c1 - c0], wkv[:, 0, h * P:h * P + 64], wkv[:, 1, h * P:h * P + 64],
                                         ckvT[:, 0, c0:c1], ckvT[:, 1, c0:c1], True, True)
                        elif what == "Kpe":
                            for t in range(4):
                                m = pe.transpose(ps[0:96, 7, t * P:(t + 1) * P], z[:, t, OFF_KR - 64:OFF_NA], ident[:])
                        else:
                            tiles = [0, 1, 2, 3] if what == "Va" else [4, 5]
                            for n, t in enumerate(tiles):
                                k0 = {4: 640, 5: LAT}.get(t, t * P)
                                src = [wkv[:, q, h * P:(h + 2) * P].rearrange("p (a b) -> p a b", a=2)[:, :, 64:P] for q in range(2)]
                                m = split_mm(ps[:, 7, n * P:(n + 1) * P], ckvT[:, 0, k0:k0 + P], ckvT[:, 1, k0:k0 + P],
                                             src[0], src[1], True, True)
                        m.then_inc(misc_ps, 1)
                        prev7[0] = (misc_done, NM, MISC_AT[(what, g)] + 1)
                pe.wait_ge(o_ready, l * NP + NP)
                for o in range(KD):
                    pe.wait_ge(wo_ready, l * KD + o + 1)
                    if o >= 3:
                        pe.wait_ge(x_done, l * XD + o - 2)
                    elif o == 2:
                        pe.wait_ge(ada_done, l * NADA + NADA)
                    for j in range(2):
                        for k in range(KD):
                            cols = slice(j * HALF, (j + 1) * HALF)
                            m = split_mm(ps[:, 2 + 2 * (o % 3) + j, 0:HALF], wo[:, o % 2, 0, k, :], wo[:, o % 2, 1, k, :],
                                         hT[:, k, 0, cols], hT[:, k, 1, cols], k == 0, k == KD - 1)
                    m.then_inc(y_ps, 1)
                for k in range(KD):
                    sum_squares(l * 2 * KD + KD, k)
                pe.wait_ge(h_ready, l * 2 * KD + 2 * KD)
                settled(pe, passed_pe)

                def ffn_block(b):
                    for j in range(2):
                        for w in range(2):
                            pe.wait_ge(x_done, l * XD + KD + b * KD - 3 + 2 * j + w)
                            if j == 0:
                                pe.wait_ge(gw_ready, l * FB + b + 1)
                            for hf_ in range(2):
                                cols = slice(hf_ * HALF, (hf_ + 1) * HALF)
                                for k in range(KD):
                                    m = split_mm(ps[:, 4 * j + 2 * w + hf_, 0:HALF], gw[:, w, 0, k, j * P:(j + 1) * P],
                                                 gw[:, w, 1, k, j * P:(j + 1) * P], hT[:, k, 0, cols], hT[:, k, 1, cols],
                                                 k == 0, k == KD - 1)
                                m.then_inc(gu_ps, 1)
                    base = (l * FB + b) * 4

                    def down(o, j, hf_):
                        cols = slice(hf_ * HALF, (hf_ + 1) * HALF)
                        return split_mm(ps[:, 2 * (o % 4) + hf_, 0:HALF], dw[:, 0, j, o * P:(o + 1) * P],
                                        dw[:, 1, j, o * P:(o + 1) * P], act[:, j, 0, cols], act[:, j, 1, cols],
                                        j == 0, j == 1)
                    pe.wait_ge(dw_ready, l * FB + b + 1)
                    pe.wait_ge(act_ready, base + 2)
                    for o in range(2):
                        for hf_ in range(2):
                            down(o, 0, hf_)
                    pe.wait_ge(act_ready, base + 3)
                    for o in range(2):
                        down(o, 1, 0)
                    pe.wait_ge(act_ready, base + 4)
                    for o in range(2):
                        down(o, 1, 1).then_inc(y_ps, 1)
                    for o in range(2, KD):
                        if o >= 4:
                            pe.wait_ge(x_done, l * XD + KD + b * KD + o - 3)
                        for hf_ in range(2):
                            for j in range(2):
                                m = down(o, j, hf_)
                        m.then_inc(y_ps, 1)

                with pe.Fori(0, FB) as b:
                    ffn_block(b)
            pe.wait_ge(x_done, DEPTH * XD)
            for k in range(KD):
                sum_squares(DEPTH * 2 * KD, k)

        @block.scalar
        def _(sc):
            def square(base, k, first):
                if not first or k >= 2:
                    sc.wait_ge(ss_done, base + k - 1)
                sc.activation(sq[:, k % 2], x[:, k], ACT.Square).then_inc(sq_ready, 1)

            def rms(n):
                sc.wait_ge(ms_ready, n)
                sc.activation(rstd[:], rstd[:], ACT.Sqrt).then_inc(rms_ready, 1)

            def modulated(l, nrm):
                base = l * 2 * KD + nrm * KD
                sc.wait_ge(coef_done, l * 2 + nrm + 1)
                for k in range(KD):
                    sc.wait_ge(tn_ready, base + k + 1)
                    for q, (c0, c1) in enumerate(((0, LAT), (LAT, T))):
                        i = sc.activation(hT[:, k, 0, c0:c1], tn[:, k % 2, c0:c1], ACT.Identity,
                                          bias=mod[:, 24 * nrm + k, q:q + 1], scale=coef[:, nrm, k, q:q + 1])
                    i.then_inc(h_hi, 1)

            sc.wait_ge(const_in, 16 * 8)
            sc.activation(silu_c[:], cond[:], ACT.Silu).then_inc(silu_done, 1)
            sc.wait_ge(x_in, 16 * KD)
            with sc.Fori(0, DEPTH) as l:
                for k in range(KD):
                    sc.wait_ge(x_done, l * XD)
                    if k >= 2:
                        sc.wait_ge(ss_done, l * 2 * KD + k - 1)
                    sc.activation(sq[:, k % 2], x[:, k], ACT.Square).then_inc(sq_ready, 1)
                rms(l * 2 + 1)

                def wi_split(c):
                    sc.wait_ge(wi_in[c % 2], 16 * (l * (IC // 2) + c // 2 + 1))
                    if c >= 2:
                        sc.wait_ge(z_ps, l * IC * NT + (c - 1) * NT)
                    sc.activation(wi[:, c % 2, 0], wi_raw[:, c % 2], ACT.Copy).then_inc(wi_hi, 1)
                wi_split(0)
                wi_split(1)
                modulated(l, 0)
                for c in range(IC):
                    for t in range(NT):
                        n = c * NT + t
                        sc.wait_ge(z_ps, l * IC * NT + n + 1)
                        sc.activation(z[:, t, c * ICW:(c + 1) * ICW], ps[:, n % 6, 0:ICW], ACT.Copy).then_inc(z_done, 1)
                    if c + 2 < IC:
                        wi_split(c + 2)
                    if c == 3:
                        sc.wait_ge(wqk_in, 32 * l + 32)
                        sc.activation(wq[:, :, 0, :], wq_raw[:], ACT.Copy).then_inc(wqk_hi, 1)
                    if c == 5:
                        sc.wait_ge(z_done, l * IC * NT + 2 * NT)
                        for t in range(NT):
                            sc.activation(ztmp[:, 0:256], z[:, t, 0:256], ACT.Square, accum_out=stat[:, t, 0:1]).then_inc(act_own, 1)
                            sc.wait_ge(act_own, l * 2 * NT + 2 * t + 1)
                            i = sc.activation(ztmp[:, 0:P], z[:, t, OFF_CKV:OFF_KR], ACT.Square, accum_out=stat[:, t, 1:2])
                            i.then_inc(act_own, 1)
                            sc.wait_ge(act_own, l * 2 * NT + 2 * t + 2)
                        sc.wait_ge(cstat_ms, 2 * l + 1)
                        sc.activation(stat[:, :, 0:2], stat[:, :, 0:2], ACT.Sqrt).then_inc(cstat_rms, 1)
                sc.wait_ge(z_done, l * IC * NT + IC * NT)
                sc.activation(wkv[:, 0], wkv_raw[:], ACT.Copy).then_inc(wqk_hi, 1)
                sc.wait_ge(small_in, (l + 1) * 160)
                sc.activation(ckvT[:, 0, LAT:640], kc_mla[:], ACT.Copy).then_inc(wqk_hi, 1)
                for e in range(4):
                    sc.wait_ge(cT_ps, l * 4 + e + 1)
                    settled(sc, passed_sc)
                    if e < 2:
                        sc.activation(cqT[:, e, 0, 0:LAT], ps[:, e, :], ACT.Copy, scale=qn_g[:, l, e:e + 1]).then_inc(cT_hi, 1)
                    elif e == 2:
                        sc.activation(ckvT[:, 0, 0:LAT], ps[:, e, :], ACT.Copy).then_inc(cT_hi, 1)
                    else:
                        for q in range(2):
                            sc.activation(cqT[:, q, 0, LAT:T], ps[:, 3, q * P:(q + 1) * P], ACT.Copy, scale=qn_g[:, l, q:q + 1])
                        sc.activation(ckvT[:, 0, 640:KEYS], ps[:, 3, 2 * P:3 * P], ACT.Copy).then_inc(cT_hi, 1)
                for t in range(NT):
                    sc.wait_ge(gstat, l * NT + t)
                    sc.activation(ztmp[:], z[:, t, OFF_G:G_V], ACT.Square).then_inc(gsq, 1)
                sc.wait_ge(cstat_ms, 2 * l + 2)
                sc.activation(stat[:, :, 2:10], stat[:, :, 2:10], ACT.Sqrt).then_inc(cstat_rms, 1)
                for n in range(2 * NT):
                    t, j = n // 2, n % 2
                    sc.wait_ge(qm_ps, l * 2 * NT + n + 1)
                    sc.activation(qm[:, t, j * 288:(j + 1) * 288], ps[:, 4 + n % 3, 0:288], ACT.Copy).then_inc(qm_done, 1)
                sc.wait_ge(qm_ps, l * 2 * NT + 2 * NT)
                sc.wait_ge(wq_ready, l + 1)
                sc.wait_ge(vz_done, l + 1)
                for s in SCHED:
                    if s[0] == "S":
                        _, g, i = s
                        kind = HEADS[g][0]
                        u = S_AT[s]
                        bk = 2 * (u % 2)
                        sc.wait_ge(max_ready, l * UNITS + u + 1)
                        if i == 0 and g >= 2:
                            sc.wait_ge(pT_ps, l * TS + last_t_of(g - 2) + 1)
                        if i == 4:
                            if g >= 2:
                                sc.wait_ge(pT_ps, l * TS + T_AT[("TP", g // 2 - 1)] + 1)
                            src, dst = ps[:, bk, 0:P], probs_p[:, g % 2, :]
                        elif kind == "na":
                            w = (NA_M[i][1] - NA_M[i][0] + 2) * P
                            src, dst = ps[:, bk, 0:w], probs[:, g % 2, i, 0:w]
                        else:
                            src = ps[:, bk:bk + 2, 0:HALF]
                            dst = probs[:, g % 2, i, :].rearrange("p (a b) -> p a b", a=2)
                        sc.activation(dst, src, ACT.Exp, bias=negmax[:, u:u + 1], accum_out=rsum[:, u:u + 1]).then_inc(exp_done, 1)
                    elif s[0] in ("T", "TP"):
                        n = T_AT[s]
                        if s[0] == "TP":
                            c0, c1 = 0, 2 * P
                        else:
                            a0, a1 = na_range(s[2]) if HEADS[s[1]][0] == "na" else (0, 3)
                            c0, c1 = a0 * P, (a1 + 1) * P
                        sc.wait_ge(pT_ps, l * TS + n + 1)
                        if n >= 2:
                            sc.wait_ge(pv_done, l * TS + n - 1)
                        sc.activation(pT[:, n % 2, 0, c0:c1], ps[:, 4 + n % 2, c0:c1], ACT.Copy).then_inc(pT_hi, 1)
                    elif s[0] == "OUT":
                        pair = s[1]
                        o = PAIR_TILE[pair]
                        sc.wait_ge(pv_done, l * TS + T_AT[("TP", pair)] + 1)
                        sc.activation(hT[:, o, 0, 0:LAT], ps[:, 6, :], ACT.Copy)
                        sc.activation(hT[:, o, 0, LAT:T], ps[:, 7, 0:P], ACT.Copy).then_inc(o_hi, 1)
                    elif s[0] == "C":
                        g = s[1]
                        kind, h = HEADS[g]
                        gb = g % 2
                        if g >= 2:
                            sc.wait_ge(s_ready, l * UNITS + 5 * (g - 1))
                        if kind == "na":
                            sc.activation(K[:, gb, 0, LAT:640], kc_na[:, h, :], ACT.Copy).then_inc(kc_hi, 1)
                        elif kind == "gqa":
                            sc.activation(K[:, gb, 0, LAT:640], kc_g[:, h // 3, :], ACT.Copy).then_inc(kc_hi, 1)
                        elif h < 2:
                            sc.activation(K[64:96, gb, 0, LAT:640], kc_pe[64:96, :], ACT.Copy).then_inc(kc_hi, 1)
                    elif s[0] == "M":
                        what, g = s[1:]
                        kind, h = HEADS[g]
                        gb = g % 2
                        e = MISC_AT[(what, g)]
                        sc.wait_ge(misc_ps, l * NM + e + 1)
                        hi = 96 if kind == "mla" else 64
                        scale = MLA_SCALE if kind == "mla" else HD_SCALE
                        if what == "Qa":
                            i = sc.activation(Q[0:hi, gb, 0, 0:LAT], ps[0:hi, 7, :], ACT.Copy, scale=scale)
                        elif what == "Qb":
                            i = sc.activation(Q[0:hi, gb, 0, LAT:T], ps[0:hi, 7, 0:P], ACT.Copy, scale=scale)
                            if kind == "mla" and h < 2:
                                i = sc.activation(K[64:96, gb, 0, 640:KEYS], ps[64:96, 7, P:2 * P], ACT.Copy)
                            if kind != "mla":
                                for r0 in (0, 64):
                                    i = sc.activation(K[r0:r0 + 64, gb, 0, 640:KEYS], ps[0:64, 7, P:2 * P], ACT.Copy)
                        elif what == "Ka":
                            for r0 in (0,) if kind == "mla" else (0, 64):
                                i = sc.activation(K[r0:r0 + 64, gb, 0, 0:LAT], ps[0:64, 7, :], ACT.Copy)
                        elif what == "Kb":
                            i = sc.activation(K[0:64, gb, 0, LAT:KEYS], ps[0:64, 7, 0:256], ACT.Copy)
                        elif what == "Kpe":
                            i = sc.activation(K[64:96, gb, 0, 0:LAT], ps[64:96, 7, :], ACT.Copy)
                        else:
                            pair = g // 2
                            if what == "Va" and pair >= 2:
                                sc.wait_ge(pv_done, l * TS + T_AT[("TP", pair - 2)] + 1)
                            t0, n = (0, 4) if what == "Va" else (4, 2)
                            dst = v_slots(pair, 0, t0, n)
                            i = sc.activation(dst, ps[:, 7, 0:n * P].rearrange("p (t a b) -> p t a b", t=n, a=2), ACT.Copy)
                        i.then_inc(misc_hi, 1)
                    elif s[0] == "V":
                        g = s[1]
                        pair = g // 2
                        if pair >= 2:
                            sc.wait_ge(pv_done, l * TS + T_AT[("TP", pair - 2)] + 1)
                        for dst, src, _ in v_sources(g, 0):
                            i = sc.activation(dst, src, ACT.Copy)
                        i.then_inc(v_hi, 1)
                for o in range(KD):
                    sc.wait_ge(wo_in[o % 2], 16 * (l * (KD // 2) + o // 2 + 1))
                    if o >= 2:
                        sc.wait_ge(y_ps, l * XD + o - 1)
                    sc.activation(wo[:, o % 2, 0], wo_raw[:, o % 2], ACT.Copy).then_inc(wo_hi, 1)
                def gw_split(b):
                    sc.wait_ge(gw_in, 32 * (l * FB + b) + 32)
                    for w in range(2):
                        sc.activation(gw[:, w, 0], gw_raw[:, w], ACT.Copy).then_inc(gw_hi, 1)
                gw_split(0)
                for k in range(KD):
                    sc.wait_ge(x_done, l * XD + KD)
                    if k >= 2:
                        sc.wait_ge(ss_done, l * 2 * KD + KD + k - 1)
                    sc.activation(sq[:, k % 2], x[:, k], ACT.Square).then_inc(sq_ready, 1)
                rms(l * 2 + 2)
                modulated(l, 1)

                def ffn_block(b, last):
                    base = (l * FB + b) * 4
                    sc.wait_ge(dw_in, 16 * (l * FB + b) + 16)
                    sc.wait_ge(y_ps, l * XD + KD + b * KD)
                    sc.activation(dw[:, 0], dw_raw[:], ACT.Copy).then_inc(dw_hi, 1)
                    for j in range(2):
                        for hf_ in range(2):
                            sc.wait_ge(gu_ps, base * 2 + 4 * j + hf_ + 1)
                            sc.wait_ge(mm_ready, base + 2 * j - 2 + hf_ + 1) if j else sc.wait_ge(mm_ready, base)
                            sc.activation(sl[:, hf_], ps[:, 4 * j + hf_, 0:HALF], ACT.Silu).then_inc(sl_ready, 1)
                        for hf_ in range(2):
                            sc.wait_ge(mm_ready, base + 2 * j + hf_ + 1)
                            sc.activation(act[:, j, 0, hf_ * HALF:(hf_ + 1) * HALF], mm[:, hf_], ACT.Copy).then_inc(act_hi, 1)
                    if not last:
                        sc.wait_ge(gu_ps, base * 2 + 8)
                        gw_split(b + 1)

                with sc.Fori(0, FB - 1) as b:
                    ffn_block(b, False)
                ffn_block(FB - 1, True)
            sc.wait_ge(x_done, DEPTH * XD)
            for k in range(KD):
                if k >= 2:
                    sc.wait_ge(ss_done, DEPTH * 2 * KD + k - 1)
                sc.activation(sq[:, k % 2], x[:, k], ACT.Square).then_inc(sq_ready, 1)
            rms(DEPTH * 2 + 1)

        @block.vector
        def _(ve):
            def f(t):
                return t.bitcast(F32)

            def lo(dst, src, hi):
                return ve.tensor_tensor(dst, src, f(hi), ALU.subtract)

            def ada(l, t):
                ve.wait_ge(ada_ps, l * NADA + t + 1)
                bank = 7 if t >= ADA1 else 6 + t % 2
                ve.tensor_scalar(mod[:, t, :], ps[:, bank, 0:2], b_ada[:, l, t:t + 1], None, ALU.add).then_inc(ada_done, 1)

            def coefs(l, nrm):
                t0 = 24 * nrm + 8
                ve.wait_ge(ada_done, l * NADA + t0 + KD)
                ve.scalar_tensor_tensor(out=coef[:, nrm], in0=mod[:, t0:t0 + KD, :], scalar=1.0,
                                        in1=norm_g[:, l, nrm, :].unsqueeze(2).broadcast_to([P, KD, 2]),
                                        op0=ALU.add, op1=ALU.mult).then_inc(coef_done, 1)

            def mean_square(n, ss):
                ve.wait_ge(ss_done, ss)
                ve.tensor_scalar(rstd[:].rearrange("p (a b) -> p a b", a=2), ps[:, 0:2, 0:HALF], 1.0 / DM, EPS,
                                 ALU.mult, ALU.add).then_inc(ms_ready, 1)
                ve.wait_ge(rms_ready, n)
                ve.reciprocal(rstd[:], rstd[:]).then_inc(rstd_ready, 1)

            def modulated(l, nrm):
                base = l * 2 * KD + nrm * KD
                for k in range(KD):
                    ve.wait_ge(tn_ready, base + k + 1)
                    if k == 0:
                        ve.wait_ge(coef_done, 2 * l + nrm + 1)
                    else:
                        ve.wait_ge(h_ready, base + k)
                    for q, (c0, c1) in enumerate(((0, LAT), (LAT, T))):
                        i = ve.tensor_scalar(hf[:, c0:c1], tn[:, k % 2, c0:c1], coef[:, nrm, k, q:q + 1],
                                             mod[:, 24 * nrm + k, q:q + 1], ALU.mult, ALU.add)
                    i.then_inc(hf_ready, 1)
                    ve.wait_ge(hf_ready, base + k + 1)
                    ve.wait_ge(h_hi, base + k + 1)
                    lo(hT[:, k, 1], hf[:], hT[:, k, 0]).then_inc(h_ready, 1)

            def residual(l, y, o, banks, part):
                ve.wait_ge(y_ps, y)
                for hf_, c0, c1, q in ((0, 0, HALF, 0), (1, HALF, LAT, 0), (1, LAT, T, 1)):
                    s0 = c0 - hf_ * HALF
                    i = ve.scalar_tensor_tensor(out=x[:, o, c0:c1], in0=ps[:, banks + hf_, s0:s0 + c1 - c0],
                                                scalar=mod[:, part * KD + o, q:q + 1], in1=x[:, o, c0:c1],
                                                op0=ALU.mult, op1=ALU.add)
                i.then_inc(x_done, 1)

            ve.wait_ge(const_in, 16 * 8)
            with ve.Fori(0, DEPTH) as l:
                for t in range(ADA1):
                    ada(l, t)
                coefs(l, 0)
                mean_square(2 * l + 1, l * 2 * KD + KD)

                def wi_split(c):
                    ve.wait_ge(wi_hi, l * IC + c + 1)
                    lo(wi[:, c % 2, 1], wi_raw[:, c % 2], wi[:, c % 2, 0]).then_inc(wi_ready, 1)
                wi_split(0)
                wi_split(1)
                modulated(l, 0)
                for c in range(2, IC):
                    wi_split(c)
                    if c == 5:
                        ve.wait_ge(wqk_hi, 3 * l + 1)
                        lo(wq[:, :, 1, :], wq_raw[:], wq[:, :, 0, :]).then_inc(wq_ready, 1)
                ve.wait_ge(act_own, (l + 1) * 2 * NT)
                ve.tensor_scalar(stat[:, :, 0:1], stat[:, :, 0:1], 1.0 / 256, EPS, ALU.mult, ALU.add)
                ve.tensor_scalar(stat[:, :, 1:2], stat[:, :, 1:2], 1.0 / P, EPS, ALU.mult, ALU.add).then_inc(cstat_ms, 1)
                ve.wait_ge(cstat_rms, 2 * l + 1)
                ve.reciprocal(stat[:, :, 0:2], stat[:, :, 0:2]).then_inc(cstat, 1)
                ve.wait_ge(cstat, 2 * l + 1)
                ve.wait_ge(small_in, (l + 1) * 160)
                for t in range(NT):
                    ve.tensor_scalar(z[:, t, 0:256], z[:, t, 0:256], stat[:, t, 0:1], None, ALU.mult)
                    ve.scalar_tensor_tensor(out=z[:, t, OFF_CKV:OFF_KR], in0=z[:, t, OFF_CKV:OFF_KR],
                                            scalar=stat[:, t, 1:2], in1=kv_g[:], op0=ALU.mult, op1=ALU.mult).then_inc(c_norm, 1)
                ve.wait_ge(wqk_hi, 3 * l + 3)
                lo(wkv[:, 1], wkv_raw[:], wkv[:, 0])
                lo(ckvT[:, 1, LAT:640], kc_mla[:], ckvT[:, 0, LAT:640]).then_inc(wkv_ready, 1)
                for e in range(4):
                    ve.wait_ge(cT_hi, l * 4 + e + 1)
                    if e < 2:
                        ve.scalar_tensor_tensor(out=cqT[:, e, 1, 0:LAT], in0=ps[:, e, :], scalar=qn_g[:, l, e:e + 1],
                                                in1=f(cqT[:, e, 0, 0:LAT]), op0=ALU.mult, op1=ALU.subtract).then_inc(cT_ready, 1)
                    elif e == 2:
                        lo(ckvT[:, 1, 0:LAT], ps[:, e, :], ckvT[:, 0, 0:LAT]).then_inc(cT_ready, 1)
                    else:
                        for q in range(2):
                            ve.scalar_tensor_tensor(out=cqT[:, q, 1, LAT:T], in0=ps[:, 3, q * P:(q + 1) * P],
                                                    scalar=qn_g[:, l, q:q + 1], in1=f(cqT[:, q, 0, LAT:T]),
                                                    op0=ALU.mult, op1=ALU.subtract)
                        lo(ckvT[:, 1, 640:KEYS], ps[:, 3, 2 * P:3 * P], ckvT[:, 0, 640:KEYS]).then_inc(cT_ready, 1)
                for t in range(NT):
                    ve.wait_ge(gsq, l * NT + t + 1)
                    ve.tensor_reduce(stat[:, t, 2:10], ztmp[:].rearrange("p (h d) -> p h d", h=8), AX.X, ALU.add).then_inc(gstat, 1)
                ve.wait_ge(gstat, l * NT + NT)
                ve.tensor_scalar(stat[:, :, 2:10], stat[:, :, 2:10], 1.0 / 64, EPS, ALU.mult, ALU.add).then_inc(cstat_ms, 1)
                ve.wait_ge(cstat_rms, 2 * l + 2)
                ve.reciprocal(stat[:, :, 2:10], stat[:, :, 2:10]).then_inc(cstat, 1)
                ve.wait_ge(cstat, 2 * l + 2)
                ve.wait_ge(qm_ps, l * 2 * NT + 2 * NT)
                ve.wait_ge(vz_done, l + 1)
                for s in SCHED:
                    if s[0] == "S":
                        _, g, i = s
                        kind = HEADS[g][0]
                        u = S_AT[s]
                        bk = 2 * (u % 2)
                        ve.wait_ge(s_ready, l * UNITS + u + 1)
                        if i == 4:
                            src = ps[:, bk, 0:P]
                        elif kind == "na":
                            w = (NA_M[i][1] - NA_M[i][0] + 1) * P
                            if i == 0:
                                ve.wait_ge(bias_ready, l * 4 + g + 1)
                            ve.tensor_tensor(ps[:, bk, 0:w], ps[:, bk, 0:w], bias_h[:, NA_OFF[i]:NA_OFF[i] + w],
                                             ALU.add).then_inc(biased, 1)
                            ve.wait_ge(biased, l * 16 + 4 * g + i + 1)
                            src = ps[:, bk, 0:w + P]
                        else:
                            src = ps[:, bk:bk + 2, 0:HALF]
                        ve.tensor_reduce(negmax[:, u:u + 1], src, AX.XY if len(src.shape) == 3 else AX.X, ALU.max,
                                         negate=True).then_inc(max_ready, 1)
                        recip_later(ve, l, u - 1)
                        if u == UNITS - 1:
                            recip_later(ve, l, u)
                    elif s[0] in ("T", "TP"):
                        n = T_AT[s]
                        if s[0] == "TP":
                            c0, c1 = 0, 2 * P
                        else:
                            a0, a1 = na_range(s[2]) if HEADS[s[1]][0] == "na" else (0, 3)
                            c0, c1 = a0 * P, (a1 + 1) * P
                            if s[2] == 0 and s[1] < NH - 1:
                                pass
                        ve.wait_ge(pT_hi, l * TS + n + 1)
                        lo(pT[:, n % 2, 1, c0:c1], ps[:, 4 + n % 2, c0:c1], pT[:, n % 2, 0, c0:c1]).then_inc(pT_ready, 1)
                    elif s[0] == "OUT":
                        pair = s[1]
                        o = PAIR_TILE[pair]
                        ve.wait_ge(o_hi, l * NP + pair + 1)
                        lo(hT[:, o, 1, 0:LAT], ps[:, 6, :], hT[:, o, 0, 0:LAT])
                        lo(hT[:, o, 1, LAT:T], ps[:, 7, 0:P], hT[:, o, 0, LAT:T]).then_inc(o_ready, 1)
                    elif s[0] == "C":
                        g = s[1]
                        kind, h = HEADS[g]
                        gb = g % 2
                        if kind == "na":
                            n, src, r = g, kc_na[0:64, h, :], slice(0, 64)
                        elif kind == "gqa":
                            n, src, r = g - 4, kc_g[0:64, h // 3, :], slice(0, 64)
                        elif h < 2:
                            n, src, r = g, kc_pe[64:96, :], slice(64, 96)
                        else:
                            continue
                        ve.wait_ge(kc_hi, l * (NH - 4) + n + 1)
                        if kind != "mla" and h < 2:
                            ve.memset(K[64:P, gb, 1, :].bitcast(F32), 0.0)
                        lo(K[r, gb, 1, LAT:640], src, K[r, gb, 0, LAT:640])
                    elif s[0] == "M":
                        what, g = s[1:]
                        kind, h = HEADS[g]
                        gb = g % 2
                        ve.wait_ge(misc_hi, l * NM + MISC_AT[(what, g)] + 1)
                        if what in ("Qa", "Qb"):
                            c0, c1 = (0, LAT) if what == "Qa" else (LAT, T)
                            if kind == "mla":
                                r, dst, scale = slice(0, 96), Q[0:96, gb, 1, c0:c1], MLA_SCALE
                            else:
                                r, dst, scale = slice(0, 64), Q[64:P, gb, 0, c0:c1], HD_SCALE
                            i = ve.scalar_tensor_tensor(out=dst, in0=ps[r, 7, 0:c1 - c0], scalar=scale,
                                                        in1=f(Q[r, gb, 0, c0:c1]), op0=ALU.mult, op1=ALU.subtract)
                            if what == "Qb" and kind == "mla" and h < 2:
                                i = lo(K[64:96, gb, 1, 640:KEYS], ps[64:96, 7, P:2 * P], K[64:96, gb, 0, 640:KEYS])
                            if what == "Qb" and kind != "mla":
                                i = lo(K[0:64, gb, 1, 640:KEYS], ps[0:64, 7, P:2 * P], K[0:64, gb, 0, 640:KEYS])
                        elif what == "Ka":
                            r = slice(0, 64)
                            i = lo(K[r, gb, 1, 0:LAT], ps[r, 7, :], K[r, gb, 0, 0:LAT])
                        elif what == "Kb":
                            i = lo(K[0:64, gb, 1, LAT:KEYS], ps[0:64, 7, 0:256], K[0:64, gb, 0, LAT:KEYS])
                        elif what == "Kpe":
                            i = lo(K[64:96, gb, 1, 0:LAT], ps[64:96, 7, :], K[64:96, gb, 0, 0:LAT])
                        else:
                            pair = g // 2
                            t0, n = (0, 4) if what == "Va" else (4, 2)
                            src = ps[:, 7, 0:n * P].rearrange("p (t a b) -> p t a b", t=n, a=2)
                            i = lo(v_slots(pair, 1, t0, n), src, v_slots(pair, 0, t0, n))
                        i.then_inc(misc_done, 1)
                    elif s[0] == "V":
                        g = s[1]
                        ve.wait_ge(v_hi, l * NV + v_at(g // 2) + 1)
                        for dst, src, hi in v_sources(g, 1):
                            i = lo(dst, src, hi)
                        i.then_inc(v_ready, 1)
                    elif s[0] == "ADA":
                        ada(l, s[1])
                        if s[1] == 24 + 15:
                            coefs(l, 1)
                    elif s[0] == "GZ":
                        t = s[1]
                        zg = z[:, t, OFF_G:G_V].rearrange("p (h d) -> p h d", h=8)
                        ve.tensor_tensor(zg, zg, stat[:, t, 2:10].unsqueeze(2).broadcast_to([P, 8, 64]), ALU.mult).then_inc(dve_own, 1)
                        ve.wait_ge(dve_own, l * NT + t + 1)
                        ve.tensor_tensor(z[:, t, OFF_G:G_V], z[:, t, OFF_G:G_V], g8[:], ALU.mult).then_inc(g_norm, 1)
                for o in range(KD):
                    ve.wait_ge(wo_hi, l * KD + o + 1)
                    lo(wo[:, o % 2, 1], wo_raw[:, o % 2], wo[:, o % 2, 0]).then_inc(wo_ready, 1)
                    if o >= 1:
                        residual(l, l * XD + o, o - 1, 2 + 2 * ((o - 1) % 3), 2)
                residual(l, l * XD + KD, KD - 1, 2 + 2 * ((KD - 1) % 3), 2)

                def gw_split(b):
                    for w in range(2):
                        ve.wait_ge(gw_hi, 2 * (l * FB + b) + w + 1)
                        i = lo(gw[:, w, 1], gw_raw[:, w], gw[:, w, 0])
                    i.then_inc(gw_ready, 1)
                gw_split(0)
                mean_square(2 * l + 2, l * 2 * KD + 2 * KD)
                modulated(l, 1)

                def ffn_block(b, last):
                    base = (l * FB + b) * 4
                    ve.wait_ge(dw_hi, l * FB + b + 1)
                    lo(dw[:, 1], dw_raw[:], dw[:, 0]).then_inc(dw_ready, 1)

                    def gated(j, hf_):
                        ve.wait_ge(sl_ready, base + 2 * j + hf_ + 1)
                        ve.wait_ge(gu_ps, base * 2 + 4 * j + 2 + hf_ + 1)
                        if j:
                            ve.wait_ge(act_ready, base + hf_ + 1)
                        else:
                            ve.wait_ge(act_ready, base)
                        ve.tensor_tensor(mm[:, hf_], sl[:, hf_], ps[:, 4 * j + 2 + hf_, 0:HALF], ALU.mult).then_inc(mm_ready, 1)

                    def act_lo(j, hf_):
                        ve.wait_ge(act_hi, base + 2 * j + hf_ + 1)
                        cols = slice(hf_ * HALF, (hf_ + 1) * HALF)
                        lo(act[:, j, 1, cols], mm[:, hf_], act[:, j, 0, cols]).then_inc(act_ready, 1)
                    for j in range(2):
                        gated(j, 0)
                        gated(j, 1)
                        act_lo(j, 0)
                        act_lo(j, 1)
                    if not last:
                        gw_split(b + 1)
                    for o in range(KD):
                        residual(l, l * XD + KD + b * KD + o + 1, o, 2 * (o % 4), 5)

                with ve.Fori(0, FB - 1) as b:
                    ffn_block(b, False)
                ffn_block(FB - 1, True)
            mean_square(DEPTH * 2 + 1, DEPTH * 2 * KD + KD)
            ve.wait_ge(rstd_ready, DEPTH * 2 + 1)
            for k in range(KD):
                ve.scalar_tensor_tensor(out=x[:, k], in0=x[:, k], scalar=fin_g[:, k:k + 1], in1=rstd[:],
                                        op0=ALU.mult, op1=ALU.mult).then_inc(y_ready, 1)

        @block.gpsimd
        def _(po):
            def rotate(own, n, d, view, cos, sin, tmp):
                w = d // 4
                halves = view.rearrange("p h (a b w) -> p h a b w", a=2, b=2)
                s4 = sin.rearrange("p (a b w) -> p a b w", a=2, b=2)
                t4 = tmp.rearrange("p h (a b w) -> p h a b w", a=2, b=2)
                for b in range(2):
                    po.tensor_tensor(t4[:, :, :, b, :], halves[:, :, :, 1 - b, :],
                                     s4[:, :, b, :].unsqueeze(1).broadcast_to([P, n, 2, w]), ALU.mult).then_inc(pool_own, 1)
                po.wait_ge(pool_own, own + 2)
                po.tensor_tensor(view, view, cos.unsqueeze(1).broadcast_to([P, n, d]), ALU.mult).then_inc(pool_own, 1)
                po.wait_ge(pool_own, own + 3)
                return po.tensor_tensor(view, view, tmp, ALU.add)

            OWN = 8 * 4 + 4 * 3

            po.memset(ones[:], 1.0).then_inc(ones_set, 1)

            def modulated(base, n):
                po.wait_ge(rstd_ready, n)
                for k in range(KD):
                    if k >= 2:
                        po.wait_ge(h_ready, base + k - 1)
                    po.tensor_tensor(tn[:, k % 2], x[:, k], rstd[:], ALU.mult).then_inc(tn_ready, 1)

            with po.Fori(0, DEPTH) as l:
                modulated(l * 2 * KD, 2 * l + 1)
                po.wait_ge(z_done, l * IC * NT + IC * NT)
                po.wait_ge(kv_out, l * 64 + 64)
                po.wait_ge(qm_done, l * 2 * NT + 2 * NT)
                settled(po, passed_po)
                i = po.memset(V[:].bitcast(F32), 0.0)
                i.then_inc(vz_done, 1)
                step = 0
                for t in range(4):
                    kr = z[:, t, OFF_KR:OFF_NA].unsqueeze(1)
                    rotate(l * OWN + 4 * step, 1, 32, kr, rope[:, t, 0, 64:96], rope[:, t, 1, 64:96],
                           win[:, 0, 0:32].unsqueeze(1)).then_inc(pool_own, 1)
                    step += 1
                    po.wait_ge(pool_own, l * OWN + step * 4)
                for t in range(4):
                    q = qm[:, t, :].rearrange("p (h d) -> p h d", h=6)[:, :, 64:96]
                    tmp = win[:, 0, 0:192].rearrange("p (h d) -> p h d", h=6)
                    i = rotate(l * OWN + 4 * step, 6, 32, q, rope[:, t, 0, 64:96], rope[:, t, 1, 64:96], tmp)
                    i.then_inc(pool_own, 1)
                    step += 1
                    po.wait_ge(pool_own, l * OWN + step * 4)
                settled(po, passed_po)
                po.memset(win[0:1, 1, 0:1], 0.0).then_inc(q_roped, 1)
                po.wait_ge(q_roped, l + 1)

                def window(h):
                    v = a["rpb"][l, h, :]
                    src = bass.AP(tensor=v.tensor, offset=v.offset, ap=[[15, 16], [1, 8], [1, WIN]])
                    po.dma_start(win[:, h % 2, 0:WIN], src).then_inc(win_in[h % 2], 16)
                window(0)
                window(1)
                for s in SCHED:
                    if s[0] == "BM":
                        h = s[1]
                        po.wait_ge(win_in[h % 2], 16 * (2 * l + h // 2 + 1))
                        if h > 0:
                            po.wait_ge(max_ready, l * UNITS + 5 * h)
                        for n in range(4):
                            m0, m1 = NA_M[n]
                            cols = (m1 - m0 + 1) * 16
                            kc0 = 16 * (m0 - n) + 16
                            w = win[:, h % 2, :]
                            src = bass.AP(tensor=w.tensor, offset=w.offset + WIN - 1 - 15 * kc0,
                                          ap=[list(w.ap[0]), [-15, cols], [-1, ROWS]])
                            c0 = NA_OFF[n]
                            i = po.tensor_tensor(bias_h[:, c0:c0 + cols * ROWS].rearrange("p (c r) -> p c r", r=ROWS), src,
                                                 mask[:, c0 // ROWS:c0 // ROWS + cols].unsqueeze(2).broadcast_to([P, cols, ROWS]),
                                                 ALU.add)
                        i.then_inc(bias_ready, 1)
                        if h + 2 < 4:
                            po.wait_ge(bias_ready, l * 4 + h + 1)
                            window(h + 2)
                    elif s[0] == "S":
                        u = S_AT[s]
                        if u > 0:
                            norm_unit(po, l, u - 1)
                        if u == UNITS - 1:
                            norm_unit(po, l, u)
                    elif s[0] == "GZ" and s[1] < 4:
                        t = s[1]
                        po.wait_ge(g_norm, l * NT + t + 1)
                        view = z[:, t, OFF_G:G_V].rearrange("p (h d) -> p h d", h=8)
                        tmp = ztmp[:].rearrange("p (h d) -> p h d", h=8)
                        if t:
                            po.wait_ge(g_roped, l * 4 + t)
                        rotate(l * OWN + 32 + 3 * t, 8, 64, view, rope[:, t, 0, 0:64], rope[:, t, 1, 0:64], tmp).then_inc(g_roped, 1)
                        po.wait_ge(g_roped, l * 4 + t + 1)
                po.wait_ge(coef_done, 2 * l + 2)
                modulated(l * 2 * KD + KD, 2 * l + 2)



def constants():
    import numpy as np
    t = np.arange(LAT)
    col, row = (t // ROWS).astype(np.float32), (t % ROWS).astype(np.float32)

    def table(d):
        ax = d // 2
        inv = np.float32(10000.0) ** (-np.arange(0, ax, 2, dtype=np.float32) / np.float32(ax))
        ar, ac = row[:, None] * inv, col[:, None] * inv
        ang = np.concatenate([ar, ar, ac, ac], axis=-1).astype(np.float32)
        sign = np.repeat(np.array([-1, 1, -1, 1], np.float32), d // 4)
        return np.cos(ang), np.sin(ang) * sign
    (cg, sg), (cm, sm) = table(64), table(32)
    rope = np.stack([np.concatenate([cg, cm], 1), np.concatenate([sg, sm], 1)], 1).reshape(4, P, 2, 96)
    rope = np.ascontiguousarray(rope.transpose(1, 0, 2, 3)).astype(np.float32)
    parts = []
    for n in range(4):
        m0, m1 = NA_M[n]
        q = 16 * n + np.arange(P) // ROWS
        k = np.arange(16 * m0, 16 * (m1 + 1))
        start = np.clip(q - 8, 0, GRID_W - 16)[:, None]
        parts.append(np.where((k >= start) & (k < start + 16), 0.0, -1e30))
    mask = np.concatenate(parts, 1).astype(np.float32)
    return rope, mask, np.eye(P, dtype=np.float32)


def kernel(**inputs):
    import numpy as np
    import concourse.bacc as bacc
    from concourse.bass_utils import run_bass_kernel_spmd as run

    g = {k: np.asarray(v) for k, v in inputs.items()}
    tile = lambda v, *lead: np.ascontiguousarray(v)
    rope, mask, ident = constants()
    xs = g["x_sample"][0].reshape(ROWS, GRID_W, DM).transpose(1, 0, 2).reshape(LAT, DM)
    rpb = np.pad(g["na_rpb"].transpose(0, 1, 3, 2), ((0, 0), (0, 0), (16, 16), (0, 0)))
    rpb = rpb.reshape(DEPTH, 4, 63 * 15)[:, :, ::-1]
    feat = lambda v: v.reshape(*v.shape[:-1], -1, P)
    arrays = {
        "x": np.concatenate([xs, g["x_prompt"][0]], 0).T,
        "cond": np.stack([feat(g["c"][0]), feat(g["c_ctx"])], -1).transpose(1, 0, 2),
        "b_ada": feat(g["b_ada"]).transpose(2, 0, 1),
        "norm_g": np.stack([feat(g["norm_mix_g"]), feat(g["norm_ffn_g"])], 1).transpose(3, 0, 1, 2),
        "fin_g": feat(g["final_norm_g"]).T,
        "qn_g": feat(g["mla_q_norm_g"]).transpose(2, 0, 1),
        "kv_g": g["mla_kv_norm_g"],
        "g8": np.concatenate([np.tile(g["gqa_q_norm_g"], (1, 6)), np.tile(g["gqa_k_norm_g"], (1, 2))], 1),
        "rope": rope, "mask": mask, "ident": ident,
        "ckvT": g["cache_mla_ckv"][0].transpose(0, 2, 1),
        "krT": g["cache_mla_krope"][0].transpose(0, 2, 1),
        "na_kT": g["cache_na_k"][0].transpose(0, 3, 2, 1),
        "g_kT": g["cache_gqa_k"][0].transpose(0, 3, 2, 1),
        "na_v": g["cache_na_v"][0].reshape(DEPTH, P, 256),
        "g_v": g["cache_gqa_v"][0].reshape(DEPTH, P, P),
        "rpb": rpb,
        "w_ada": g["w_ada"], "w_in": g["w_in"], "w_q_up": g["w_q_up"], "w_kv_up": g["w_kv_up"],
        "w_out": g["w_out"], "w_gate": g["w_gate"], "w_up": g["w_up"], "w_down": g["w_down"],
    }
    outs = {"o_y": (DM, T), "o_ckv": (DEPTH, P, P), "o_kr": (DEPTH, P, 32), "o_nak": (DEPTH, P, 256),
            "o_nav": (DEPTH, P, 256), "o_gk": (DEPTH, P, P), "o_gv": (DEPTH, P, P)}
    nc = bacc.Bacc("TRN2", target_bir_lowering=False, num_devices=1)
    arrays = {k: np.ascontiguousarray(v) for k, v in arrays.items()}
    a = {k: nc.dram_tensor("in_" + k, v.shape, F32, kind="ExternalInput").ap() for k, v in arrays.items()}
    o = {k: nc.dram_tensor("out_" + k, s, F32, kind="ExternalOutput").ap() for k, s in outs.items()}
    build(nc, a, o)
    r = run(nc, [{"in_" + k: v for k, v in arrays.items()}], core_ids=[0]).results[0]
    y = r["out_o_y"].T
    ys = y[:LAT].reshape(GRID_W, ROWS, DM).transpose(1, 0, 2).reshape(1, LAT, DM)
    return (np.ascontiguousarray(y[LAT:])[None], np.ascontiguousarray(ys),
            r["out_o_ckv"][None], r["out_o_kr"][None], r["out_o_nak"].reshape(1, DEPTH, P, 4, 64),
            r["out_o_nav"].reshape(1, DEPTH, P, 4, 64), r["out_o_gk"].reshape(1, DEPTH, P, 2, 64),
            r["out_o_gv"].reshape(1, DEPTH, P, 2, 64))
```

```python
from contextlib import ExitStack

import concourse.bass as bass
from concourse import mybir

F32 = mybir.dt.float32
F32R = mybir.dt.float32r
ALU = mybir.AluOpType
ACT = mybir.ActivationFunctionType
AX = mybir.AxisListType

P = 128
DM = 1024
KD = DM // P
LAT, CTX, T = 512, 128, 640
HALF = T // 2
NT = T // P
DEPTH = 2
EPS = 1e-6
GRID_W, ROWS = 64, 8

OFF_CKV, OFF_KR, OFF_NA = 256, 384, 416
NA_Q, NA_K, NA_V = OFF_NA, OFF_NA + 256, OFF_NA + 512
OFF_G = OFF_NA + 768
G_K = OFF_G + 384
G_V = OFF_G + 512
IN_COLS = G_V + 128
IC = 8
ICW = IN_COLS // IC
QW = 576
FF = 2816
FB = FF // 256
NADA = 48
ADA1 = 16
POOL_ADA1 = [2, 5, 8, 11, 14]
POOL_ADA2 = [t for t in range(ADA1, NADA) if (t - ADA1) % 16 % 2 and (t - ADA1) % 16 < 15]
DVE_ADA1 = [t for t in range(ADA1) if t not in POOL_ADA1]
DVE_ADA2 = [t for t in range(ADA1, NADA) if t not in POOL_ADA2]
DVE_RING1, DVE_RING2, POOL_RING = 7, 2, 2
PSUMS = 2 * (len(POOL_ADA1) + len(POOL_ADA2))
NDVE = NADA - PSUMS // 2
DVE_GROUP = 3
POOL_GROUP = 2
KEYS = 768
WIN = 713
MLA_SCALE = 96.0 ** -0.5
HD_SCALE = 0.125

HEADS = [("na", h) for h in range(4)] + [("mla", h) for h in range(6)] + [("gqa", h) for h in range(6)]
PAIR_TILE = [3, 4, 0, 1, 2, 5, 6, 7]
NH = len(HEADS)
NP = NH // 2
UNITS = 5 * NH
TS = 5 * NH + NP
NA_M = [(0, 1), (0, 2), (1, 3), (2, 3)]
NA_OFF = [0, 256, 640, 1024]
NA_COLS = 1280


def na_range(m):
    if m == 4:
        return 0, 3
    ns = [n for n in range(4) if NA_M[n][0] <= m <= NA_M[n][1]]
    return ns[0], ns[-1]


def prep_steps(g):
    kind, h = HEADS[g]
    if kind == "mla":
        s = [("Qa", g), ("Qb", g), ("Ka", g), ("Kb", g)]
        if h < 2:
            s.append(("Kpe", g))
        return s
    return [("Ka", g), ("Qa", g), ("Qb", g)]


def schedule():
    def prep(g):
        steps = []
        if g < NH:
            steps += [("C", g)] + [("M",) + s for s in prep_steps(g)]
        if g >= 1 and g % 2 == 1:
            steps += [("M", "Va", g - 1), ("M", "Vb", g - 1)] if HEADS[g - 1][0] == "mla" else [("V", g - 1)]
        if g < NH and HEADS[g][0] == "na":
            steps.append(("BM", g))
        return steps

    slots = 5 * NH + 7
    extra = [[] for _ in range(2 * slots)]

    def spread(steps, first, count):
        for n, st in enumerate(steps):
            extra[2 * first + n * 2 * count // len(steps)].append(st)
    for g in range(NH):
        spread(prep(g + 1), 5 * g, 5)
    spread([("KR", t) for t in range(4)] + [("QR", t) for t in range(4)], 0, 12)
    spread([("GS", t) for t in range(NT)] + [("GR",)], 3, 12)
    spread([("WK",)], 6, 1)
    spread([("GZ", t) for t in range(NT)], 18, 20)
    order = [("BM", 0)]
    trans = []
    for g in range(NH):
        trans += [("T", g, m) for m in range(5)]
    late = []
    for n in range(slots):
        if n < 5 * NH:
            order.append(("S", n // 5, n % 5))
        order += late
        late = []
        order += extra[2 * n]
        k = n - 6
        if 0 <= k < len(trans):
            order.append(trans[k])
        order += extra[2 * n + 1]
        if 0 <= k < len(trans) and k % 10 == 9:
            order.append(("TP", k // 10))
            late = [("OUT", k // 10)]
    return order + late


SCHED = schedule()
HEAD0 = [("C", 0)] + [("M",) + s for s in prep_steps(0)]
MISC = [s[1:] for s in HEAD0 + SCHED if s[0] == "M"]
MISC_AT = {s: n for n, s in enumerate(MISC)}
NM = len(MISC)
T_AT = {s: n for n, s in enumerate([s for s in SCHED if s[0] in ("T", "TP")])}
S_AT = {s: n for n, s in enumerate([s for s in SCHED if s[0] == "S"])}
NV = 5


def kind_of_pair(pair):
    return HEADS[2 * pair][0]


def v_at(pair):
    return pair if pair < 2 else pair - 3


def last_t_of(g):
    return T_AT[("T", g, 4)]


def build(nc, a, out):
    ctx = ExitStack()
    with ctx:
        def sem(name):
            return ctx.enter_context(nc.semaphore(name))

        def sb(name, shape, dt=F32, scope=ctx):
            return scope.enter_context(nc.sbuf_tensor(name, shape, dt))

        x = sb("x", [P, KD, T])
        ada_w = sb("ada_w", [P, DVE_RING2, DM])
        mod = sb("mod", [P, NADA, 2])
        coef = sb("coef", [P, 2, KD, 2])
        rstd = sb("rstd", [P, T])
        b_ada = sb("b_ada", [P, DEPTH, NADA])
        norm_g = sb("norm_g", [P, DEPTH, 2, KD])
        fin_g = sb("fin_g", [P, KD])
        qn_g = sb("qn_g", [P, DEPTH, 2])
        kv_g = sb("kv_g", [P, P])
        g8 = sb("g8", [P, 512])
        rope = sb("rope", [P, 4, 2, 96])
        mask = sb("mask", [P, NA_COLS // ROWS])
        ident = sb("ident", [P, P])
        ones = sb("ones", [P, P])
        stat = sb("stat", [P, NT, 10])
        kc_na = sb("kc_na", [P, 4, P])
        kc_g = sb("kc_g", [P, 2, P])
        kc_mla = sb("kc_mla", [P, P])
        kc_pe = sb("kc_pe", [P, P])
        vc_na = sb("vc_na", [P, 256])
        vc_g = sb("vc_g", [P, P])
        negmax = sb("negmax", [P, UNITS])
        rsum = sb("rsum", [P, UNITS])
        rinv = sb("rinv", [P, UNITS])

        s1 = ExitStack()
        bias_h = sb("bias_h", [P, 2, NA_COLS], F32, s1)
        win = sb("win", [P, WIN + 7], F32, s1)
        sb("pad_h", [P, 10 * T - 2 * NA_COLS - WIN - 7], F32, s1)
        ckvT = sb("ckvT", [P, 2, KEYS], F32R, s1)
        wkv = sb("wkv", [P, 2, KEYS], F32R, s1)
        s1.close()
        hT = sb("hT", [P, KD, 2, T], F32R)

        s2 = ExitStack()
        sq = sb("sq", [P, 2, T], F32, s2)
        tn = sb("tn", [P, 2, T], F32, s2)
        hf = sb("hf", [P, T], F32, s2)
        ada_w1 = sb("ada_w1", [P, DVE_RING1 - DVE_RING2, DM], F32, s2)
        sb("pad_z", [P, NT * IN_COLS - 5 * T - (DVE_RING1 - DVE_RING2) * DM], F32, s2)
        ada_wp = sb("ada_wp", [P, POOL_RING, DM], F32, s2)
        s2.close()
        s3 = ExitStack()
        act = sb("act", [P, 2, 2, T], F32R, s3)
        sl = sb("sl", [P, 2, HALF], F32, s3)
        mm = sb("mm", [P, 2, HALF], F32, s3)
        wo_raw = sb("wo_raw", [P, 2, KD, P], F32, s3)
        wo = sb("wo", [P, 2, 2, KD, P], F32R, s3)
        dw_raw = sb("dw_raw", [P, 2, DM], F32, s3)
        s3.close()
        z = sb("z", [P, NT, IN_COLS])
        qm = sb("qm", [P, NT, QW])
        sb("z_end", [P, 32])

        s4 = ExitStack()
        wi_raw = sb("wi_raw", [P, 2, KD, ICW], F32, s4)
        wi = sb("wi", [P, 2, 2, KD, ICW], F32R, s4)
        s6 = ExitStack()
        silu_c = sb("silu_c", [P, 2, DM], F32, s6)
        s6.close()
        cqT = sb("cqT", [P, 2, 2, T], F32R, s4)
        wq_raw = sb("wq_raw", [P, 2, QW], F32, s4)
        wq = sb("wq", [P, 2, 2, QW], F32R, s4)
        s4.close()
        s5 = ExitStack()
        gw_raw = sb("gw_raw", [P, 2, KD, 256], F32, s5)
        gw = sb("gw", [P, 2, 2, KD, 256], F32R, s5)
        dw = sb("dw", [P, 2, 2, DM], F32R, s5)
        s5.close()
        V = sb("V", [P, 2, 2, 6, 192], F32R)
        K = sb("K", [P, 2, 2, KEYS], F32R)
        Q = sb("Q", [P, 2, 2, T], F32R)
        pT = sb("pT", [P, 2, 2, 512], F32R)
        probs = sb("probs", [P, 2, 4, T])
        probs_p = sb("probs_p", [P, 2, P])
        s7 = ExitStack()
        product = sb("product", [P, DM], F32, s7)
        s7.close()
        ztmp = sb("ztmp", [P, 512])
        wkv_raw = sb("wkv_raw", [P, KEYS])

        ps = ctx.enter_context(nc.psum_tensor("ps", [P, 8, 512], F32))

        const_in = sem("const_in")
        x_in = sem("x_in")
        small_in = sem("small_in")
        ones_set = sem("ones_set")
        cond_in = sem("cond_in")
        silu_done = sem("silu_done")
        dve_in1 = [sem(f"dve_in1_{i}") for i in range(DVE_RING1)]
        dve_in2 = [sem(f"dve_in2_{i}") for i in range(DVE_RING2)]
        pool_in = [sem(f"pool_in{i}") for i in range(POOL_RING)]
        product_ready = sem("product_ready")
        product_summed = sem("product_summed")
        ada_done = sem("ada_done")
        coef_done = sem("coef_done")
        sq_ready = sem("sq_ready")
        ss_done = sem("ss_done")
        ms_ready = sem("ms_ready")
        rms_ready = sem("rms_ready")
        rstd_ready = sem("rstd_ready")
        tn_ready = sem("tn_ready")
        hf_ready = sem("hf_ready")
        h_hi = sem("h_hi")
        h_ready = sem("h_ready")
        wi_in = [sem(f"wi_in{i}") for i in range(2)]
        wi_hi = sem("wi_hi")
        wi_ready = sem("wi_ready")
        z_ps = sem("z_ps")
        z_done = sem("z_done")
        wq_in = sem("wq_in")
        wkv_in = sem("wkv_in")
        wqk_hi = sem("wqk_hi")
        wq_ready = sem("wq_ready")
        wkv_ready = sem("wkv_ready")
        cstat = sem("cstat")
        cstat_ms = sem("cstat_ms")
        cstat_rms = sem("cstat_rms")
        c_norm = sem("c_norm")
        cT_ps = sem("cT_ps")
        cT_hi = sem("cT_hi")
        cT_ready = sem("cT_ready")
        gsq = sem("gsq")
        gstat = sem("gstat")
        qm_ps = sem("qm_ps")
        qm_done = sem("qm_done")
        q_roped = sem("q_roped")
        g_norm = sem("g_norm")
        g_roped = sem("g_roped")
        kv_out = sem("kv_out")
        norm_out = sem("norm_out")
        vz_done = sem("vz_done")
        win_in = sem("win_in")
        bias_ready = sem("bias_ready")
        misc_ps = sem("misc_ps")
        misc_hi = sem("misc_hi")
        misc_done = sem("misc_done")
        kc_hi = sem("kc_hi")
        v_hi = sem("v_hi")
        v_ready = sem("v_ready")
        s_ready = sem("s_ready")
        biased = sem("biased")
        max_ready = sem("max_ready")
        exp_done = sem("exp_done")
        rinv_ready = sem("rinv_ready")
        p_ready = sem("p_ready")
        p3_ready = sem("p3_ready")
        pT_ps = sem("pT_ps")
        pT_hi = sem("pT_hi")
        pT_ready = sem("pT_ready")
        pv_done = sem("pv_done")
        o_hi = sem("o_hi")
        o_ready = sem("o_ready")
        wo_in = [sem(f"wo_in{i}") for i in range(2)]
        wo_hi = sem("wo_hi")
        wo_ready = sem("wo_ready")
        y_ps = sem("y_ps")
        x_done = sem("x_done")
        gw_in = sem("gw_in")
        dw_in = sem("dw_in")
        gw_hi = sem("gw_hi")
        gw_ready = sem("gw_ready")
        dw_hi = sem("dw_hi")
        dw_ready = sem("dw_ready")
        gu_ps = sem("gu_ps")
        sl_ready = sem("sl_ready")
        mm_ready = sem("mm_ready")
        act_hi = sem("act_hi")
        act_ready = sem("act_ready")
        dve_own = sem("dve_own")
        dots = sem("dots")
        pool_own = sem("pool_own")
        act_own = sem("act_own")
        y_ready = sem("y_ready")
        passed_pe = sem("passed_pe")
        passed_sc = sem("passed_sc")
        passed_po = sem("passed_po")
        y_out = sem("y_out")

        XD = KD + FB * KD

        def settled(eng, passed):
            eng.sem_inc(passed, 1)

        block = ctx.enter_context(nc.Block())

        def v_slots(pair, q, t0, n):
            v = V[:, pair % 2, q, t0:t0 + n, :]
            return bass.AP(tensor=v.tensor, offset=v.offset, ap=[list(v.ap[0]), [192, n], [128, 2], [1, 64]])

        def v_sources(g, q):
            kind, h = HEADS[g]
            pair = g // 2
            res = []
            for slot in range(2):
                c0 = NA_V + 64 * (h + slot) if kind == "na" else G_V + 64 * ((h + slot) // 3)
                cc = 64 * (h + slot) if kind == "na" else 64 * ((h + slot) // 3)
                cache = vc_na if kind == "na" else vc_g
                d0 = 128 * slot
                res.append((V[:, pair % 2, q, 0:NT, d0:d0 + 64], z[:, 0:NT, c0:c0 + 64], V[:, pair % 2, 0, 0:NT, d0:d0 + 64]))
                res.append((V[:, pair % 2, q, 5, d0:d0 + 64], cache[:, cc:cc + 64], V[:, pair % 2, 0, 5, d0:d0 + 64]))
            return res

        def dve_slot(t):
            tiles, ring, arrived = (DVE_ADA1, DVE_RING1, dve_in1) if t < ADA1 else (DVE_ADA2, DVE_RING2, dve_in2)
            n = tiles.index(t)
            slot = n % ring
            per_layer = len(range(slot, len(tiles), ring))
            where = ada_w[:, slot] if slot < DVE_RING2 else ada_w1[:, slot - DVE_RING2]
            return where, arrived[slot], lambda l: 16 * (l * per_layer + n // ring + 1)

        def pool_slot(t):
            tiles = POOL_ADA1 + POOL_ADA2
            n = tiles.index(t)
            slot = n % POOL_RING
            per_layer = len(range(slot, len(tiles), POOL_RING))
            return ada_wp[:, slot], pool_in[slot], lambda l: 16 * (l * per_layer + n // POOL_RING + 1), n

        def in_flight(u, lag):
            return ([u - lag] if u >= lag else []) + (list(range(UNITS - lag, UNITS)) if u == UNITS - 1 else [])

        def reciprocals(ve, l, u):
            for w in in_flight(u, 2):
                ve.wait_ge(exp_done, l * UNITS + w + 1)
                ve.reciprocal(rinv[:, w:w + 1], rsum[:, w:w + 1]).then_inc(rinv_ready, 1)
                norm_unit(ve, l, w, (3,))

        def norm_unit(po, l, u, tiles):
            g, i = u // 5, u % 5
            if i not in tiles:
                return
            kind = HEADS[g][0]
            if i == 4:
                t = probs_p[:, g % 2, :]
            elif kind == "na":
                t = probs[:, g % 2, i, 0:(NA_M[i][1] - NA_M[i][0] + 2) * P]
            else:
                t = probs[:, g % 2, i, :]
            po.wait_ge(rinv_ready, l * UNITS + u + 1)
            if i == 3:
                po.tensor_scalar(t, t, rinv[:, u:u + 1], None, ALU.mult).then_inc(p3_ready, 1)
            else:
                settled(po, passed_po)
                po.tensor_scalar(t, t, rinv[:, u:u + 1], None, ALU.mult).then_inc(p_ready, 1)

        @block.sync
        def _(sp):
            for dst, src in ((b_ada, a["b_ada"]), (norm_g, a["norm_g"]), (fin_g, a["fin_g"]),
                             (qn_g, a["qn_g"]), (rope, a["rope"]), (mask, a["mask"]), (ident, a["ident"])):
                sp.dma_start(dst[:], src).then_inc(const_in, 16)
            for k in range(KD):
                sp.dma_start(x[:, k, :], a["x"][k * P:(k + 1) * P, :]).then_inc(x_in, 16)

            def ada_load(l, t):
                if t in POOL_ADA1 + POOL_ADA2:
                    dst, arrived, _, n = pool_slot(t)
                    if n >= POOL_RING:
                        sp.wait_ge(product_summed, l * PSUMS + 2 * (n - POOL_RING) + 2)
                elif t < ADA1:
                    dst, arrived, _ = dve_slot(t)
                    n = DVE_ADA1.index(t)
                    if n >= DVE_RING1:
                        sp.wait_ge(dots, 2 * (l * NDVE + n - DVE_RING1 + 1))
                else:
                    dst, arrived, _ = dve_slot(t)
                    n = len(DVE_ADA1) + DVE_ADA2.index(t)
                    sp.wait_ge(dots, 2 * (l * NDVE + n - DVE_RING2 + 1))
                sp.dma_start(dst, a["w_adaT"][l, t * P:(t + 1) * P, :]).then_inc(arrived, 16)

            def wi_load(l, c):
                if c >= 2:
                    sp.wait_ge(wi_ready, l * IC + c - 1)
                sp.dma_start(wi_raw[:, c % 2], a["w_in"][l, :, c * ICW:(c + 1) * ICW]
                             .rearrange("(k p) n -> p k n", p=P)).then_inc(wi_in[c % 2], 16)

            with sp.Fori(0, DEPTH) as l:
                sp.wait_ge(x_done, l * XD + 1)
                sp.dma_start(silu_c[:], a["cond"].unsqueeze(0).broadcast_to([P, 2, DM])).then_inc(cond_in, 16)
                for t in range(ADA1):
                    ada_load(l, t)
                    if t == 8:
                        wi_load(l, 0)
                wi_load(l, 1)
                sp.dma_start(kv_g[:], a["kv_g"][bass.ts(l, 1), :].to_broadcast([P, P])).then_inc(small_in, 16)
                sp.dma_start(g8[:], a["g8"][bass.ts(l, 1), :].to_broadcast([P, 512])).then_inc(small_in, 16)
                for r in range(2):
                    sp.dma_start(kc_na[64 * r:64 * r + 64], a["na_kT"][l]).then_inc(small_in, 16)
                    sp.dma_start(kc_g[64 * r:64 * r + 64], a["g_kT"][l]).then_inc(small_in, 16)
                sp.dma_start(kc_mla[:], a["ckvT"][l]).then_inc(small_in, 16)
                sp.dma_start(kc_pe[64:96, :], a["krT"][l]).then_inc(small_in, 16)
                sp.dma_start(vc_na[:], a["na_v"][l]).then_inc(small_in, 16)
                sp.dma_start(vc_g[:], a["g_v"][l]).then_inc(small_in, 16)
                for c in range(1, IC):
                    if c + 1 < IC:
                        wi_load(l, c + 1)
                    if c == 1:
                        sp.dma_start(wq_raw[:], a["w_q_up"][l].rearrange("(k p) n -> p k n", p=P)).then_inc(wq_in, 16)
                    if c >= 2:
                        for t in DVE_ADA2[DVE_GROUP * (c - 2):DVE_GROUP * (c - 1)]:
                            ada_load(l, t)
                    for t in POOL_ADA2[POOL_GROUP * (c - 1):POOL_GROUP * c]:
                        ada_load(l, t)
                sp.wait_ge(product_summed, (l + 1) * PSUMS)
                sp.dma_start(wkv_raw[:], a["w_kv_up"][l]).then_inc(wkv_in, 16)
                tile = NT - 1
                sp.wait_ge(z_done, l * IC * NT + IC * NT)
                for name, c0, w in (("o_kr", OFF_KR, 32), ("o_nak", NA_K, 256), ("o_nav", NA_V, 256), ("o_gv", G_V, P)):
                    sp.dma_start(out[name][l], z[:, tile, c0:c0 + w]).then_inc(kv_out, 16)
                sp.wait_ge(c_norm, l * NT + NT)
                sp.dma_start(out["o_ckv"][l], z[:, tile, OFF_CKV:OFF_KR]).then_inc(norm_out, 16)
                for s in SCHED:
                    if s[0] == "GZ" and s[1] == NT - 1:
                        sp.wait_ge(g_norm, l * NT + NT)
                        sp.dma_start(out["o_gk"][l], z[:, tile, G_K:G_V]).then_inc(norm_out, 16)
                sp.wait_ge(misc_done, l * NM + NM)
                sp.wait_ge(v_ready, l * NV + NV)
                sp.wait_ge(kv_out, l * 64 + 64)
                sp.wait_ge(norm_out, l * 32 + 32)
                for o in range(KD):
                    if o >= 2:
                        sp.wait_ge(wo_ready, l * KD + o - 1)
                    sp.dma_start(wo_raw[:, o % 2], a["w_out"][l, :, o * P:(o + 1) * P]
                                 .rearrange("(k p) n -> p k n", p=P)).then_inc(wo_in[o % 2], 16)
                    if o == 1:
                        sp.wait_ge(o_ready, l * NP + NP)
                        sp.dma_start(gw_raw[:, 0], a["w_gate"][l, :, 0:256].rearrange("(k p) n -> p k n", p=P)).then_inc(gw_in, 16)
                        sp.dma_start(gw_raw[:, 1], a["w_up"][l, :, 0:256].rearrange("(k p) n -> p k n", p=P)).then_inc(gw_in, 16)
                        sp.dma_start(dw_raw[:], a["w_down"][l, 0:256, :].rearrange("(j p) n -> p j n", p=P)).then_inc(dw_in, 16)
                with sp.Fori(1, FB) as b:
                    sp.wait_ge(gw_ready, l * FB + b)
                    sp.dma_start(gw_raw[:, 0], a["w_gate"][l, :, bass.ts(b, 256)].rearrange("(k p) n -> p k n", p=P)).then_inc(gw_in, 16)
                    sp.dma_start(gw_raw[:, 1], a["w_up"][l, :, bass.ts(b, 256)].rearrange("(k p) n -> p k n", p=P)).then_inc(gw_in, 16)
                    sp.wait_ge(dw_ready, l * FB + b)
                    sp.dma_start(dw_raw[:], a["w_down"][l, bass.ts(b, 256), :].rearrange("(j p) n -> p j n", p=P)).then_inc(dw_in, 16)
            for k in range(KD):
                sp.wait_ge(y_ready, k + 1)
                sp.dma_start(out["o_y"][k * P:(k + 1) * P, :], x[:, k]).then_inc(y_out, 16)
            sp.wait_ge(y_out, 16 * KD)
            sp.wait_ge(kv_out, DEPTH * 64)
            sp.wait_ge(norm_out, DEPTH * 32)

        @block.tensor
        def _(pe):
            def split_mm(dst, lh, ll, rh, rl, start, stop):
                pe.matmul(dst, lh, rh, start=start, stop=False, skip_group_check=True)
                pe.matmul(dst, lh, rl, start=False, stop=False, skip_group_check=True)
                return pe.matmul(dst, ll, rh, start=False, stop=stop, skip_group_check=True)

            def sum_squares(base, k):
                pe.wait_ge(sq_ready, base + k + 1)
                for j in range(2):
                    m = pe.matmul(ps[:, j, 0:HALF], ones[:], sq[:, k % 2, j * HALF:(j + 1) * HALF],
                                  start=k == 0, stop=k == KD - 1, skip_group_check=True)
                m.then_inc(ss_done, 1)

            prev7 = [None]

            def take7(l):
                done, per_layer, n = prev7[0]
                pe.wait_ge(done, l * per_layer + n)

            def misc_step(l, what, g):
                kind, h = HEADS[g]
                take7(l)
                settled(pe, passed_pe)
                if what in ("Qa", "Qb"):
                    if kind == "mla" and g == 4 and what == "Qa":
                        pe.wait_ge(q_roped, 8 * l + 8)
                    if kind == "gqa" and what == "Qa" and h == 0:
                        pe.wait_ge(g_roped, l * 4 + 4)
                        settled(pe, passed_pe)
                if what == "Qa" or (what == "Ka" and kind != "mla") or what == "Qb":
                    ts_ = range(4) if what != "Qb" else [4]
                    for t in ts_:
                        o0 = (t % 4) * P
                        if kind == "mla":
                            m = pe.transpose(ps[0:96, 7, o0:o0 + P], qm[:, t, h * 96:(h + 1) * 96], ident[:])
                            if what == "Qb" and h < 2:
                                m = pe.transpose(ps[0:96, 7, P:2 * P], z[:, t, OFF_KR - 64:OFF_NA], ident[:])
                        else:
                            qc = (NA_Q if kind == "na" else OFF_G) + 64 * h
                            kc = NA_K + 64 * h if kind == "na" else G_K + 64 * (h // 3)
                            c0 = kc if what == "Ka" else qc
                            if kind == "gqa" and what == "Ka" and h == 0 and t == 0:
                                pe.wait_ge(g_roped, l * 4 + 4)
                                pe.wait_ge(g_norm, l * NT + NT)
                                settled(pe, passed_pe)
                            m = pe.transpose(ps[0:64, 7, o0:o0 + P], z[:, t, c0:c0 + 64], ident[:])
                            if what == "Qb":
                                m = pe.transpose(ps[0:64, 7, P:2 * P], z[:, t, kc:kc + 64], ident[:])
                elif what in ("Ka", "Kb"):
                    c0, c1 = (0, LAT) if what == "Ka" else (LAT, KEYS)
                    if g == 4:
                        pe.wait_ge(wkv_ready, l + 1)
                    m = split_mm(ps[0:64, 7, 0:c1 - c0], wkv[:, 0, h * P:h * P + 64], wkv[:, 1, h * P:h * P + 64],
                                 ckvT[:, 0, c0:c1], ckvT[:, 1, c0:c1], True, True)
                elif what == "Kpe":
                    for t in range(4):
                        m = pe.transpose(ps[0:96, 7, t * P:(t + 1) * P], z[:, t, OFF_KR - 64:OFF_NA], ident[:])
                else:
                    tiles = [0, 1, 2, 3] if what == "Va" else [4, 5]
                    for n, t in enumerate(tiles):
                        k0 = {4: 640, 5: LAT}.get(t, t * P)
                        src = [wkv[:, q, h * P:(h + 2) * P].rearrange("p (a b) -> p a b", a=2)[:, :, 64:P] for q in range(2)]
                        m = split_mm(ps[:, 7, n * P:(n + 1) * P], ckvT[:, 0, k0:k0 + P], ckvT[:, 1, k0:k0 + P],
                                     src[0], src[1], True, True)
                m.then_inc(misc_ps, 1)
                prev7[0] = (misc_done, NM, MISC_AT[(what, g)] + 1)

            pe.wait_ge(ones_set, 1)
            pe.wait_ge(const_in, 16 * 7)
            with pe.Fori(0, DEPTH) as l:
                pe.wait_ge(x_done, l * XD + 1)
                for k in range(KD):
                    sum_squares(l * 2 * KD, k)
                for c in range(IC):
                    pe.wait_ge(wi_ready, l * IC + c + 1)
                    for t in range(NT):
                        n = c * NT + t
                        if c == 0 and t == 0:
                            for k in range(KD):
                                pe.wait_ge(h_ready, l * 2 * KD + k + 1)
                                m = split_mm(ps[:, 0, 0:ICW], hT[:, k, 0, 0:P], hT[:, k, 1, 0:P],
                                             wi[:, 0, 0, k, :], wi[:, 0, 1, k, :], k == 0, k == KD - 1)
                            m.then_inc(z_ps, 1)
                            continue
                        if n >= 6:
                            pe.wait_ge(z_done, l * IC * NT + n - 5)
                        for k in range(KD):
                            m = split_mm(ps[:, n % 6, 0:ICW], hT[:, k, 0, t * P:(t + 1) * P], hT[:, k, 1, t * P:(t + 1) * P],
                                         wi[:, c % 2, 0, k, :], wi[:, c % 2, 1, k, :], k == 0, k == KD - 1)
                        m.then_inc(z_ps, 1)
                pe.wait_ge(z_done, l * IC * NT + IC * NT)
                prev7[0] = (ada_done, 2, 2)
                misc_step(l, "Ka", 0)
                pe.wait_ge(c_norm, l * NT + NT)
                for e in range(3):
                    for t in range(4):
                        m = pe.transpose(ps[:, e, t * P:(t + 1) * P], z[:, t, e * P:(e + 1) * P], ident[:])
                    m.then_inc(cT_ps, 1)
                    if e == 1:
                        misc_step(l, "Qa", 0)
                for e in range(3):
                    m = pe.transpose(ps[:, 3, e * P:(e + 1) * P], z[:, 4, e * P:(e + 1) * P], ident[:])
                m.then_inc(cT_ps, 1)
                misc_step(l, "Qb", 0)
                pe.wait_ge(cT_ready, l * 4 + 4)
                pe.wait_ge(wq_ready, l + 1)
                for n in range(2 * NT):
                    t, j = n // 2, n % 2
                    if n >= 3:
                        pe.wait_ge(qm_done, l * 2 * NT + n - 2)
                    for e in range(2):
                        m = split_mm(ps[:, 4 + n % 3, 0:288], cqT[:, e, 0, t * P:(t + 1) * P], cqT[:, e, 1, t * P:(t + 1) * P],
                                     wq[:, e, 0, j * 288:(j + 1) * 288], wq[:, e, 1, j * 288:(j + 1) * 288], e == 0, e == 1)
                    m.then_inc(qm_ps, 1)
                pe.wait_ge(qm_done, l * 2 * NT + 2 * NT)
                pending = []

                def flush():
                    if pending:
                        pending.pop()()

                for s in SCHED:
                    if s[0] == "S":
                        _, g, i = s
                        kind = HEADS[g][0]
                        u, gb = S_AT[s], g % 2
                        if i == 0:
                            pe.wait_ge(misc_done, l * NM + MISC_AT[prep_steps(g)[-1]] + 1)
                        if u >= 2:
                            pe.wait_ge(exp_done, l * UNITS + u - 1)
                        bk = 2 * (u % 2)
                        qs = slice(i * P, (i + 1) * P)
                        if i == 4:
                            parts = [(bk, 0, P, 640)]
                        elif kind == "na":
                            m0, m1 = NA_M[i]
                            w = (m1 - m0 + 1) * P
                            parts = [(bk, 0, w, m0 * P), (bk, w, P, LAT)]
                        else:
                            parts = [(bk, 0, HALF, 0), (bk + 1, 0, HALF, HALF)]
                        for n, (bank, c0, w, k0) in enumerate(parts):
                            dst = ps[:, bank, c0:c0 + w]
                            first = c0 == 0
                            if kind == "mla":
                                m = split_mm(dst, Q[0:96, gb, 0, qs], Q[0:96, gb, 1, qs], K[0:96, gb, 0, k0:k0 + w],
                                             K[0:96, gb, 1, k0:k0 + w], first, True)
                            else:
                                pe.matmul(dst, Q[:, gb, 0, qs], K[:, gb, 0, k0:k0 + w], start=first, stop=False,
                                          skip_group_check=True)
                                m = pe.matmul(dst, Q[:, gb, 0, qs], K[:, gb, 1, k0:k0 + w], start=False, stop=True,
                                              skip_group_check=True)
                        m.then_inc(s_ready, 1)
                    elif s[0] == "T":
                        _, g, mt = s
                        kind = HEADS[g][0]
                        n = T_AT[s]
                        if mt == 0:
                            pe.wait_ge(p_ready, l * 4 * NH + 4 * g + 3)
                            pe.wait_ge(p3_ready, l * NH + g + 1)
                        if n >= 2:
                            pe.wait_ge(pT_ready, l * TS + n - 1)
                        a0, a1 = na_range(mt) if kind == "na" else (0, 3)
                        for i in range(a0, a1 + 1):
                            if kind == "na":
                                m0, m1 = NA_M[i]
                                pos = (m1 - m0 + 1 if mt == 4 else mt - m0) * P
                            else:
                                pos = mt * P
                            m = pe.transpose(ps[:, 4 + n % 2, i * P:(i + 1) * P], probs[:, g % 2, i, pos:pos + P], ident[:])
                        m.then_inc(pT_ps, 1)
                        flush()

                        def pv(g=g, mt=mt, n=n, a0=a0, a1=a1):
                            pair, slot = g // 2, g % 2
                            if slot == 0 and mt == 0:
                                if kind_of_pair(pair) == "mla":
                                    pe.wait_ge(misc_done, l * NM + MISC_AT[("Vb", 2 * pair)] + 1)
                                else:
                                    pe.wait_ge(v_ready, l * NV + v_at(pair) + 1)
                                if pair > 0:
                                    pe.wait_ge(o_ready, l * NP + pair)
                            pe.wait_ge(pT_ready, l * TS + n + 1)
                            vt = 5 if mt == 4 else mt
                            cols = slice(a0 * P, (a1 + 1) * P)
                            lh, ll = (V[:, pair % 2, q, vt, 64 * slot:64 * slot + P] for q in range(2))
                            m = split_mm(ps[:, 6, cols], lh, ll, pT[:, n % 2, 0, cols], pT[:, n % 2, 1, cols],
                                         slot == 0 and mt == 0, False)
                            m.then_inc(pv_done, 1)
                        pending.append(pv)
                    elif s[0] == "TP":
                        pair = s[1]
                        n = T_AT[s]
                        pe.wait_ge(p_ready, l * 4 * NH + 8 * pair + 8)
                        pe.wait_ge(pT_ready, l * TS + n - 1)
                        for slot in range(2):
                            m = pe.transpose(ps[:, 4 + n % 2, slot * P:(slot + 1) * P], probs_p[:, slot, :], ident[:])
                        m.then_inc(pT_ps, 1)
                        flush()

                        def pvp(pair=pair, n=n):
                            pe.wait_ge(pT_ready, l * TS + n + 1)
                            take7(l)
                            for slot in range(2):
                                lh, ll = (V[:, pair % 2, q, 4, 64 * slot:64 * slot + P] for q in range(2))
                                cols = slice(slot * P, (slot + 1) * P)
                                m = split_mm(ps[:, 7, 0:P], lh, ll, pT[:, n % 2, 0, cols], pT[:, n % 2, 1, cols],
                                             slot == 0, slot == 1)
                            m.then_inc(pv_done, 1)
                            prev7[0] = (o_ready, NP, pair + 1)
                        pending.append(pvp)
                    elif s[0] == "OUT":
                        flush()
                    elif s[0] == "M":
                        misc_step(l, *s[1:])
                pe.wait_ge(o_ready, l * NP + NP)
                for o in range(KD):
                    pe.wait_ge(wo_ready, l * KD + o + 1)
                    if o >= 3:
                        pe.wait_ge(x_done, l * XD + 1 + o - 2)
                    for j in range(2):
                        for k in range(KD):
                            cols = slice(j * HALF, (j + 1) * HALF)
                            m = split_mm(ps[:, 2 + 2 * (o % 3) + j, 0:HALF], wo[:, o % 2, 0, k, :], wo[:, o % 2, 1, k, :],
                                         hT[:, k, 0, cols], hT[:, k, 1, cols], k == 0, k == KD - 1)
                    m.then_inc(y_ps, 1)
                for k in range(KD):
                    sum_squares(l * 2 * KD + KD, k)
                pe.wait_ge(h_ready, l * 2 * KD + 2 * KD)
                settled(pe, passed_pe)

                def ffn_block(b):
                    for j in range(2):
                        for w in range(2):
                            pe.wait_ge(x_done, l * XD + 1 + KD + b * KD - 3 + 2 * j + w)
                            if j == 0:
                                pe.wait_ge(gw_ready, l * FB + b + 1)
                            for hf_ in range(2):
                                cols = slice(hf_ * HALF, (hf_ + 1) * HALF)
                                for k in range(KD):
                                    m = split_mm(ps[:, 4 * j + 2 * w + hf_, 0:HALF], gw[:, w, 0, k, j * P:(j + 1) * P],
                                                 gw[:, w, 1, k, j * P:(j + 1) * P], hT[:, k, 0, cols], hT[:, k, 1, cols],
                                                 k == 0, k == KD - 1)
                                m.then_inc(gu_ps, 1)
                    base = (l * FB + b) * 4

                    def down(o, j, hf_):
                        cols = slice(hf_ * HALF, (hf_ + 1) * HALF)
                        return split_mm(ps[:, 2 * (o % 4) + hf_, 0:HALF], dw[:, 0, j, o * P:(o + 1) * P],
                                        dw[:, 1, j, o * P:(o + 1) * P], act[:, j, 0, cols], act[:, j, 1, cols],
                                        j == 0, j == 1)
                    pe.wait_ge(dw_ready, l * FB + b + 1)
                    pe.wait_ge(act_ready, base + 3)
                    for o in range(2):
                        for hf_ in range(2):
                            down(o, 0, hf_)
                    pe.wait_ge(act_ready, base + 4)
                    for o in range(2):
                        down(o, 1, 0)
                    pe.wait_ge(act_ready, base + 5)
                    for o in range(2):
                        down(o, 1, 1).then_inc(y_ps, 1)
                    for o in range(2, KD):
                        if o >= 4:
                            pe.wait_ge(x_done, l * XD + 1 + KD + b * KD + o - 3)
                        for hf_ in range(2):
                            for j in range(2):
                                m = down(o, j, hf_)
                        m.then_inc(y_ps, 1)

                with pe.Fori(0, FB) as b:
                    ffn_block(b)
            pe.wait_ge(x_done, DEPTH * XD + 1)
            for k in range(KD):
                sum_squares(DEPTH * 2 * KD, k)

        @block.scalar
        def _(sc):
            def square(base, k, first):
                if not first or k >= 2:
                    sc.wait_ge(ss_done, base + k - 1)
                sc.activation(sq[:, k % 2], x[:, k], ACT.Square).then_inc(sq_ready, 1)

            def rms(n):
                sc.wait_ge(ms_ready, n)
                sc.activation(rstd[:], rstd[:], ACT.Sqrt).then_inc(rms_ready, 1)

            def modulated(l, nrm):
                base = l * 2 * KD + nrm * KD
                sc.wait_ge(coef_done, l * 2 + nrm + 1)
                for k in range(KD):
                    sc.wait_ge(tn_ready, base + k + 1)
                    for q, (c0, c1) in enumerate(((0, LAT), (LAT, T))):
                        i = sc.activation(hT[:, k, 0, c0:c1], tn[:, k % 2, c0:c1], ACT.Identity,
                                          bias=mod[:, 24 * nrm + k, q:q + 1], scale=coef[:, nrm, k, q:q + 1])
                    i.then_inc(h_hi, 1)

            def cached_keys(l, g):
                kind, h = HEADS[g]
                gb = g % 2
                if g >= 2:
                    sc.wait_ge(s_ready, l * UNITS + 5 * (g - 1))
                if kind == "na":
                    sc.activation(K[:, gb, 0, LAT:640], kc_na[:, h, :], ACT.Copy).then_inc(kc_hi, 1)
                elif kind == "gqa":
                    sc.activation(K[:, gb, 0, LAT:640], kc_g[:, h // 3, :], ACT.Copy).then_inc(kc_hi, 1)
                elif h < 2:
                    sc.activation(K[64:96, gb, 0, LAT:640], kc_pe[64:96, :], ACT.Copy).then_inc(kc_hi, 1)

            def misc_hi_part(l, what, g):
                kind, h = HEADS[g]
                gb = g % 2
                e = MISC_AT[(what, g)]
                sc.wait_ge(misc_ps, l * NM + e + 1)
                hi = 96 if kind == "mla" else 64
                scale = MLA_SCALE if kind == "mla" else HD_SCALE
                if what == "Qa":
                    i = sc.activation(Q[0:hi, gb, 0, 0:LAT], ps[0:hi, 7, :], ACT.Copy, scale=scale)
                elif what == "Qb":
                    i = sc.activation(Q[0:hi, gb, 0, LAT:T], ps[0:hi, 7, 0:P], ACT.Copy, scale=scale)
                    if kind == "mla" and h < 2:
                        i = sc.activation(K[64:96, gb, 0, 640:KEYS], ps[64:96, 7, P:2 * P], ACT.Copy)
                    if kind != "mla":
                        for r0 in (0, 64):
                            i = sc.activation(K[r0:r0 + 64, gb, 0, 640:KEYS], ps[0:64, 7, P:2 * P], ACT.Copy)
                elif what == "Ka":
                    for r0 in (0,) if kind == "mla" else (0, 64):
                        i = sc.activation(K[r0:r0 + 64, gb, 0, 0:LAT], ps[0:64, 7, :], ACT.Copy)
                elif what == "Kb":
                    i = sc.activation(K[0:64, gb, 0, LAT:KEYS], ps[0:64, 7, 0:256], ACT.Copy)
                elif what == "Kpe":
                    i = sc.activation(K[64:96, gb, 0, 0:LAT], ps[64:96, 7, :], ACT.Copy)
                else:
                    pair = g // 2
                    if what == "Va" and pair >= 2:
                        sc.wait_ge(pv_done, l * TS + T_AT[("TP", pair - 2)] + 1)
                    t0, n = (0, 4) if what == "Va" else (4, 2)
                    dst = v_slots(pair, 0, t0, n)
                    i = sc.activation(dst, ps[:, 7, 0:n * P].rearrange("p (t a b) -> p t a b", t=n, a=2), ACT.Copy)
                i.then_inc(misc_hi, 1)

            def exponentials(l, u):
                g, i = u // 5, u % 5
                kind = HEADS[g][0]
                bk = 2 * (u % 2)
                sc.wait_ge(max_ready, l * UNITS + u + 1)
                if i == 0 and g >= 2:
                    sc.wait_ge(pT_ps, l * TS + last_t_of(g - 2) + 1)
                if i == 4:
                    if g >= 2:
                        sc.wait_ge(pT_ps, l * TS + T_AT[("TP", g // 2 - 1)] + 1)
                    src, dst = ps[:, bk, 0:P], probs_p[:, g % 2, :]
                elif kind == "na":
                    w = (NA_M[i][1] - NA_M[i][0] + 2) * P
                    src, dst = ps[:, bk, 0:w], probs[:, g % 2, i, 0:w]
                else:
                    src = ps[:, bk:bk + 2, 0:HALF]
                    dst = probs[:, g % 2, i, :].rearrange("p (a b) -> p a b", a=2)
                sc.activation(dst, src, ACT.Exp, bias=negmax[:, u:u + 1], accum_out=rsum[:, u:u + 1]).then_inc(exp_done, 1)

            sc.wait_ge(const_in, 16 * 7)

            def sum_product(l, n, q):
                t = (POOL_ADA1 + POOL_ADA2)[n]
                v = ada_wp[:, n % POOL_RING] if q else product[:]
                sc.wait_ge(product_ready, l * PSUMS + 2 * n + q + 1)
                sc.activation(v, v, ACT.Copy, accum_out=mod[:, t, q:q + 1]).then_inc(product_summed, 1)

            with sc.Fori(0, DEPTH) as l:
                sc.wait_ge(cond_in, 16 * l + 16)
                sc.activation(silu_c[:], silu_c[:], ACT.Silu).then_inc(silu_done, 1)
                for k in range(KD):
                    sc.wait_ge(x_done, l * XD + 1)
                    if k >= 2:
                        sc.wait_ge(ss_done, l * 2 * KD + k - 1)
                    sc.activation(sq[:, k % 2], x[:, k], ACT.Square).then_inc(sq_ready, 1)
                for n in range(2):
                    sum_product(l, n, 0)
                    sum_product(l, n, 1)
                rms(l * 2 + 1)

                def wi_split(c):
                    sc.wait_ge(wi_in[c % 2], 16 * (l * (IC // 2) + c // 2 + 1))
                    if c >= 2:
                        sc.wait_ge(z_ps, l * IC * NT + (c - 1) * NT)
                    sc.activation(wi[:, c % 2, 0], wi_raw[:, c % 2], ACT.Copy).then_inc(wi_hi, 1)
                wi_split(0)
                for n in range(2, len(POOL_ADA1)):
                    sum_product(l, n, 0)
                    sum_product(l, n, 1)
                wi_split(1)
                modulated(l, 0)
                for c in range(IC):
                    for t in range(NT):
                        n = c * NT + t
                        sc.wait_ge(z_ps, l * IC * NT + n + 1)
                        sc.activation(z[:, t, c * ICW:(c + 1) * ICW], ps[:, n % 6, 0:ICW], ACT.Copy).then_inc(z_done, 1)
                        if c >= 1 and t < 2 * POOL_GROUP:
                            sum_product(l, len(POOL_ADA1) + POOL_GROUP * (c - 1) + t // 2, t % 2)
                    if c + 2 < IC:
                        wi_split(c + 2)
                    if c == 3:
                        sc.wait_ge(wq_in, 16 * l + 16)
                        sc.activation(wq[:, :, 0, :], wq_raw[:], ACT.Copy).then_inc(wqk_hi, 1)
                    if c == 5:
                        sc.wait_ge(z_done, l * IC * NT + 2 * NT)
                        for t in range(NT):
                            sc.activation(rstd[:, 0:256], z[:, t, 0:256], ACT.Square, accum_out=stat[:, t, 0:1]).then_inc(act_own, 1)
                            sc.wait_ge(act_own, l * 2 * NT + 2 * t + 1)
                            i = sc.activation(rstd[:, 0:P], z[:, t, OFF_CKV:OFF_KR], ACT.Square, accum_out=stat[:, t, 1:2])
                            i.then_inc(act_own, 1)
                            sc.wait_ge(act_own, l * 2 * NT + 2 * t + 2)
                        sc.wait_ge(cstat_ms, 2 * l + 1)
                        sc.activation(stat[:, :, 0:2], stat[:, :, 0:2], ACT.Sqrt).then_inc(cstat_rms, 1)
                sc.wait_ge(z_done, l * IC * NT + IC * NT)
                sc.wait_ge(small_in, (l + 1) * 160)
                cached_keys(l, 0)
                misc_hi_part(l, "Ka", 0)
                for e in range(4):
                    sc.wait_ge(cT_ps, l * 4 + e + 1)
                    settled(sc, passed_sc)
                    if e == 2:
                        misc_hi_part(l, "Qa", 0)
                    if e < 2:
                        sc.activation(cqT[:, e, 0, 0:LAT], ps[:, e, :], ACT.Copy, scale=qn_g[:, l, e:e + 1]).then_inc(cT_hi, 1)
                    elif e == 2:
                        sc.activation(ckvT[:, 0, 0:LAT], ps[:, e, :], ACT.Copy).then_inc(cT_hi, 1)
                    else:
                        for q in range(2):
                            sc.activation(cqT[:, q, 0, LAT:T], ps[:, 3, q * P:(q + 1) * P], ACT.Copy, scale=qn_g[:, l, q:q + 1])
                        sc.activation(ckvT[:, 0, 640:KEYS], ps[:, 3, 2 * P:3 * P], ACT.Copy).then_inc(cT_hi, 1)
                misc_hi_part(l, "Qb", 0)
                for n in range(2 * NT):
                    t, j = n // 2, n % 2
                    sc.wait_ge(qm_ps, l * 2 * NT + n + 1)
                    sc.activation(qm[:, t, j * 288:(j + 1) * 288], ps[:, 4 + n % 3, 0:288], ACT.Copy).then_inc(qm_done, 1)
                sc.wait_ge(qm_ps, l * 2 * NT + 2 * NT)
                sc.wait_ge(wq_ready, l + 1)
                sc.wait_ge(vz_done, l + 1)
                for s in SCHED:
                    if s[0] == "S":
                        for u in in_flight(S_AT[s], 1):
                            exponentials(l, u)
                    elif s[0] in ("T", "TP"):
                        n = T_AT[s]
                        if s[0] == "TP":
                            c0, c1 = 0, 2 * P
                        else:
                            a0, a1 = na_range(s[2]) if HEADS[s[1]][0] == "na" else (0, 3)
                            c0, c1 = a0 * P, (a1 + 1) * P
                        sc.wait_ge(pT_ps, l * TS + n + 1)
                        if n >= 2:
                            sc.wait_ge(pv_done, l * TS + n - 1)
                        sc.activation(pT[:, n % 2, 0, c0:c1], ps[:, 4 + n % 2, c0:c1], ACT.Copy).then_inc(pT_hi, 1)
                    elif s[0] == "OUT":
                        pair = s[1]
                        o = PAIR_TILE[pair]
                        sc.wait_ge(pv_done, l * TS + T_AT[("TP", pair)] + 1)
                        sc.activation(hT[:, o, 0, 0:LAT], ps[:, 6, :], ACT.Copy)
                        sc.activation(hT[:, o, 0, LAT:T], ps[:, 7, 0:P], ACT.Copy).then_inc(o_hi, 1)
                    elif s[0] == "C":
                        cached_keys(l, s[1])
                    elif s[0] == "M":
                        misc_hi_part(l, *s[1:])
                    elif s[0] == "WK":
                        sc.wait_ge(wkv_in, 16 * l + 16)
                        settled(sc, passed_sc)
                        sc.activation(wkv[:, 0], wkv_raw[:], ACT.Copy).then_inc(wqk_hi, 1)
                        sc.activation(ckvT[:, 0, LAT:640], kc_mla[:], ACT.Copy).then_inc(wqk_hi, 1)
                    elif s[0] == "GS":
                        t = s[1]
                        if t:
                            sc.wait_ge(gstat, l * NT + t)
                        sc.activation(ztmp[:], z[:, t, OFF_G:G_V], ACT.Square).then_inc(gsq, 1)
                    elif s[0] == "GR":
                        sc.wait_ge(cstat_ms, 2 * l + 2)
                        sc.activation(stat[:, :, 2:10], stat[:, :, 2:10], ACT.Sqrt).then_inc(cstat_rms, 1)
                    elif s[0] == "V":
                        g = s[1]
                        pair = g // 2
                        if pair >= 2:
                            sc.wait_ge(pv_done, l * TS + T_AT[("TP", pair - 2)] + 1)
                        for dst, src, _ in v_sources(g, 0):
                            i = sc.activation(dst, src, ACT.Copy)
                        i.then_inc(v_hi, 1)
                for o in range(KD):
                    sc.wait_ge(wo_in[o % 2], 16 * (l * (KD // 2) + o // 2 + 1))
                    if o >= 2:
                        sc.wait_ge(y_ps, l * XD + o - 1)
                    sc.activation(wo[:, o % 2, 0], wo_raw[:, o % 2], ACT.Copy).then_inc(wo_hi, 1)
                def gw_split(b):
                    sc.wait_ge(gw_in, 32 * (l * FB + b) + 32)
                    for w in range(2):
                        sc.activation(gw[:, w, 0], gw_raw[:, w], ACT.Copy).then_inc(gw_hi, 1)
                gw_split(0)
                for k in range(KD):
                    sc.wait_ge(x_done, l * XD + 1 + KD)
                    if k >= 2:
                        sc.wait_ge(ss_done, l * 2 * KD + KD + k - 1)
                    sc.activation(sq[:, k % 2], x[:, k], ACT.Square).then_inc(sq_ready, 1)
                rms(l * 2 + 2)
                modulated(l, 1)

                def ffn_block(b, last):
                    base = (l * FB + b) * 4
                    sc.wait_ge(dw_in, 16 * (l * FB + b) + 16)
                    sc.wait_ge(y_ps, l * XD + KD + b * KD)
                    sc.activation(dw[:, 0], dw_raw[:], ACT.Copy).then_inc(dw_hi, 1)
                    for j in range(2):
                        for hf_ in range(2):
                            sc.wait_ge(gu_ps, base * 2 + 4 * j + hf_ + 1)
                            sc.activation(sl[:, hf_], ps[:, 4 * j + hf_, 0:HALF], ACT.Silu).then_inc(sl_ready, 1)
                        for hf_ in range(2):
                            sc.wait_ge(mm_ready, base + 2 * j + hf_ + 1)
                            sc.activation(act[:, j, 0, hf_ * HALF:(hf_ + 1) * HALF], mm[:, hf_], ACT.Copy).then_inc(act_hi, 1)
                    if not last:
                        sc.wait_ge(gu_ps, base * 2 + 8)
                        gw_split(b + 1)

                with sc.Fori(0, FB - 1) as b:
                    ffn_block(b, False)
                ffn_block(FB - 1, True)
            sc.wait_ge(x_done, DEPTH * XD + 1)
            for k in range(KD):
                if k >= 2:
                    sc.wait_ge(ss_done, DEPTH * 2 * KD + k - 1)
                sc.activation(sq[:, k % 2], x[:, k], ACT.Square).then_inc(sq_ready, 1)
            rms(DEPTH * 2 + 1)

        @block.vector
        def _(ve):
            def f(t):
                return t.bitcast(F32)

            def lo(dst, src, hi):
                return ve.tensor_tensor(dst, src, f(hi), ALU.subtract)

            def ada(l, t):
                w, arrived, count = dve_slot(t)
                ve.wait_ge(arrived, count(l))
                junk = ps[:, 6:8, :].rearrange("p a b -> p (a b)")
                for q in range(2):
                    own = 2 * (l * NDVE + (DVE_ADA1 + DVE_ADA2).index(t)) + q
                    if q or t:
                        ve.wait_ge(dots, own)
                    i = ve.scalar_tensor_tensor(out=junk, in0=w, scalar=1.0, in1=silu_c[:, q], op0=ALU.mult,
                                                op1=ALU.mult, accum_out=mod[:, t, q:q + 1])
                    i.then_inc(dots, 1)

            def ada_bias(l, t0, t1, summed):
                ve.wait_ge(product_summed, l * PSUMS + summed)
                ve.wait_ge(dots, 2 * (l * NDVE + len([t for t in DVE_ADA1 + DVE_ADA2 if t < t1])))
                ve.tensor_tensor(mod[:, t0:t1, :], mod[:, t0:t1, :],
                                 b_ada[:, l, t0:t1].unsqueeze(2).broadcast_to([P, t1 - t0, 2]), ALU.add).then_inc(ada_done, 1)

            def coefs(l, nrm):
                t0 = 24 * nrm + 8
                ve.wait_ge(ada_done, 2 * l + nrm + 1)
                ve.scalar_tensor_tensor(out=coef[:, nrm], in0=mod[:, t0:t0 + KD, :], scalar=1.0,
                                        in1=norm_g[:, l, nrm, :].unsqueeze(2).broadcast_to([P, KD, 2]),
                                        op0=ALU.add, op1=ALU.mult).then_inc(coef_done, 1)

            def mean_square(n, ss):
                ve.wait_ge(ss_done, ss)
                ve.tensor_scalar(rstd[:].rearrange("p (a b) -> p a b", a=2), ps[:, 0:2, 0:HALF], 1.0 / DM, EPS,
                                 ALU.mult, ALU.add).then_inc(ms_ready, 1)
                ve.wait_ge(rms_ready, n)
                ve.reciprocal(rstd[:], rstd[:]).then_inc(rstd_ready, 1)

            def modulated(l, nrm):
                base = l * 2 * KD + nrm * KD
                for k in range(KD):
                    ve.wait_ge(tn_ready, base + k + 1)
                    if k == 0:
                        ve.wait_ge(coef_done, 2 * l + nrm + 1)
                    else:
                        ve.wait_ge(h_ready, base + k)
                    for q, (c0, c1) in enumerate(((0, LAT), (LAT, T))):
                        i = ve.tensor_scalar(hf[:, c0:c1], tn[:, k % 2, c0:c1], coef[:, nrm, k, q:q + 1],
                                             mod[:, 24 * nrm + k, q:q + 1], ALU.mult, ALU.add)
                    i.then_inc(hf_ready, 1)
                    ve.wait_ge(hf_ready, base + k + 1)
                    ve.wait_ge(h_hi, base + k + 1)
                    lo(hT[:, k, 1], hf[:], hT[:, k, 0]).then_inc(h_ready, 1)

            def residual(l, y, o, banks, part):
                ve.wait_ge(y_ps, y)
                for hf_, c0, c1, q in ((0, 0, HALF, 0), (1, HALF, LAT, 0), (1, LAT, T, 1)):
                    s0 = c0 - hf_ * HALF
                    i = ve.scalar_tensor_tensor(out=x[:, o, c0:c1], in0=ps[:, banks + hf_, s0:s0 + c1 - c0],
                                                scalar=mod[:, part * KD + o, q:q + 1], in1=x[:, o, c0:c1],
                                                op0=ALU.mult, op1=ALU.add)
                i.then_inc(x_done, 1)

            def cached_keys(l, g):
                kind, h = HEADS[g]
                gb = g % 2
                if kind == "na":
                    n, src, r = g, kc_na[0:64, h, :], slice(0, 64)
                elif kind == "gqa":
                    n, src, r = g - 4, kc_g[0:64, h // 3, :], slice(0, 64)
                elif h < 2:
                    n, src, r = g, kc_pe[64:96, :], slice(64, 96)
                else:
                    return
                ve.wait_ge(kc_hi, l * (NH - 4) + n + 1)
                if kind != "mla" and h < 2:
                    ve.memset(K[64:P, gb, 1, :].bitcast(F32), 0.0)
                lo(K[r, gb, 1, LAT:640], src, K[r, gb, 0, LAT:640])

            def misc_lo_part(l, what, g):
                kind, h = HEADS[g]
                gb = g % 2
                ve.wait_ge(misc_hi, l * NM + MISC_AT[(what, g)] + 1)
                if what in ("Qa", "Qb"):
                    c0, c1 = (0, LAT) if what == "Qa" else (LAT, T)
                    if kind == "mla":
                        r, dst, scale = slice(0, 96), Q[0:96, gb, 1, c0:c1], MLA_SCALE
                    else:
                        r, dst, scale = slice(0, 64), Q[64:P, gb, 0, c0:c1], HD_SCALE
                    i = ve.scalar_tensor_tensor(out=dst, in0=ps[r, 7, 0:c1 - c0], scalar=scale,
                                                in1=f(Q[r, gb, 0, c0:c1]), op0=ALU.mult, op1=ALU.subtract)
                    if what == "Qb" and kind == "mla" and h < 2:
                        i = lo(K[64:96, gb, 1, 640:KEYS], ps[64:96, 7, P:2 * P], K[64:96, gb, 0, 640:KEYS])
                    if what == "Qb" and kind != "mla":
                        i = lo(K[0:64, gb, 1, 640:KEYS], ps[0:64, 7, P:2 * P], K[0:64, gb, 0, 640:KEYS])
                elif what == "Ka":
                    r = slice(0, 64)
                    i = lo(K[r, gb, 1, 0:LAT], ps[r, 7, :], K[r, gb, 0, 0:LAT])
                elif what == "Kb":
                    i = lo(K[0:64, gb, 1, LAT:KEYS], ps[0:64, 7, 0:256], K[0:64, gb, 0, LAT:KEYS])
                elif what == "Kpe":
                    i = lo(K[64:96, gb, 1, 0:LAT], ps[64:96, 7, :], K[64:96, gb, 0, 0:LAT])
                else:
                    pair = g // 2
                    t0, n = (0, 4) if what == "Va" else (4, 2)
                    src = ps[:, 7, 0:n * P].rearrange("p (t a b) -> p t a b", t=n, a=2)
                    i = lo(v_slots(pair, 1, t0, n), src, v_slots(pair, 0, t0, n))
                i.then_inc(misc_done, 1)

            ve.wait_ge(const_in, 16 * 7)
            ve.wait_ge(x_in, 16 * KD)
            ve.sem_inc(x_done, 1)
            ve.sem_inc(act_ready, 1)
            with ve.Fori(0, DEPTH) as l:
                ve.wait_ge(silu_done, l + 1)
                for t in DVE_ADA1[:6]:
                    ada(l, t)
                mean_square(2 * l + 1, l * 2 * KD + KD)
                for t in DVE_ADA1[6:]:
                    ada(l, t)
                ada_bias(l, 0, ADA1, 2 * len(POOL_ADA1))
                coefs(l, 0)

                def wi_split(c):
                    ve.wait_ge(wi_hi, l * IC + c + 1)
                    lo(wi[:, c % 2, 1], wi_raw[:, c % 2], wi[:, c % 2, 0]).then_inc(wi_ready, 1)
                wi_split(0)
                wi_split(1)
                modulated(l, 0)
                for c in range(2, IC):
                    wi_split(c)
                    if c == IC - 1:
                        ve.wait_ge(act_own, (l + 1) * 2 * NT)
                        ve.tensor_scalar(stat[:, :, 0:1], stat[:, :, 0:1], 1.0 / 256, EPS, ALU.mult, ALU.add)
                        ve.tensor_scalar(stat[:, :, 1:2], stat[:, :, 1:2], 1.0 / P, EPS, ALU.mult, ALU.add).then_inc(cstat_ms, 1)
                    for t in DVE_ADA2[DVE_GROUP * (c - 2):DVE_GROUP * (c - 1)]:
                        ada(l, t)
                    if c == 5:
                        ve.wait_ge(wqk_hi, 3 * l + 1)
                        lo(wq[:, :, 1, :], wq_raw[:], wq[:, :, 0, :]).then_inc(wq_ready, 1)
                ve.wait_ge(cstat_rms, 2 * l + 1)
                ve.reciprocal(stat[:, :, 0:2], stat[:, :, 0:2]).then_inc(cstat, 1)
                ve.wait_ge(cstat, 2 * l + 1)
                ve.wait_ge(small_in, (l + 1) * 160)
                for t in range(NT):
                    ve.tensor_scalar(z[:, t, 0:256], z[:, t, 0:256], stat[:, t, 0:1], None, ALU.mult)
                    ve.scalar_tensor_tensor(out=z[:, t, OFF_CKV:OFF_KR], in0=z[:, t, OFF_CKV:OFF_KR],
                                            scalar=stat[:, t, 1:2], in1=kv_g[:], op0=ALU.mult, op1=ALU.mult).then_inc(c_norm, 1)
                ada_bias(l, ADA1, NADA, PSUMS)
                coefs(l, 1)
                cached_keys(l, 0)
                misc_lo_part(l, "Ka", 0)
                for e in range(4):
                    if e == 2:
                        misc_lo_part(l, "Qa", 0)
                    ve.wait_ge(cT_hi, l * 4 + e + 1)
                    if e < 2:
                        ve.scalar_tensor_tensor(out=cqT[:, e, 1, 0:LAT], in0=ps[:, e, :], scalar=qn_g[:, l, e:e + 1],
                                                in1=f(cqT[:, e, 0, 0:LAT]), op0=ALU.mult, op1=ALU.subtract).then_inc(cT_ready, 1)
                    elif e == 2:
                        lo(ckvT[:, 1, 0:LAT], ps[:, e, :], ckvT[:, 0, 0:LAT]).then_inc(cT_ready, 1)
                    else:
                        for q in range(2):
                            ve.scalar_tensor_tensor(out=cqT[:, q, 1, LAT:T], in0=ps[:, 3, q * P:(q + 1) * P],
                                                    scalar=qn_g[:, l, q:q + 1], in1=f(cqT[:, q, 0, LAT:T]),
                                                    op0=ALU.mult, op1=ALU.subtract)
                        lo(ckvT[:, 1, 640:KEYS], ps[:, 3, 2 * P:3 * P], ckvT[:, 0, 640:KEYS]).then_inc(cT_ready, 1)
                misc_lo_part(l, "Qb", 0)
                ve.wait_ge(qm_ps, l * 2 * NT + 2 * NT)
                ve.wait_ge(vz_done, l + 1)
                for s in SCHED:
                    if s[0] == "S":
                        _, g, i = s
                        kind = HEADS[g][0]
                        u = S_AT[s]
                        bk = 2 * (u % 2)
                        ve.wait_ge(s_ready, l * UNITS + u + 1)
                        if i == 4:
                            src = ps[:, bk, 0:P]
                        elif kind == "na":
                            w = (NA_M[i][1] - NA_M[i][0] + 1) * P
                            if i == 0:
                                ve.wait_ge(bias_ready, l * 4 + g + 1)
                            ve.tensor_tensor(ps[:, bk, 0:w], ps[:, bk, 0:w], bias_h[:, g % 2, NA_OFF[i]:NA_OFF[i] + w],
                                             ALU.add).then_inc(biased, 1)
                            ve.wait_ge(biased, l * 16 + 4 * g + i + 1)
                            src = ps[:, bk, 0:w + P]
                        else:
                            src = ps[:, bk:bk + 2, 0:HALF]
                        ve.tensor_reduce(negmax[:, u:u + 1], src, AX.XY if len(src.shape) == 3 else AX.X, ALU.max,
                                         negate=True).then_inc(max_ready, 1)
                        reciprocals(ve, l, u)
                    elif s[0] in ("T", "TP"):
                        n = T_AT[s]
                        if s[0] == "TP":
                            c0, c1 = 0, 2 * P
                        else:
                            a0, a1 = na_range(s[2]) if HEADS[s[1]][0] == "na" else (0, 3)
                            c0, c1 = a0 * P, (a1 + 1) * P
                        ve.wait_ge(pT_hi, l * TS + n + 1)
                        lo(pT[:, n % 2, 1, c0:c1], ps[:, 4 + n % 2, c0:c1], pT[:, n % 2, 0, c0:c1]).then_inc(pT_ready, 1)
                    elif s[0] == "OUT":
                        pair = s[1]
                        o = PAIR_TILE[pair]
                        ve.wait_ge(o_hi, l * NP + pair + 1)
                        lo(hT[:, o, 1, 0:LAT], ps[:, 6, :], hT[:, o, 0, 0:LAT])
                        lo(hT[:, o, 1, LAT:T], ps[:, 7, 0:P], hT[:, o, 0, LAT:T]).then_inc(o_ready, 1)
                    elif s[0] == "C":
                        cached_keys(l, s[1])
                    elif s[0] == "M":
                        misc_lo_part(l, *s[1:])
                    elif s[0] == "WK":
                        ve.wait_ge(wqk_hi, 3 * l + 3)
                        lo(wkv[:, 1], wkv_raw[:], wkv[:, 0])
                        lo(ckvT[:, 1, LAT:640], kc_mla[:], ckvT[:, 0, LAT:640]).then_inc(wkv_ready, 1)
                    elif s[0] == "GS":
                        t = s[1]
                        ve.wait_ge(gsq, l * NT + t + 1)
                        ve.tensor_reduce(stat[:, t, 2:10], ztmp[:].rearrange("p (h d) -> p h d", h=8), AX.X, ALU.add).then_inc(gstat, 1)
                    elif s[0] == "GR":
                        ve.wait_ge(gstat, l * NT + NT)
                        ve.tensor_scalar(stat[:, :, 2:10], stat[:, :, 2:10], 1.0 / 64, EPS, ALU.mult, ALU.add).then_inc(cstat_ms, 1)
                    elif s[0] == "V":
                        g = s[1]
                        ve.wait_ge(v_hi, l * NV + v_at(g // 2) + 1)
                        for dst, src, hi in v_sources(g, 1):
                            i = lo(dst, src, hi)
                        i.then_inc(v_ready, 1)
                    elif s[0] == "GZ":
                        t = s[1]
                        zg = z[:, t, OFF_G:G_V].rearrange("p (h d) -> p h d", h=8)
                        if t == 0:
                            ve.wait_ge(cstat_rms, 2 * l + 2)
                            ve.reciprocal(stat[:, :, 2:10], stat[:, :, 2:10]).then_inc(cstat, 1)
                            ve.wait_ge(cstat, 2 * l + 2)
                        ve.tensor_tensor(zg, zg, stat[:, t, 2:10].unsqueeze(2).broadcast_to([P, 8, 64]), ALU.mult).then_inc(dve_own, 1)
                        ve.wait_ge(dve_own, l * NT + t + 1)
                        ve.tensor_tensor(z[:, t, OFF_G:G_V], z[:, t, OFF_G:G_V], g8[:], ALU.mult).then_inc(g_norm, 1)
                for o in range(KD):
                    ve.wait_ge(wo_hi, l * KD + o + 1)
                    lo(wo[:, o % 2, 1], wo_raw[:, o % 2], wo[:, o % 2, 0]).then_inc(wo_ready, 1)
                    if o >= 1:
                        residual(l, l * XD + o, o - 1, 2 + 2 * ((o - 1) % 3), 2)
                residual(l, l * XD + KD, KD - 1, 2 + 2 * ((KD - 1) % 3), 2)

                def gw_split(b):
                    for w in range(2):
                        ve.wait_ge(gw_hi, 2 * (l * FB + b) + w + 1)
                        i = lo(gw[:, w, 1], gw_raw[:, w], gw[:, w, 0])
                    i.then_inc(gw_ready, 1)
                gw_split(0)
                mean_square(2 * l + 2, l * 2 * KD + 2 * KD)
                modulated(l, 1)

                def ffn_block(b, last):
                    base = (l * FB + b) * 4
                    ve.wait_ge(dw_hi, l * FB + b + 1)
                    lo(dw[:, 1], dw_raw[:], dw[:, 0]).then_inc(dw_ready, 1)

                    def gated(j, hf_):
                        ve.wait_ge(sl_ready, base + 2 * j + hf_ + 1)
                        ve.wait_ge(gu_ps, base * 2 + 4 * j + 2 + hf_ + 1)
                        ve.wait_ge(act_ready, base + (hf_ + 1 if j else 0) + 1)
                        ve.tensor_tensor(mm[:, hf_], sl[:, hf_], ps[:, 4 * j + 2 + hf_, 0:HALF], ALU.mult).then_inc(mm_ready, 1)

                    def act_lo(j, hf_):
                        ve.wait_ge(act_hi, base + 2 * j + hf_ + 1)
                        cols = slice(hf_ * HALF, (hf_ + 1) * HALF)
                        lo(act[:, j, 1, cols], mm[:, hf_], act[:, j, 0, cols]).then_inc(act_ready, 1)
                    for j in range(2):
                        gated(j, 0)
                        gated(j, 1)
                        act_lo(j, 0)
                        act_lo(j, 1)
                    if not last:
                        gw_split(b + 1)
                    for o in range(KD):
                        residual(l, l * XD + KD + b * KD + o + 1, o, 2 * (o % 4), 5)

                with ve.Fori(0, FB - 1) as b:
                    ffn_block(b, False)
                ffn_block(FB - 1, True)
            mean_square(DEPTH * 2 + 1, DEPTH * 2 * KD + KD)
            ve.wait_ge(rstd_ready, DEPTH * 2 + 1)
            for k in range(KD):
                ve.scalar_tensor_tensor(out=x[:, k], in0=x[:, k], scalar=fin_g[:, k:k + 1], in1=rstd[:],
                                        op0=ALU.mult, op1=ALU.mult).then_inc(y_ready, 1)

        @block.gpsimd
        def _(po):
            def rotate(own, n, d, view, cos, sin, tmp):
                w = d // 4
                halves = view.rearrange("p h (a b w) -> p h a b w", a=2, b=2)
                s4 = sin.rearrange("p (a b w) -> p a b w", a=2, b=2)
                t4 = tmp.rearrange("p h (a b w) -> p h a b w", a=2, b=2)
                for b in range(2):
                    po.tensor_tensor(t4[:, :, :, b, :], halves[:, :, :, 1 - b, :],
                                     s4[:, :, b, :].unsqueeze(1).broadcast_to([P, n, 2, w]), ALU.mult).then_inc(pool_own, 1)
                po.wait_ge(pool_own, own + 2)
                po.tensor_tensor(view, view, cos.unsqueeze(1).broadcast_to([P, n, d]), ALU.mult).then_inc(pool_own, 1)
                po.wait_ge(pool_own, own + 3)
                return po.tensor_tensor(view, view, tmp, ALU.add)

            OWN = 3 * 12

            po.memset(ones[:], 1.0).then_inc(ones_set, 1)

            def modulated(base, n):
                po.wait_ge(rstd_ready, n)
                for k in range(KD):
                    if k >= 2:
                        po.wait_ge(h_ready, base + k - 1)
                    po.tensor_tensor(tn[:, k % 2], x[:, k], rstd[:], ALU.mult).then_inc(tn_ready, 1)

            def window(l, h):
                v = a["rpb"][l, h, :]
                src = bass.AP(tensor=v.tensor, offset=v.offset, ap=[[15, 16], [1, 8], [1, WIN]])
                po.dma_start(win[:, 0:WIN], src).then_inc(win_in, 16)

            def ada(l, t):
                w, arrived, count, n = pool_slot(t)
                po.wait_ge(arrived, count(l))
                if n:
                    po.wait_ge(product_summed, l * PSUMS + 2 * n - 1)
                settled(po, passed_po)
                po.tensor_tensor(product[:], w, silu_c[:, 0], ALU.mult).then_inc(product_ready, 1)
                po.wait_ge(product_ready, l * PSUMS + 2 * n + 1)
                po.tensor_tensor(w, w, silu_c[:, 1], ALU.mult).then_inc(product_ready, 1)

            with po.Fori(0, DEPTH) as l:
                po.wait_ge(silu_done, l + 1)
                for t in POOL_ADA1:
                    ada(l, t)
                modulated(l * 2 * KD, 2 * l + 1)
                for t in POOL_ADA2:
                    ada(l, t)
                po.wait_ge(z_done, l * IC * NT + IC * NT)
                window(l, 0)
                po.wait_ge(wi_ready, l * IC + IC)
                settled(po, passed_po)
                zeros = V[:, 0, 0, 0, 64:P].bitcast(F32)
                po.memset(bass.AP(tensor=zeros.tensor, offset=zeros.offset, ap=[list(zeros.ap[0]), [192, 24], [1, 64]]),
                          0.0).then_inc(vz_done, 1)
                turned = 0
                for s in SCHED:
                    if s[0] == "BM":
                        h = s[1]
                        po.wait_ge(win_in, 16 * (4 * l + h + 1))
                        if h >= 2:
                            po.wait_ge(max_ready, l * UNITS + 5 * (h - 1))
                        for n in range(4):
                            m0, m1 = NA_M[n]
                            cols = (m1 - m0 + 1) * 16
                            kc0 = 16 * (m0 - n) + 16
                            w = win[:]
                            src = bass.AP(tensor=w.tensor, offset=w.offset + WIN - 1 - 15 * kc0,
                                          ap=[list(w.ap[0]), [-15, cols], [-1, ROWS]])
                            c0 = NA_OFF[n]
                            i = po.tensor_tensor(bias_h[:, h % 2, c0:c0 + cols * ROWS].rearrange("p (c r) -> p c r", r=ROWS), src,
                                                 mask[:, c0 // ROWS:c0 // ROWS + cols].unsqueeze(2).broadcast_to([P, cols, ROWS]),
                                                 ALU.add)
                        i.then_inc(bias_ready, 1)
                        if h + 1 < 4:
                            po.wait_ge(bias_ready, l * 4 + h + 1)
                            window(l, h + 1)
                    elif s[0] in ("KR", "QR"):
                        t = s[1]
                        if t == 0 and s[0] == "KR":
                            po.wait_ge(kv_out, l * 64 + 64)
                        if t == 0 and s[0] == "QR":
                            po.wait_ge(qm_done, l * 2 * NT + 2 * NT)
                        if turned:
                            po.wait_ge(q_roped, l * 8 + turned)
                        if s[0] == "KR":
                            n, view = 1, z[:, t, OFF_KR:OFF_NA].unsqueeze(1)
                        else:
                            n, view = 6, qm[:, t, :].rearrange("p (h d) -> p h d", h=6)[:, :, 64:96]
                        tmp = rstd[:, 0:32 * n].rearrange("p (h d) -> p h d", h=n)
                        rotate(l * OWN + 3 * turned, n, 32, view, rope[:, t, 0, 64:96], rope[:, t, 1, 64:96],
                               tmp).then_inc(q_roped, 1)
                        turned += 1
                    elif s[0] == "S":
                        for u in in_flight(S_AT[s], 2):
                            norm_unit(po, l, u, (0, 1, 2, 4))
                    elif s[0] == "GZ" and s[1] < 4:
                        t = s[1]
                        po.wait_ge(g_norm, l * NT + t + 1)
                        view = z[:, t, OFF_G:G_V].rearrange("p (h d) -> p h d", h=8)
                        tmp = ztmp[:].rearrange("p (h d) -> p h d", h=8)
                        if t:
                            po.wait_ge(g_roped, l * 4 + t)
                        rotate(l * OWN + 24 + 3 * t, 8, 64, view, rope[:, t, 0, 0:64], rope[:, t, 1, 0:64], tmp).then_inc(g_roped, 1)
                        po.wait_ge(g_roped, l * 4 + t + 1)
                po.wait_ge(coef_done, 2 * l + 2)
                modulated(l * 2 * KD + KD, 2 * l + 2)



def constants():
    import numpy as np
    t = np.arange(LAT)
    col, row = (t // ROWS).astype(np.float32), (t % ROWS).astype(np.float32)

    def table(d):
        ax = d // 2
        inv = np.float32(10000.0) ** (-np.arange(0, ax, 2, dtype=np.float32) / np.float32(ax))
        ar, ac = row[:, None] * inv, col[:, None] * inv
        ang = np.concatenate([ar, ar, ac, ac], axis=-1).astype(np.float32)
        sign = np.repeat(np.array([-1, 1, -1, 1], np.float32), d // 4)
        return np.cos(ang), np.sin(ang) * sign
    (cg, sg), (cm, sm) = table(64), table(32)
    rope = np.stack([np.concatenate([cg, cm], 1), np.concatenate([sg, sm], 1)], 1).reshape(4, P, 2, 96)
    rope = np.ascontiguousarray(rope.transpose(1, 0, 2, 3)).astype(np.float32)
    parts = []
    for n in range(4):
        m0, m1 = NA_M[n]
        q = 16 * n + np.arange(P) // ROWS
        k = np.arange(16 * m0, 16 * (m1 + 1))
        start = np.clip(q - 8, 0, GRID_W - 16)[:, None]
        parts.append(np.where((k >= start) & (k < start + 16), 0.0, -1e30))
    mask = np.concatenate(parts, 1).astype(np.float32)
    return rope, mask, np.eye(P, dtype=np.float32)


def kernel(**inputs):
    import numpy as np
    import concourse.bacc as bacc
    from concourse.bass_utils import run_bass_kernel_spmd as run

    g = {k: np.asarray(v) for k, v in inputs.items()}
    tile = lambda v, *lead: np.ascontiguousarray(v)
    rope, mask, ident = constants()
    xs = g["x_sample"][0].reshape(ROWS, GRID_W, DM).transpose(1, 0, 2).reshape(LAT, DM)
    rpb = np.pad(g["na_rpb"].transpose(0, 1, 3, 2), ((0, 0), (0, 0), (16, 16), (0, 0)))
    rpb = rpb.reshape(DEPTH, 4, 63 * 15)[:, :, ::-1]
    feat = lambda v: v.reshape(*v.shape[:-1], -1, P)
    arrays = {
        "x": np.concatenate([xs, g["x_prompt"][0]], 0).T,
        "cond": np.stack([g["c"][0], g["c_ctx"]]),
        "b_ada": feat(g["b_ada"]).transpose(2, 0, 1),
        "norm_g": np.stack([feat(g["norm_mix_g"]), feat(g["norm_ffn_g"])], 1).transpose(3, 0, 1, 2),
        "fin_g": feat(g["final_norm_g"]).T,
        "qn_g": feat(g["mla_q_norm_g"]).transpose(2, 0, 1),
        "kv_g": g["mla_kv_norm_g"],
        "g8": np.concatenate([np.tile(g["gqa_q_norm_g"], (1, 6)), np.tile(g["gqa_k_norm_g"], (1, 2))], 1),
        "rope": rope, "mask": mask, "ident": ident,
        "ckvT": g["cache_mla_ckv"][0].transpose(0, 2, 1),
        "krT": g["cache_mla_krope"][0].transpose(0, 2, 1),
        "na_kT": g["cache_na_k"][0].transpose(0, 3, 2, 1),
        "g_kT": g["cache_gqa_k"][0].transpose(0, 3, 2, 1),
        "na_v": g["cache_na_v"][0].reshape(DEPTH, P, 256),
        "g_v": g["cache_gqa_v"][0].reshape(DEPTH, P, P),
        "rpb": rpb,
        "w_adaT": g["w_ada"].transpose(0, 2, 1), "w_in": g["w_in"], "w_q_up": g["w_q_up"], "w_kv_up": g["w_kv_up"],
        "w_out": g["w_out"], "w_gate": g["w_gate"], "w_up": g["w_up"], "w_down": g["w_down"],
    }
    outs = {"o_y": (DM, T), "o_ckv": (DEPTH, P, P), "o_kr": (DEPTH, P, 32), "o_nak": (DEPTH, P, 256),
            "o_nav": (DEPTH, P, 256), "o_gk": (DEPTH, P, P), "o_gv": (DEPTH, P, P)}
    nc = bacc.Bacc("TRN2", target_bir_lowering=False, num_devices=1)
    arrays = {k: np.ascontiguousarray(v) for k, v in arrays.items()}
    a = {k: nc.dram_tensor("in_" + k, v.shape, F32, kind="ExternalInput").ap() for k, v in arrays.items()}
    o = {k: nc.dram_tensor("out_" + k, s, F32, kind="ExternalOutput").ap() for k, s in outs.items()}
    build(nc, a, o)
    r = run(nc, [{"in_" + k: v for k, v in arrays.items()}], core_ids=[0]).results[0]
    y = r["out_o_y"].T
    ys = y[:LAT].reshape(GRID_W, ROWS, DM).transpose(1, 0, 2).reshape(1, LAT, DM)
    return (np.ascontiguousarray(y[LAT:])[None], np.ascontiguousarray(ys),
            r["out_o_ckv"][None], r["out_o_kr"][None], r["out_o_nak"].reshape(1, DEPTH, P, 4, 64),
            r["out_o_nav"].reshape(1, DEPTH, P, 4, 64), r["out_o_gk"].reshape(1, DEPTH, P, 2, 64),
            r["out_o_gv"].reshape(1, DEPTH, P, 2, 64))
```

```python
from contextlib import ExitStack

import concourse.bass as bass
from concourse import mybir

F32 = mybir.dt.float32
F32R = mybir.dt.float32r
ALU = mybir.AluOpType
ACT = mybir.ActivationFunctionType
AX = mybir.AxisListType

P = 128
DM = 1024
KD = DM // P
LAT, CTX, T = 512, 128, 640
HALF = T // 2
NT = T // P
DEPTH = 2
EPS = 1e-6
GRID_W, ROWS = 64, 8

OFF_CKV, OFF_KR, OFF_NA = 256, 384, 416
NA_Q, NA_K, NA_V = OFF_NA, OFF_NA + 256, OFF_NA + 512
OFF_G = OFF_NA + 768
G_K = OFF_G + 384
G_V = OFF_G + 512
IN_COLS = G_V + 128
IC = 8
ICW = IN_COLS // IC
QW = 576
FB = 2816 // 256
NADA = 48
ADA1 = 16
POOL_ADA1 = [1, 4, 7, 9, 12, 15]
POOL_ADA2 = [t for t in range(ADA1, NADA) if (t - ADA1) % 16 % 2 and (t - ADA1) % 16 < 15]
DVE_ADA1 = [t for t in range(ADA1) if t not in POOL_ADA1]
DVE_ADA2 = [t for t in range(ADA1, NADA) if t not in POOL_ADA2]
DVE_RING1, DVE_RING2, POOL_RING = 7, 2, 2
PSUMS = 2 * (len(POOL_ADA1) + len(POOL_ADA2))
NDVE = NADA - PSUMS // 2
DVE_GROUP = 3
POOL_GROUP = 2
KEYS = 768
WIN = 713
MLA_SCALE = 96.0 ** -0.5
HD_SCALE = 0.125

HEADS = [("na", h) for h in range(4)] + [("mla", h) for h in range(6)] + [("gqa", h) for h in range(6)]
PAIR_TILE = [3, 4, 0, 1, 2, 5, 6, 7]
NH = len(HEADS)
NP = NH // 2
UNITS = 5 * NH
TS = 5 * NH + NP
NA_M = [(0, 1), (0, 2), (1, 3), (2, 3)]
NA_OFF = [0, 256, 640, 1024]
NA_COLS = 1280


def na_range(m):
    if m == 4:
        return 0, 3
    ns = [n for n in range(4) if NA_M[n][0] <= m <= NA_M[n][1]]
    return ns[0], ns[-1]


def normaliser(g):
    na = HEADS[g][0] == "na"
    return {"pool": (0, 4) if na else (0, 1, 4), "act": (1, 2) if na else (2,), "dve": (3,)}


def normalised(engine, g):
    return sum(len(normaliser(h)[engine]) for h in range(g))


def key_slot(g):
    kind, h = HEADS[g]
    return (h // 3, h % 3 == 0) if kind == "gqa" else (g % 2, True)


def prep_steps(g):
    kind, h = HEADS[g]
    if kind == "mla":
        s = [("Qa", g), ("Qb", g), ("Ka", g), ("Kb", g)]
        if h < 2:
            s.append(("Kpe", g))
        return s
    return [("Ka", g), ("Qa", g), ("Qb", g)] if key_slot(g)[1] else [("Qa", g), ("Qb", g)]


def schedule():
    def prep(g):
        steps = [("BM", g)] if g < NH and HEADS[g][0] == "na" else []
        if g < NH:
            steps += [("C", g)] + [("M",) + s for s in prep_steps(g)]
        if g >= 1 and g % 2 == 1:
            steps += [("M", "Va", g - 1), ("M", "Vb", g - 1)] if HEADS[g - 1][0] == "mla" else [("V", g - 1)]
        return steps

    slots = 5 * NH + 7
    extra = [[] for _ in range(2 * slots)]

    def spread(steps, first, count, leave=()):
        places = [i for i in range(2 * count) if i not in leave]
        for n, st in enumerate(steps):
            extra[2 * first + places[n * len(places) // len(steps)]].append(st)
    for g in range(NH):
        spread(prep(g + 1), 5 * g, 5, (2, 3) if g % 2 else (9,))
    spread([("KR", t) for t in range(4)] + [("QR", t) for t in range(4)], 0, 15)
    spread([("GS", t) for t in range(NT)] + [("GR",)], 8, 16)
    spread([("WK",)], 6, 1)
    spread([("GZ", t) for t in range(NT)], 25, 18)
    order = [("BM", 0)]
    trans = []
    for g in range(NH):
        trans += [("T", g, m) for m in range(5)]
    for n in range(slots):
        if n < 5 * NH:
            order.append(("S", n // 5, n % 5))
        k = n - 6
        prompt = k >= 10 and k % 10 == 0
        if prompt:
            order += [("TP", k // 10 - 1), ("OL", k // 10 - 1)]
        order += extra[2 * n]
        if 0 <= k < len(trans):
            order.append(trans[k])
        if prompt:
            order.append(("OP", k // 10 - 1))
        for i in (1, 2):
            g = (n - i - 3) // 5
            if n >= i + 3 and (n - i - 3) % 5 == 0 and g < NH and i in normaliser(g)["act"]:
                order.append(("N", g, i))
        order += extra[2 * n + 1]
    return order


SCHED = schedule()
HEAD0 = [("M",) + s for s in prep_steps(0)]
MISC = [s[1:] for s in HEAD0 + SCHED if s[0] == "M"]
MISC_AT = {s: n for n, s in enumerate(MISC)}
NM = len(MISC)
T_AT = {s: n for n, s in enumerate([s for s in SCHED if s[0] in ("T", "TP")])}
S_AT = {s: n for n, s in enumerate([s for s in SCHED if s[0] == "S"])}
NV = 5


def kind_of_pair(pair):
    return HEADS[2 * pair][0]


def v_at(pair):
    return pair if pair < 2 else pair - 3


def last_t_of(g):
    return T_AT[("T", g, 4)]


def build(nc, a, out):
    ctx = ExitStack()
    with ctx:
        def sem(name):
            return ctx.enter_context(nc.semaphore(name))

        def sb(name, shape, dt=F32, scope=ctx):
            return scope.enter_context(nc.sbuf_tensor(name, shape, dt))

        x = sb("x", [P, KD, T])
        ada_w = sb("ada_w", [P, DVE_RING2, DM])
        mod = sb("mod", [P, NADA, 2])
        coef = sb("coef", [P, 2, KD, 2])
        rstd = sb("rstd", [P, T])
        b_ada = sb("b_ada", [P, DEPTH, NADA])
        norm_g = sb("norm_g", [P, DEPTH, 2, KD])
        fin_g = sb("fin_g", [P, KD])
        qn_g = sb("qn_g", [P, DEPTH, 2])
        kv_g = sb("kv_g", [P, P])
        g8 = sb("g8", [P, 512])
        rope = sb("rope", [P, 4, 2, 96])
        mask = sb("mask", [P, NA_COLS // ROWS])
        ident = sb("ident", [P, P])
        ones = sb("ones", [P, P])
        stat = sb("stat", [P, NT, 10])
        kc_na = sb("kc_na", [P, 4, P])
        kc_g = sb("kc_g", [P, 2, P])
        kc_mla = sb("kc_mla", [P, P])
        kc_pe = sb("kc_pe", [P, P])
        vc_na = sb("vc_na", [P, 256])
        vc_g = sb("vc_g", [P, P])
        negmax = sb("negmax", [P, UNITS])
        rsum = sb("rsum", [P, UNITS])
        rinv = sb("rinv", [P, UNITS])

        s1 = ExitStack()
        bias_h = sb("bias_h", [P, 2, NA_COLS], F32, s1)
        win = sb("win", [P, WIN + 7], F32, s1)
        sb("pad_h", [P, 10 * T - 2 * NA_COLS - WIN - 7], F32, s1)
        ckvT = sb("ckvT", [P, 2, KEYS], F32R, s1)
        wkv = sb("wkv", [P, 2, KEYS], F32R, s1)
        s1.close()
        hT = sb("hT", [P, KD, 2, T], F32R)

        s2 = ExitStack()
        tn = sb("tn", [P, 2, T], F32, s2)
        hf = sb("hf", [P, 2, T], F32, s2)
        sq = sb("sq", [P, 2, T], F32, s2)
        ada_w1 = sb("ada_w1", [P, DVE_RING1 - DVE_RING2, DM], F32, s2)
        sb("pad_z", [P, NT * IN_COLS - 6 * T - (DVE_RING1 - DVE_RING2) * DM], F32, s2)
        ada_wp = sb("ada_wp", [P, POOL_RING, DM], F32, s2)
        s2.close()
        s3 = ExitStack()
        act = sb("act", [P, 2, 2, T], F32R, s3)
        sl = sb("sl", [P, 2, HALF], F32, s3)
        mm = sb("mm", [P, 2, HALF], F32, s3)
        wo_raw = sb("wo_raw", [P, 2, KD, P], F32, s3)
        wo = sb("wo", [P, 2, 2, KD, P], F32R, s3)
        dw_raw = sb("dw_raw", [P, 2, DM], F32, s3)
        s3.close()
        z = sb("z", [P, NT, IN_COLS])
        qm = sb("qm", [P, NT, QW])
        sb("z_end", [P, 32])

        s4 = ExitStack()
        wi_raw = sb("wi_raw", [P, 2, KD, ICW], F32, s4)
        wi = sb("wi", [P, 2, 2, KD, ICW], F32R, s4)
        s6 = ExitStack()
        silu_c = sb("silu_c", [P, 2, DM], F32, s6)
        s6.close()
        cqT = sb("cqT", [P, 2, 2, T], F32R, s4)
        wq_raw = sb("wq_raw", [P, 2, QW], F32, s4)
        wq = sb("wq", [P, 2, 2, QW], F32R, s4)
        s4.close()
        s5 = ExitStack()
        gw_raw = sb("gw_raw", [P, 2, KD, 256], F32, s5)
        gw = sb("gw", [P, 2, 2, KD, 256], F32R, s5)
        dw = sb("dw", [P, 2, 2, DM], F32R, s5)
        s5.close()
        V = sb("V", [P, 2, 2, 6, 192], F32R)
        K = sb("K", [P, 2, 2, KEYS], F32R)
        Q = sb("Q", [P, 2, 2, T], F32R)
        pT = sb("pT", [P, 2, 2, 512], F32R)
        probs = sb("probs", [P, 2, 4, T])
        probs_p = sb("probs_p", [P, 4, P])
        s7 = ExitStack()
        product = sb("product", [P, DM], F32, s7)
        s7.close()
        ztmp = sb("ztmp", [P, 512])
        wkv_raw = sb("wkv_raw", [P, KEYS])

        ps = ctx.enter_context(nc.psum_tensor("ps", [P, 8, 512], F32))

        const_in = sem("const_in")
        x_in = sem("x_in")
        small_in = sem("small_in")
        ones_set = sem("ones_set")
        cond_in = sem("cond_in")
        silu_done = sem("silu_done")
        dve_in1 = [sem(f"dve_in1_{i}") for i in range(DVE_RING1)]
        dve_in2 = [sem(f"dve_in2_{i}") for i in range(DVE_RING2)]
        pool_in = [sem(f"pool_in{i}") for i in range(POOL_RING)]
        product_ready = sem("product_ready")
        product_summed = sem("product_summed")
        ada_done = sem("ada_done")
        coef_done = sem("coef_done")
        sq_ready = sem("sq_ready")
        acc_ready = sem("acc_ready")
        sq_summed = sem("sq_summed")
        ss_done = sem("ss_done")
        ms_ready = sem("ms_ready")
        rms_ready = sem("rms_ready")
        rstd_ready = sem("rstd_ready")
        tn_ready = sem("tn_ready")
        hf_ready = sem("hf_ready")
        h_hi = sem("h_hi")
        h_ready = sem("h_ready")
        wi_in = [sem(f"wi_in{i}") for i in range(2)]
        wi_hi = sem("wi_hi")
        wi_ready = sem("wi_ready")
        z_ps = sem("z_ps")
        z_done = sem("z_done")
        wq_in = sem("wq_in")
        wkv_in = sem("wkv_in")
        wqk_hi = sem("wqk_hi")
        wq_ready = sem("wq_ready")
        wkv_ready = sem("wkv_ready")
        cstat = sem("cstat")
        cstat_ms = sem("cstat_ms")
        cstat_rms = sem("cstat_rms")
        c_norm = sem("c_norm")
        cT_ps = sem("cT_ps")
        cT_hi = sem("cT_hi")
        cT_ready = sem("cT_ready")
        gsq = sem("gsq")
        gstat = sem("gstat")
        qm_ps = sem("qm_ps")
        qm_done = sem("qm_done")
        q_roped = sem("q_roped")
        g_norm = sem("g_norm")
        g_roped = sem("g_roped")
        kv_out = sem("kv_out")
        norm_out = sem("norm_out")
        vz_done = sem("vz_done")
        win_in = sem("win_in")
        bias_ready = sem("bias_ready")
        misc_ps = sem("misc_ps")
        misc_hi = sem("misc_hi")
        misc_done = sem("misc_done")
        kc_hi = sem("kc_hi")
        v_hi = sem("v_hi")
        v_ready = sem("v_ready")
        s_ready = sem("s_ready")
        biased = sem("biased")
        max_ready = sem("max_ready")
        exp_done = sem("exp_done")
        rinv_ready = sem("rinv_ready")
        p_ready = sem("p_ready")
        p2_ready = sem("p2_ready")
        p3_ready = sem("p3_ready")
        pT_ps = sem("pT_ps")
        pT_hi = sem("pT_hi")
        pT_ready = sem("pT_ready")
        pv_done = sem("pv_done")
        o_hi = sem("o_hi")
        o_ready = sem("o_ready")
        wo_in = [sem(f"wo_in{i}") for i in range(2)]
        wo_hi = sem("wo_hi")
        wo_ready = sem("wo_ready")
        y_ps = sem("y_ps")
        x_done = sem("x_done")
        gw_in = sem("gw_in")
        dw_in = sem("dw_in")
        gw_hi = sem("gw_hi")
        gate_ready = sem("gate_ready")
        up_ready = sem("up_ready")
        dw_hi = sem("dw_hi")
        dw_ready = sem("dw_ready")
        gu_ps = sem("gu_ps")
        sl_ready = sem("sl_ready")
        mm_ready = sem("mm_ready")
        act_hi = sem("act_hi")
        act_ready = sem("act_ready")
        dve_own = sem("dve_own")
        dots = sem("dots")
        pool_own = sem("pool_own")
        act_own = sem("act_own")
        y_ready = sem("y_ready")
        passed_pe = sem("passed_pe")
        passed_sc = sem("passed_sc")
        passed_po = sem("passed_po")
        y_out = sem("y_out")

        XD = KD + FB * KD

        def settled(eng, passed):
            eng.sem_inc(passed, 1)

        block = ctx.enter_context(nc.Block())

        def v_slots(pair, q, t0, n):
            v = V[:, pair % 2, q, t0:t0 + n, :]
            return bass.AP(tensor=v.tensor, offset=v.offset, ap=[list(v.ap[0]), [192, n], [128, 2], [1, 64]])

        def v_sources(g, q):
            kind, h = HEADS[g]
            pair = g // 2
            res = []
            for slot in range(2):
                c0 = NA_V + 64 * (h + slot) if kind == "na" else G_V + 64 * ((h + slot) // 3)
                cc = 64 * (h + slot) if kind == "na" else 64 * ((h + slot) // 3)
                cache = vc_na if kind == "na" else vc_g
                d0 = 128 * slot
                res.append((V[:, pair % 2, q, 0:NT, d0:d0 + 64], z[:, 0:NT, c0:c0 + 64], V[:, pair % 2, 0, 0:NT, d0:d0 + 64]))
                res.append((V[:, pair % 2, q, 5, d0:d0 + 64], cache[:, cc:cc + 64], V[:, pair % 2, 0, 5, d0:d0 + 64]))
            return res

        def dve_slot(t):
            tiles, ring, arrived = (DVE_ADA1, DVE_RING1, dve_in1) if t < ADA1 else (DVE_ADA2, DVE_RING2, dve_in2)
            n = tiles.index(t)
            slot = n % ring
            per_layer = len(range(slot, len(tiles), ring))
            where = ada_w[:, slot] if slot < DVE_RING2 else ada_w1[:, slot - DVE_RING2]
            return where, arrived[slot], lambda l: 16 * (l * per_layer + n // ring + 1)

        def pool_slot(t):
            tiles = POOL_ADA1 + POOL_ADA2
            n = tiles.index(t)
            slot = n % POOL_RING
            per_layer = len(range(slot, len(tiles), POOL_RING))
            return ada_wp[:, slot], pool_in[slot], lambda l: 16 * (l * per_layer + n // POOL_RING + 1), n

        def in_flight(u, lag):
            return ([u - lag] if u >= lag else []) + (list(range(UNITS - lag, UNITS)) if u == UNITS - 1 else [])

        def reciprocals(ve, l, u):
            for w in in_flight(u, 2):
                ve.wait_ge(exp_done, l * UNITS + w + 1)
                ve.reciprocal(rinv[:, w:w + 1], rsum[:, w:w + 1]).then_inc(rinv_ready, 1)
                norm_unit(ve, "dve", l, w)

        def norm_unit(eng, who, l, u):
            g, i = u // 5, u % 5
            if i not in normaliser(g)[who]:
                return
            kind = HEADS[g][0]
            if i == 4:
                t = probs_p[:, g % 4, :]
            elif kind == "na":
                t = probs[:, g % 2, i, 0:(NA_M[i][1] - NA_M[i][0] + 2) * P]
            else:
                t = probs[:, g % 2, i, :]
            eng.wait_ge(rinv_ready, l * UNITS + u + 1)
            if who == "act":
                settled(eng, passed_sc)
                eng.activation(t, t, ACT.Copy, scale=rinv[:, u:u + 1]).then_inc(p2_ready, 1)
            elif who == "dve":
                eng.tensor_scalar(t, t, rinv[:, u:u + 1], None, ALU.mult).then_inc(p3_ready, 1)
            else:
                settled(eng, passed_po)
                eng.tensor_scalar(t, t, rinv[:, u:u + 1], None, ALU.mult).then_inc(p_ready, 1)

        @block.sync
        def _(sp):
            def ada_load(l, t):
                if t in POOL_ADA1 + POOL_ADA2:
                    dst, arrived, _, n = pool_slot(t)
                    if n >= POOL_RING:
                        sp.wait_ge(product_summed, l * PSUMS + 2 * (n - POOL_RING) + 2)
                elif t < ADA1:
                    dst, arrived, _ = dve_slot(t)
                    n = DVE_ADA1.index(t)
                    if n >= DVE_RING1:
                        sp.wait_ge(dots, 2 * (l * NDVE + n - DVE_RING1 + 1))
                else:
                    dst, arrived, _ = dve_slot(t)
                    n = len(DVE_ADA1) + DVE_ADA2.index(t)
                    sp.wait_ge(dots, 2 * (l * NDVE + n - DVE_RING2 + 1))
                sp.dma_start(dst, a["w_adaT"][l, t * P:(t + 1) * P, :]).then_inc(arrived, 16)

            def wi_load(l, c):
                if c >= 2:
                    sp.wait_ge(wi_ready, l * IC + c - 1)
                sp.dma_start(wi_raw[:, c % 2], a["w_in"][l, :, c * ICW:(c + 1) * ICW]
                             .rearrange("(k p) n -> p k n", p=P)).then_inc(wi_in[c % 2], 16)

            with sp.Fori(0, DEPTH) as l:
                sp.wait_ge(x_done, l * XD + 1)
                sp.dma_start(silu_c[:], a["cond"].unsqueeze(0).broadcast_to([P, 2, DM])).then_inc(cond_in, 16)
                for t in range(ADA1):
                    ada_load(l, t)
                    if t == 8:
                        wi_load(l, 0)
                wi_load(l, 1)
                sp.dma_start(kv_g[:], a["kv_g"][bass.ts(l, 1), :].to_broadcast([P, P])).then_inc(small_in, 16)
                sp.dma_start(g8[:], a["g8"][bass.ts(l, 1), :].to_broadcast([P, 512])).then_inc(small_in, 16)
                for r in range(2):
                    sp.dma_start(kc_na[64 * r:64 * r + 64], a["na_kT"][l]).then_inc(small_in, 16)
                    sp.dma_start(kc_g[64 * r:64 * r + 64], a["g_kT"][l]).then_inc(small_in, 16)
                sp.dma_start(kc_mla[:], a["ckvT"][l]).then_inc(small_in, 16)
                sp.dma_start(kc_pe[64:96, :], a["krT"][l]).then_inc(small_in, 16)
                sp.dma_start(vc_na[:], a["na_v"][l]).then_inc(small_in, 16)
                sp.dma_start(vc_g[:], a["g_v"][l]).then_inc(small_in, 16)
                for c in range(1, IC):
                    if c + 1 < IC:
                        wi_load(l, c + 1)
                    if c == 1:
                        sp.dma_start(wq_raw[:], a["w_q_up"][l].rearrange("(k p) n -> p k n", p=P)).then_inc(wq_in, 16)
                    if c >= 2:
                        for t in DVE_ADA2[DVE_GROUP * (c - 2):DVE_GROUP * (c - 1)]:
                            ada_load(l, t)
                    for t in POOL_ADA2[POOL_GROUP * (c - 1):POOL_GROUP * c]:
                        ada_load(l, t)
                sp.wait_ge(product_summed, (l + 1) * PSUMS)
                sp.dma_start(wkv_raw[:], a["w_kv_up"][l]).then_inc(wkv_in, 16)
                tile = NT - 1
                sp.wait_ge(z_done, l * IC * NT + IC * NT)
                for name, c0, w in (("o_kr", OFF_KR, 32), ("o_nak", NA_K, 256), ("o_nav", NA_V, 256), ("o_gv", G_V, P)):
                    sp.dma_start(out[name][l], z[:, tile, c0:c0 + w]).then_inc(kv_out, 16)
                sp.wait_ge(c_norm, l * NT + NT)
                sp.dma_start(out["o_ckv"][l], z[:, tile, OFF_CKV:OFF_KR]).then_inc(norm_out, 16)
                for s in SCHED:
                    if s[0] == "GZ" and s[1] == NT - 1:
                        sp.wait_ge(g_norm, l * NT + NT)
                        sp.dma_start(out["o_gk"][l], z[:, tile, G_K:G_V]).then_inc(norm_out, 16)
                sp.wait_ge(misc_done, l * NM + NM)
                sp.wait_ge(v_ready, l * NV + NV)
                sp.wait_ge(kv_out, l * 64 + 64)
                sp.wait_ge(norm_out, l * 32 + 32)
                for o in range(KD):
                    if o >= 2:
                        sp.wait_ge(wo_ready, l * KD + o - 1)
                    sp.dma_start(wo_raw[:, o % 2], a["w_out"][l, :, o * P:(o + 1) * P]
                                 .rearrange("(k p) n -> p k n", p=P)).then_inc(wo_in[o % 2], 16)
                    if o == 1:
                        sp.wait_ge(o_ready, l * 2 * NP + 2 * NP)
                        sp.dma_start(gw_raw[:, 0], a["w_gate"][l, :, 0:256].rearrange("(k p) n -> p k n", p=P)).then_inc(gw_in, 16)
                        sp.dma_start(gw_raw[:, 1], a["w_up"][l, :, 0:256].rearrange("(k p) n -> p k n", p=P)).then_inc(gw_in, 16)
                        sp.dma_start(dw_raw[:], a["w_down"][l, 0:256, :].rearrange("(j p) n -> p j n", p=P)).then_inc(dw_in, 16)
                with sp.Fori(1, FB) as b:
                    sp.wait_ge(gate_ready, l * FB + b)
                    sp.wait_ge(up_ready, l * FB + b)
                    sp.dma_start(gw_raw[:, 0], a["w_gate"][l, :, bass.ts(b, 256)].rearrange("(k p) n -> p k n", p=P)).then_inc(gw_in, 16)
                    sp.dma_start(gw_raw[:, 1], a["w_up"][l, :, bass.ts(b, 256)].rearrange("(k p) n -> p k n", p=P)).then_inc(gw_in, 16)
                    sp.wait_ge(dw_ready, l * FB + b)
                    sp.dma_start(dw_raw[:], a["w_down"][l, bass.ts(b, 256), :].rearrange("(j p) n -> p j n", p=P)).then_inc(dw_in, 16)
            for k in range(KD):
                sp.wait_ge(y_ready, k + 1)
                sp.dma_start(out["o_y"][k * P:(k + 1) * P, :], x[:, k]).then_inc(y_out, 16)
            sp.wait_ge(y_out, 16 * KD)
            sp.wait_ge(kv_out, DEPTH * 64)
            sp.wait_ge(norm_out, DEPTH * 32)

        @block.tensor
        def _(pe):
            def split_mm(dst, lh, ll, rh, rl, start, stop):
                pe.matmul(dst, lh, rh, start=start, stop=False, skip_group_check=True)
                pe.matmul(dst, lh, rl, start=False, stop=False, skip_group_check=True)
                return pe.matmul(dst, ll, rh, start=False, stop=stop, skip_group_check=True)

            def sum_squares(n):
                pe.wait_ge(acc_ready, n * (KD - 1))
                for j in range(2):
                    m = pe.matmul(ps[:, j, 0:HALF], ones[:], rstd[:, j * HALF:(j + 1) * HALF],
                                  start=True, stop=True, skip_group_check=True)
                m.then_inc(ss_done, 1)

            prev7 = [None]

            def take7(l):
                done, per_layer, n = prev7[0]
                pe.wait_ge(done, l * per_layer + n)

            def misc_step(l, what, g):
                kind, h = HEADS[g]
                take7(l)
                settled(pe, passed_pe)
                if what in ("Qa", "Qb"):
                    if kind == "mla" and g == 4 and what == "Qa":
                        pe.wait_ge(q_roped, 8 * l + 8)
                    if kind == "gqa" and what == "Qa" and h == 0:
                        pe.wait_ge(g_roped, l * 4 + 4)
                        settled(pe, passed_pe)
                if what == "Qa" or (what == "Ka" and kind != "mla") or what == "Qb":
                    ts_ = range(4) if what != "Qb" else [4]
                    for t in ts_:
                        o0 = (t % 4) * P
                        if kind == "mla":
                            m = pe.transpose(ps[0:96, 7, o0:o0 + P], qm[:, t, h * 96:(h + 1) * 96], ident[:])
                            if what == "Qb" and h < 2:
                                m = pe.transpose(ps[0:96, 7, P:2 * P], z[:, t, OFF_KR - 64:OFF_NA], ident[:])
                        else:
                            qc = (NA_Q if kind == "na" else OFF_G) + 64 * h
                            kc = NA_K + 64 * h if kind == "na" else G_K + 64 * (h // 3)
                            c0 = kc if what == "Ka" else qc
                            if kind == "gqa" and what == "Ka" and h == 0 and t == 0:
                                pe.wait_ge(g_roped, l * 4 + 4)
                                pe.wait_ge(g_norm, l * NT + NT)
                                settled(pe, passed_pe)
                            m = pe.transpose(ps[0:64, 7, o0:o0 + P], z[:, t, c0:c0 + 64], ident[:])
                            if what == "Qb" and key_slot(g)[1]:
                                m = pe.transpose(ps[0:64, 7, P:2 * P], z[:, t, kc:kc + 64], ident[:])
                elif what in ("Ka", "Kb"):
                    c0, c1 = (0, LAT) if what == "Ka" else (LAT, KEYS)
                    if g == 4:
                        pe.wait_ge(wkv_ready, l + 1)
                    m = split_mm(ps[0:64, 7, 0:c1 - c0], wkv[:, 0, h * P:h * P + 64], wkv[:, 1, h * P:h * P + 64],
                                 ckvT[:, 0, c0:c1], ckvT[:, 1, c0:c1], True, True)
                elif what == "Kpe":
                    for t in range(4):
                        m = pe.transpose(ps[0:96, 7, t * P:(t + 1) * P], z[:, t, OFF_KR - 64:OFF_NA], ident[:])
                else:
                    tiles = [0, 1, 2, 3] if what == "Va" else [4, 5]
                    for n, t in enumerate(tiles):
                        k0 = {4: 640, 5: LAT}.get(t, t * P)
                        src = [wkv[:, q, h * P:(h + 2) * P].rearrange("p (a b) -> p a b", a=2)[:, :, 64:P] for q in range(2)]
                        m = split_mm(ps[:, 7, n * P:(n + 1) * P], ckvT[:, 0, k0:k0 + P], ckvT[:, 1, k0:k0 + P],
                                     src[0], src[1], True, True)
                m.then_inc(misc_ps, 1)
                prev7[0] = (misc_done, NM, MISC_AT[(what, g)] + 1)

            pe.wait_ge(ones_set, 1)
            with pe.Fori(0, DEPTH) as l:
                pe.wait_ge(x_done, l * XD + 1)
                for k in range(KD):
                    pe.wait_ge(sq_ready, 2 * l * KD + k + 1)
                    for j in range(2):
                        m = pe.matmul(ps[:, j, 0:HALF], ones[:], sq[:, k % 2, j * HALF:(j + 1) * HALF],
                                      start=k == 0, stop=k == KD - 1, skip_group_check=True)
                    m.then_inc(sq_summed, 1)
                for c in range(IC):
                    pe.wait_ge(wi_ready, l * IC + c + 1)
                    for t in range(NT):
                        n = c * NT + t
                        if c == 0 and t == 0:
                            for k in range(KD):
                                pe.wait_ge(h_ready, l * 2 * KD + k + 1)
                                m = split_mm(ps[:, 0, 0:ICW], hT[:, k, 0, 0:P], hT[:, k, 1, 0:P],
                                             wi[:, 0, 0, k, :], wi[:, 0, 1, k, :], k == 0, k == KD - 1)
                            m.then_inc(z_ps, 1)
                            continue
                        if n >= 6:
                            pe.wait_ge(z_done, l * IC * NT + n - 5)
                        for k in range(KD):
                            m = split_mm(ps[:, n % 6, 0:ICW], hT[:, k, 0, t * P:(t + 1) * P], hT[:, k, 1, t * P:(t + 1) * P],
                                         wi[:, c % 2, 0, k, :], wi[:, c % 2, 1, k, :], k == 0, k == KD - 1)
                        m.then_inc(z_ps, 1)
                pe.wait_ge(z_done, l * IC * NT + IC * NT)
                pe.wait_ge(const_in, 16 * 7)
                prev7[0] = (ada_done, 2, 2)
                misc_step(l, "Ka", 0)
                pe.wait_ge(c_norm, l * NT + NT)
                for e in range(3):
                    for t in range(4):
                        m = pe.transpose(ps[:, e, t * P:(t + 1) * P], z[:, t, e * P:(e + 1) * P], ident[:])
                    m.then_inc(cT_ps, 1)
                    if e == 1:
                        misc_step(l, "Qa", 0)
                for e in range(3):
                    m = pe.transpose(ps[:, 3, e * P:(e + 1) * P], z[:, 4, e * P:(e + 1) * P], ident[:])
                m.then_inc(cT_ps, 1)
                misc_step(l, "Qb", 0)
                pe.wait_ge(cT_ready, l * 4 + 4)
                pe.wait_ge(wq_ready, l + 1)
                for n in range(2 * NT):
                    t, j = n // 2, n % 2
                    if n >= 3:
                        pe.wait_ge(qm_done, l * 2 * NT + n - 2)
                    for e in range(2):
                        m = split_mm(ps[:, 4 + n % 3, 0:288], cqT[:, e, 0, t * P:(t + 1) * P], cqT[:, e, 1, t * P:(t + 1) * P],
                                     wq[:, e, 0, j * 288:(j + 1) * 288], wq[:, e, 1, j * 288:(j + 1) * 288], e == 0, e == 1)
                    m.then_inc(qm_ps, 1)
                pe.wait_ge(qm_done, l * 2 * NT + 2 * NT)
                pending = []

                def flush():
                    if pending:
                        pending.pop()()

                for s in SCHED:
                    if s[0] == "S":
                        _, g, i = s
                        kind = HEADS[g][0]
                        u, gb, kb = S_AT[s], g % 2, key_slot(g)[0]
                        if i == 0:
                            pe.wait_ge(misc_done, l * NM + MISC_AT[prep_steps(g)[-1]] + 1)
                        if u >= 2:
                            pe.wait_ge(exp_done, l * UNITS + u - 1)
                        bk = 2 * (u % 2)
                        qs = slice(i * P, (i + 1) * P)
                        if i == 4:
                            parts = [(bk, 0, P, 640)]
                        elif kind == "na":
                            m0, m1 = NA_M[i]
                            w = (m1 - m0 + 1) * P
                            parts = [(bk, 0, w, m0 * P), (bk, w, P, LAT)]
                        else:
                            parts = [(bk, 0, HALF, 0), (bk + 1, 0, HALF, HALF)]
                        for n, (bank, c0, w, k0) in enumerate(parts):
                            dst = ps[:, bank, c0:c0 + w]
                            first = c0 == 0
                            if kind == "mla":
                                m = split_mm(dst, Q[0:96, gb, 0, qs], Q[0:96, gb, 1, qs], K[0:96, kb, 0, k0:k0 + w],
                                             K[0:96, kb, 1, k0:k0 + w], first, True)
                            else:
                                pe.matmul(dst, Q[:, gb, 0, qs], K[:, kb, 0, k0:k0 + w], start=first, stop=False,
                                          skip_group_check=True)
                                m = pe.matmul(dst, Q[:, gb, 0, qs], K[:, kb, 1, k0:k0 + w], start=False, stop=True,
                                              skip_group_check=True)
                        m.then_inc(s_ready, 1)
                    elif s[0] == "T":
                        _, g, mt = s
                        kind = HEADS[g][0]
                        n = T_AT[s]
                        if mt == 0:
                            pe.wait_ge(p_ready, l * normalised("pool", NH) + normalised("pool", g + 1) - 1)
                            pe.wait_ge(p2_ready, l * normalised("act", NH) + normalised("act", g + 1))
                            pe.wait_ge(p3_ready, l * NH + g + 1)
                        if n >= 2:
                            pe.wait_ge(pT_ready, l * TS + n - 1)
                        a0, a1 = na_range(mt) if kind == "na" else (0, 3)
                        for i in range(a0, a1 + 1):
                            if kind == "na":
                                m0, m1 = NA_M[i]
                                pos = (m1 - m0 + 1 if mt == 4 else mt - m0) * P
                            else:
                                pos = mt * P
                            m = pe.transpose(ps[:, 4 + n % 2, i * P:(i + 1) * P], probs[:, g % 2, i, pos:pos + P], ident[:])
                        m.then_inc(pT_ps, 1)
                        flush()

                        def pv(g=g, mt=mt, n=n, a0=a0, a1=a1):
                            pair, slot = g // 2, g % 2
                            if slot == 0 and mt == 0:
                                if kind_of_pair(pair) == "mla":
                                    pe.wait_ge(misc_done, l * NM + MISC_AT[("Vb", 2 * pair)] + 1)
                                else:
                                    pe.wait_ge(v_ready, l * NV + v_at(pair) + 1)
                                if pair > 0:
                                    pe.wait_ge(o_ready, l * 2 * NP + 2 * pair - 1)
                            pe.wait_ge(pT_ready, l * TS + n + 1)
                            vt = 5 if mt == 4 else mt
                            cols = slice(a0 * P, (a1 + 1) * P)
                            lh, ll = (V[:, pair % 2, q, vt, 64 * slot:64 * slot + P] for q in range(2))
                            m = split_mm(ps[:, 6, cols], lh, ll, pT[:, n % 2, 0, cols], pT[:, n % 2, 1, cols],
                                         slot == 0 and mt == 0, False)
                            m.then_inc(pv_done, 1)
                        pending.append(pv)
                    elif s[0] == "TP":
                        pair = s[1]
                        n = T_AT[s]
                        pe.wait_ge(p_ready, l * normalised("pool", NH) + normalised("pool", 2 * pair + 2))
                        pe.wait_ge(pT_ready, l * TS + n - 1)
                        for slot in range(2):
                            m = pe.transpose(ps[:, 4 + n % 2, slot * P:(slot + 1) * P], probs_p[:, (2 * pair + slot) % 4, :], ident[:])
                        m.then_inc(pT_ps, 1)
                        flush()

                        def pvp(pair=pair, n=n):
                            pe.wait_ge(pT_ready, l * TS + n + 1)
                            take7(l)
                            for slot in range(2):
                                lh, ll = (V[:, pair % 2, q, 4, 64 * slot:64 * slot + P] for q in range(2))
                                cols = slice(slot * P, (slot + 1) * P)
                                m = split_mm(ps[:, 7, 0:P], lh, ll, pT[:, n % 2, 0, cols], pT[:, n % 2, 1, cols],
                                             slot == 0, slot == 1)
                            m.then_inc(pv_done, 1)
                            prev7[0] = (o_ready, 2 * NP, 2 * pair + 2)
                        pending.append(pvp)
                    elif s[0] == "OP":
                        flush()
                    elif s[0] == "M":
                        misc_step(l, *s[1:])
                pe.wait_ge(o_ready, l * 2 * NP + 2 * NP)
                for o in range(KD):
                    pe.wait_ge(wo_ready, l * KD + o + 1)
                    if o >= 3:
                        pe.wait_ge(x_done, l * XD + 1 + o - 2)
                    for j in range(2):
                        for k in range(KD):
                            cols = slice(j * HALF, (j + 1) * HALF)
                            m = split_mm(ps[:, 2 + 2 * (o % 3) + j, 0:HALF], wo[:, o % 2, 0, k, :], wo[:, o % 2, 1, k, :],
                                         hT[:, k, 0, cols], hT[:, k, 1, cols], k == 0, k == KD - 1)
                    m.then_inc(y_ps, 1)
                sum_squares(l + 1)
                pe.wait_ge(h_ready, l * 2 * KD + 2 * KD)
                settled(pe, passed_pe)

                def ffn_block(b):
                    for j in range(2):
                        for w in range(2):
                            pe.wait_ge(x_done, l * XD + 1 + KD + b * KD - 3 + 2 * j + w)
                            if j == 0:
                                pe.wait_ge(up_ready if w else gate_ready, l * FB + b + 1)
                            for hf_ in range(2):
                                cols = slice(hf_ * HALF, (hf_ + 1) * HALF)
                                for k in range(KD):
                                    m = split_mm(ps[:, 4 * j + 2 * w + hf_, 0:HALF], gw[:, w, 0, k, j * P:(j + 1) * P],
                                                 gw[:, w, 1, k, j * P:(j + 1) * P], hT[:, k, 0, cols], hT[:, k, 1, cols],
                                                 k == 0, k == KD - 1)
                                m.then_inc(gu_ps, 1)
                    base = (l * FB + b) * 4

                    def down(o, j, hf_):
                        cols = slice(hf_ * HALF, (hf_ + 1) * HALF)
                        return split_mm(ps[:, 2 * (o % 4) + hf_, 0:HALF], dw[:, 0, j, o * P:(o + 1) * P],
                                        dw[:, 1, j, o * P:(o + 1) * P], act[:, j, 0, cols], act[:, j, 1, cols],
                                        j == 0, j == 1)
                    pe.wait_ge(dw_ready, l * FB + b + 1)
                    pe.wait_ge(act_ready, base + 3)
                    for o in range(3):
                        if o == 2:
                            pe.wait_ge(sl_ready, base + 4)
                        for hf_ in range(2):
                            down(o, 0, hf_)
                    pe.wait_ge(act_ready, base + 4)
                    for o in range(3):
                        down(o, 1, 0)
                    pe.wait_ge(act_ready, base + 5)
                    for o in range(3):
                        down(o, 1, 1).then_inc(y_ps, 1)
                    for o in range(3, KD):
                        if o >= 4:
                            pe.wait_ge(x_done, l * XD + 1 + KD + b * KD + o - 3)
                        for hf_ in range(2):
                            for j in range(2):
                                m = down(o, j, hf_)
                        m.then_inc(y_ps, 1)

                with pe.Fori(0, FB) as b:
                    ffn_block(b)
            pe.wait_ge(x_done, DEPTH * XD + 1)
            sum_squares(DEPTH + 1)

        @block.scalar
        def _(sc):
            def square(n, x_first, k):
                sc.wait_ge(x_done, x_first + k)
                if k >= 2:
                    sc.wait_ge(acc_ready, n * (KD - 1) + max(1, k - 2))
                sc.activation(sq[:, k % 2], x[:, k], ACT.Square).then_inc(sq_ready, 1)

            def rms(n):
                sc.wait_ge(ms_ready, n)
                sc.activation(rstd[:], rstd[:], ACT.Sqrt).then_inc(rms_ready, 1)

            def modulated(l, nrm):
                base = l * 2 * KD + nrm * KD
                sc.wait_ge(coef_done, l * 2 + nrm + 1)
                for k in range(KD):
                    sc.wait_ge(tn_ready, base + k + 1)
                    for q, (c0, c1) in enumerate(((0, LAT), (LAT, T))):
                        i = sc.activation(hT[:, k, 0, c0:c1], tn[:, k % 2, c0:c1], ACT.Identity,
                                          bias=mod[:, 24 * nrm + k, q:q + 1], scale=coef[:, nrm, k, q:q + 1])
                    i.then_inc(h_hi, 1)

            def cached_keys(l, g):
                kind, h = HEADS[g]
                gb, (kb, new_keys) = g % 2, key_slot(g)
                if g >= 2:
                    sc.wait_ge(s_ready, l * UNITS + 5 * (g - 1))
                if kind == "na":
                    sc.activation(K[:, kb, 0, LAT:640], kc_na[:, h, :], ACT.Copy).then_inc(kc_hi, 1)
                elif kind == "gqa" and new_keys:
                    sc.activation(K[:, kb, 0, LAT:640], kc_g[:, h // 3, :], ACT.Copy).then_inc(kc_hi, 1)
                elif kind == "mla" and h < 2:
                    sc.activation(K[64:96, kb, 0, LAT:640], kc_pe[64:96, :], ACT.Copy).then_inc(kc_hi, 1)

            def misc_hi_part(l, what, g):
                kind, h = HEADS[g]
                gb, (kb, new_keys) = g % 2, key_slot(g)
                e = MISC_AT[(what, g)]
                sc.wait_ge(misc_ps, l * NM + e + 1)
                hi = 96 if kind == "mla" else 64
                scale = MLA_SCALE if kind == "mla" else HD_SCALE
                if what == "Qa":
                    i = sc.activation(Q[0:hi, gb, 0, 0:LAT], ps[0:hi, 7, :], ACT.Copy, scale=scale)
                elif what == "Qb":
                    i = sc.activation(Q[0:hi, gb, 0, LAT:T], ps[0:hi, 7, 0:P], ACT.Copy, scale=scale)
                    if kind == "mla" and h < 2:
                        i = sc.activation(K[64:96, kb, 0, 640:KEYS], ps[64:96, 7, P:2 * P], ACT.Copy)
                    if kind != "mla" and new_keys:
                        for r0 in (0, 64):
                            i = sc.activation(K[r0:r0 + 64, kb, 0, 640:KEYS], ps[0:64, 7, P:2 * P], ACT.Copy)
                elif what == "Ka":
                    for r0 in (0,) if kind == "mla" else (0, 64):
                        i = sc.activation(K[r0:r0 + 64, kb, 0, 0:LAT], ps[0:64, 7, :], ACT.Copy)
                elif what == "Kb":
                    i = sc.activation(K[0:64, kb, 0, LAT:KEYS], ps[0:64, 7, 0:256], ACT.Copy)
                elif what == "Kpe":
                    i = sc.activation(K[64:96, kb, 0, 0:LAT], ps[64:96, 7, :], ACT.Copy)
                else:
                    pair = g // 2
                    if what == "Va" and pair >= 2:
                        sc.wait_ge(pv_done, l * TS + T_AT[("TP", pair - 2)] + 1)
                    t0, n = (0, 4) if what == "Va" else (4, 2)
                    dst = v_slots(pair, 0, t0, n)
                    i = sc.activation(dst, ps[:, 7, 0:n * P].rearrange("p (t a b) -> p t a b", t=n, a=2), ACT.Copy)
                i.then_inc(misc_hi, 1)

            def exponentials(l, u):
                g, i = u // 5, u % 5
                kind = HEADS[g][0]
                bk = 2 * (u % 2)
                sc.wait_ge(max_ready, l * UNITS + u + 1)
                if i == 0 and g >= 2:
                    sc.wait_ge(pT_ps, l * TS + last_t_of(g - 2) + 1)
                if i == 4:
                    if g >= 4:
                        sc.wait_ge(pT_ps, l * TS + T_AT[("TP", g // 2 - 2)] + 1)
                    src, dst = ps[:, bk, 0:P], probs_p[:, g % 4, :]
                elif kind == "na":
                    w = (NA_M[i][1] - NA_M[i][0] + 2) * P
                    src, dst = ps[:, bk, 0:w], probs[:, g % 2, i, 0:w]
                else:
                    src = ps[:, bk:bk + 2, 0:HALF]
                    dst = probs[:, g % 2, i, :].rearrange("p (a b) -> p a b", a=2)
                sc.activation(dst, src, ACT.Exp, bias=negmax[:, u:u + 1], accum_out=rsum[:, u:u + 1]).then_inc(exp_done, 1)

            for k in range(KD):
                sc.dma_start(x[:, k, :], a["x"][k * P:(k + 1) * P, :]).then_inc(x_in, 16)
            for dst, src in ((b_ada, a["b_ada"]), (norm_g, a["norm_g"]), (fin_g, a["fin_g"]), (qn_g, a["qn_g"]),
                             (rope, a["rope"]), (mask, a["mask"]), (ident, a["ident"])):
                sc.dma_start(dst[:], src).then_inc(const_in, 16)

            def sum_product(l, n, q):
                t = (POOL_ADA1 + POOL_ADA2)[n]
                v = ada_wp[:, n % POOL_RING] if q else product[:]
                sc.wait_ge(product_ready, l * PSUMS + 2 * n + q + 1)
                sc.activation(v, v, ACT.Copy, accum_out=mod[:, t, q:q + 1]).then_inc(product_summed, 1)

            with sc.Fori(0, DEPTH) as l:
                sc.wait_ge(x_done, l * XD + 1)
                sc.wait_ge(cond_in, 16 * l + 16)
                sc.activation(silu_c[:], silu_c[:], ACT.Silu).then_inc(silu_done, 1)
                sum_product(l, 0, 0)
                for k in range(KD):
                    if k >= 2:
                        sc.wait_ge(sq_summed, l * KD + k - 1)
                    else:
                        sc.wait_ge(x_in, 16 * KD)
                    sc.activation(sq[:, k % 2], x[:, k], ACT.Square).then_inc(sq_ready, 1)
                    if k in (1, 3, 4, 6, 7):
                        n = 1 + (1, 3, 4, 6, 7).index(k)
                        sum_product(l, n // 2, n % 2)
                rms(l * 2 + 1)

                def wi_split(c):
                    sc.wait_ge(wi_in[c % 2], 16 * (l * (IC // 2) + c // 2 + 1))
                    if c >= 2:
                        sc.wait_ge(z_ps, l * IC * NT + (c - 1) * NT)
                    sc.activation(wi[:, c % 2, 0], wi_raw[:, c % 2], ACT.Copy).then_inc(wi_hi, 1)
                wi_split(0)
                for n in range(3, len(POOL_ADA1)):
                    sum_product(l, n, 0)
                    sum_product(l, n, 1)
                modulated(l, 0)
                wi_split(1)
                for c in range(IC):
                    for t in range(NT):
                        n = c * NT + t
                        sc.wait_ge(z_ps, l * IC * NT + n + 1)
                        sc.activation(z[:, t, c * ICW:(c + 1) * ICW], ps[:, n % 6, 0:ICW], ACT.Copy).then_inc(z_done, 1)
                        if c >= 1 and t < 2 * POOL_GROUP:
                            sum_product(l, len(POOL_ADA1) + POOL_GROUP * (c - 1) + t // 2, t % 2)
                    if c + 2 < IC:
                        wi_split(c + 2)
                    if c == 3:
                        sc.wait_ge(wq_in, 16 * l + 16)
                        sc.activation(wq[:, :, 0, :], wq_raw[:], ACT.Copy).then_inc(wqk_hi, 1)
                    if c == 5:
                        sc.wait_ge(z_done, l * IC * NT + 2 * NT)
                        for t in range(NT):
                            sc.activation(rstd[:, 0:256], z[:, t, 0:256], ACT.Square, accum_out=stat[:, t, 0:1]).then_inc(act_own, 1)
                            sc.wait_ge(act_own, l * 2 * NT + 2 * t + 1)
                            i = sc.activation(rstd[:, 0:P], z[:, t, OFF_CKV:OFF_KR], ACT.Square, accum_out=stat[:, t, 1:2])
                            i.then_inc(act_own, 1)
                            sc.wait_ge(act_own, l * 2 * NT + 2 * t + 2)
                        sc.wait_ge(cstat_ms, 2 * l + 1)
                        sc.activation(stat[:, :, 0:2], stat[:, :, 0:2], ACT.Sqrt).then_inc(cstat_rms, 1)
                sc.wait_ge(z_done, l * IC * NT + IC * NT)
                sc.wait_ge(small_in, (l + 1) * 160)
                cached_keys(l, 0)
                misc_hi_part(l, "Ka", 0)
                for e in range(4):
                    sc.wait_ge(cT_ps, l * 4 + e + 1)
                    settled(sc, passed_sc)
                    if e == 2:
                        misc_hi_part(l, "Qa", 0)
                    if e < 2:
                        sc.activation(cqT[:, e, 0, 0:LAT], ps[:, e, :], ACT.Copy, scale=qn_g[:, l, e:e + 1]).then_inc(cT_hi, 1)
                    elif e == 2:
                        sc.activation(ckvT[:, 0, 0:LAT], ps[:, e, :], ACT.Copy).then_inc(cT_hi, 1)
                    else:
                        for q in range(2):
                            sc.activation(cqT[:, q, 0, LAT:T], ps[:, 3, q * P:(q + 1) * P], ACT.Copy, scale=qn_g[:, l, q:q + 1])
                        sc.activation(ckvT[:, 0, 640:KEYS], ps[:, 3, 2 * P:3 * P], ACT.Copy).then_inc(cT_hi, 1)
                misc_hi_part(l, "Qb", 0)
                for n in range(2 * NT):
                    t, j = n // 2, n % 2
                    sc.wait_ge(qm_ps, l * 2 * NT + n + 1)
                    sc.activation(qm[:, t, j * 288:(j + 1) * 288], ps[:, 4 + n % 3, 0:288], ACT.Copy).then_inc(qm_done, 1)
                sc.wait_ge(qm_ps, l * 2 * NT + 2 * NT)
                sc.wait_ge(wq_ready, l + 1)
                sc.wait_ge(vz_done, l + 1)
                for s in SCHED:
                    if s[0] == "S":
                        for u in in_flight(S_AT[s], 1):
                            exponentials(l, u)
                    elif s[0] in ("T", "TP"):
                        n = T_AT[s]
                        if s[0] == "TP":
                            c0, c1 = 0, 2 * P
                        else:
                            a0, a1 = na_range(s[2]) if HEADS[s[1]][0] == "na" else (0, 3)
                            c0, c1 = a0 * P, (a1 + 1) * P
                        sc.wait_ge(pT_ps, l * TS + n + 1)
                        if n >= 2:
                            sc.wait_ge(pv_done, l * TS + n - 1)
                        sc.activation(pT[:, n % 2, 0, c0:c1], ps[:, 4 + n % 2, c0:c1], ACT.Copy).then_inc(pT_hi, 1)
                    elif s[0] == "OL":
                        sc.wait_ge(pv_done, l * TS + T_AT[("TP", s[1])])
                        sc.activation(hT[:, PAIR_TILE[s[1]], 0, 0:LAT], ps[:, 6, :], ACT.Copy).then_inc(o_hi, 1)
                    elif s[0] == "OP":
                        sc.wait_ge(pv_done, l * TS + T_AT[("TP", s[1])] + 1)
                        sc.activation(hT[:, PAIR_TILE[s[1]], 0, LAT:T], ps[:, 7, 0:P], ACT.Copy).then_inc(o_hi, 1)
                    elif s[0] == "N":
                        norm_unit(sc, "act", l, 5 * s[1] + s[2])
                    elif s[0] == "C":
                        cached_keys(l, s[1])
                    elif s[0] == "M":
                        misc_hi_part(l, *s[1:])
                    elif s[0] == "WK":
                        sc.wait_ge(wkv_in, 16 * l + 16)
                        settled(sc, passed_sc)
                        sc.activation(wkv[:, 0], wkv_raw[:], ACT.Copy).then_inc(wqk_hi, 1)
                        sc.activation(ckvT[:, 0, LAT:640], kc_mla[:], ACT.Copy).then_inc(wqk_hi, 1)
                    elif s[0] == "GS":
                        t = s[1]
                        if t:
                            sc.wait_ge(gstat, l * NT + t)
                        sc.activation(ztmp[:], z[:, t, OFF_G:G_V], ACT.Square).then_inc(gsq, 1)
                    elif s[0] == "GR":
                        sc.wait_ge(cstat_ms, 2 * l + 2)
                        sc.activation(stat[:, :, 2:10], stat[:, :, 2:10], ACT.Sqrt).then_inc(cstat_rms, 1)
                    elif s[0] == "V":
                        g = s[1]
                        pair = g // 2
                        if pair >= 2:
                            sc.wait_ge(pv_done, l * TS + T_AT[("TP", pair - 2)] + 1)
                        for dst, src, _ in v_sources(g, 0):
                            i = sc.activation(dst, src, ACT.Copy)
                        i.then_inc(v_hi, 1)
                for o in range(KD):
                    sc.wait_ge(wo_in[o % 2], 16 * (l * (KD // 2) + o // 2 + 1))
                    if o >= 2:
                        sc.wait_ge(y_ps, l * XD + o - 1)
                    sc.activation(wo[:, o % 2, 0], wo_raw[:, o % 2], ACT.Copy).then_inc(wo_hi, 1)
                    if o >= 3:
                        square(l, l * XD + 2, o - 3)
                def gw_split(b):
                    sc.wait_ge(gw_in, 32 * (l * FB + b) + 32)
                    for w in range(2):
                        sc.activation(gw[:, w, 0], gw_raw[:, w], ACT.Copy).then_inc(gw_hi, 1)
                gw_split(0)
                for k in range(5, KD):
                    square(l, l * XD + 2, k)
                rms(l * 2 + 2)
                modulated(l, 1)

                def ffn_block(b, last):
                    base = (l * FB + b) * 4
                    for j in range(2):
                        for hf_ in range(2):
                            sc.wait_ge(gu_ps, base * 2 + 4 * j + hf_ + 1)
                            sc.activation(sl[:, hf_], ps[:, 4 * j + hf_, 0:HALF], ACT.Silu).then_inc(sl_ready, 1)
                        if j == 0:
                            sc.wait_ge(dw_in, 16 * (l * FB + b) + 16)
                            sc.wait_ge(y_ps, l * XD + KD + b * KD)
                            sc.activation(dw[:, 0], dw_raw[:], ACT.Copy).then_inc(dw_hi, 1)
                        for hf_ in range(2):
                            sc.wait_ge(mm_ready, base + 2 * j + hf_ + 1)
                            sc.activation(act[:, j, 0, hf_ * HALF:(hf_ + 1) * HALF], mm[:, hf_], ACT.Copy).then_inc(act_hi, 1)
                    if not last:
                        sc.wait_ge(gu_ps, base * 2 + 8)
                        gw_split(b + 1)

                with sc.Fori(0, FB - 1) as b:
                    ffn_block(b, False)
                ffn_block(FB - 1, True)
            sc.wait_ge(x_done, DEPTH * XD + 1)
            for k in range(KD):
                square(DEPTH, DEPTH * XD + 1 - k, k)
            rms(DEPTH * 2 + 1)

        @block.vector
        def _(ve):
            def f(t):
                return t.bitcast(F32)

            def lo(dst, src, hi):
                return ve.tensor_tensor(dst, src, f(hi), ALU.subtract)

            def ada(l, t):
                w, arrived, count = dve_slot(t)
                ve.wait_ge(arrived, count(l))
                junk = ps[:, 6:8, :].rearrange("p a b -> p (a b)")
                for q in range(2):
                    own = 2 * (l * NDVE + (DVE_ADA1 + DVE_ADA2).index(t)) + q
                    if q or t:
                        ve.wait_ge(dots, own)
                    i = ve.scalar_tensor_tensor(out=junk, in0=w, scalar=1.0, in1=silu_c[:, q], op0=ALU.mult,
                                                op1=ALU.mult, accum_out=mod[:, t, q:q + 1])
                    i.then_inc(dots, 1)

            def ada_bias(l, t0, t1, summed):
                ve.wait_ge(product_summed, l * PSUMS + summed)
                ve.wait_ge(dots, 2 * (l * NDVE + len([t for t in DVE_ADA1 + DVE_ADA2 if t < t1])))
                ve.tensor_tensor(mod[:, t0:t1, :], mod[:, t0:t1, :],
                                 b_ada[:, l, t0:t1].unsqueeze(2).broadcast_to([P, t1 - t0, 2]), ALU.add).then_inc(ada_done, 1)

            def coefs(l, nrm):
                t0 = 24 * nrm + 8
                ve.wait_ge(ada_done, 2 * l + nrm + 1)
                ve.scalar_tensor_tensor(out=coef[:, nrm], in0=mod[:, t0:t0 + KD, :], scalar=1.0,
                                        in1=norm_g[:, l, nrm, :].unsqueeze(2).broadcast_to([P, KD, 2]),
                                        op0=ALU.add, op1=ALU.mult).then_inc(coef_done, 1)

            def add_square(n, sq_n, k):
                ve.wait_ge(sq_ready, sq_n * KD + k + 1)
                if k == 1:
                    ve.tensor_tensor(rstd[:], sq[:, 0], sq[:, 1], ALU.add).then_inc(acc_ready, 1)
                elif k >= 2:
                    ve.wait_ge(acc_ready, n * (KD - 1) + k - 1)
                    ve.tensor_tensor(rstd[:], rstd[:], sq[:, k % 2], ALU.add).then_inc(acc_ready, 1)

            def mean_square(n, summed, count):
                ve.wait_ge(summed, count)
                ve.tensor_scalar(rstd[:].rearrange("p (a b) -> p a b", a=2), ps[:, 0:2, 0:HALF], 1.0 / DM, EPS,
                                 ALU.mult, ALU.add).then_inc(ms_ready, 1)
                ve.wait_ge(rms_ready, n)
                ve.reciprocal(rstd[:], rstd[:]).then_inc(rstd_ready, 1)

            def modulated(l, nrm):
                base = l * 2 * KD + nrm * KD
                ve.wait_ge(coef_done, 2 * l + nrm + 1)
                for k in range(KD + 1):
                    if k < KD:
                        ve.wait_ge(tn_ready, base + k + 1)
                        if k >= 2:
                            ve.wait_ge(h_ready, base + k - 1)
                        for q, (c0, c1) in enumerate(((0, LAT), (LAT, T))):
                            i = ve.tensor_scalar(hf[:, k % 2, c0:c1], tn[:, k % 2, c0:c1], coef[:, nrm, k, q:q + 1],
                                                 mod[:, 24 * nrm + k, q:q + 1], ALU.mult, ALU.add)
                        i.then_inc(hf_ready, 1)
                    if k >= 1:
                        ve.wait_ge(hf_ready, base + k)
                        ve.wait_ge(h_hi, base + k)
                        lo(hT[:, k - 1, 1], hf[:, (k - 1) % 2], hT[:, k - 1, 0]).then_inc(h_ready, 1)

            def residual(l, y, o, banks, part):
                ve.wait_ge(y_ps, y)
                for hf_, c0, c1, q in ((0, 0, HALF, 0), (1, HALF, LAT, 0), (1, LAT, T, 1)):
                    s0 = c0 - hf_ * HALF
                    i = ve.scalar_tensor_tensor(out=x[:, o, c0:c1], in0=ps[:, banks + hf_, s0:s0 + c1 - c0],
                                                scalar=mod[:, part * KD + o, q:q + 1], in1=x[:, o, c0:c1],
                                                op0=ALU.mult, op1=ALU.add)
                i.then_inc(x_done, 1)

            def cached_keys(l, g):
                kind, h = HEADS[g]
                gb, (kb, new_keys) = g % 2, key_slot(g)
                if kind == "na":
                    n, src, r = g, kc_na[0:64, h, :], slice(0, 64)
                elif kind == "gqa" and new_keys:
                    n, src, r = 6 + kb, kc_g[0:64, h // 3, :], slice(0, 64)
                elif kind == "mla" and h < 2:
                    n, src, r = g, kc_pe[64:96, :], slice(64, 96)
                else:
                    return
                ve.wait_ge(kc_hi, l * 8 + n + 1)
                if kind == "gqa" or kind == "na" and h < 2:
                    ve.memset(K[64:P, kb, 1, :].bitcast(F32), 0.0)
                lo(K[r, kb, 1, LAT:640], src, K[r, kb, 0, LAT:640])

            def misc_lo_part(l, what, g):
                kind, h = HEADS[g]
                gb, (kb, new_keys) = g % 2, key_slot(g)
                ve.wait_ge(misc_hi, l * NM + MISC_AT[(what, g)] + 1)
                if what in ("Qa", "Qb"):
                    c0, c1 = (0, LAT) if what == "Qa" else (LAT, T)
                    if kind == "mla":
                        r, dst, scale = slice(0, 96), Q[0:96, gb, 1, c0:c1], MLA_SCALE
                    else:
                        r, dst, scale = slice(0, 64), Q[64:P, gb, 0, c0:c1], HD_SCALE
                    i = ve.scalar_tensor_tensor(out=dst, in0=ps[r, 7, 0:c1 - c0], scalar=scale,
                                                in1=f(Q[r, gb, 0, c0:c1]), op0=ALU.mult, op1=ALU.subtract)
                    if what == "Qb" and kind == "mla" and h < 2:
                        i = lo(K[64:96, kb, 1, 640:KEYS], ps[64:96, 7, P:2 * P], K[64:96, kb, 0, 640:KEYS])
                    if what == "Qb" and kind != "mla" and new_keys:
                        i = lo(K[0:64, kb, 1, 640:KEYS], ps[0:64, 7, P:2 * P], K[0:64, kb, 0, 640:KEYS])
                elif what == "Ka":
                    r = slice(0, 64)
                    i = lo(K[r, kb, 1, 0:LAT], ps[r, 7, :], K[r, kb, 0, 0:LAT])
                elif what == "Kb":
                    i = lo(K[0:64, kb, 1, LAT:KEYS], ps[0:64, 7, 0:256], K[0:64, kb, 0, LAT:KEYS])
                elif what == "Kpe":
                    i = lo(K[64:96, kb, 1, 0:LAT], ps[64:96, 7, :], K[64:96, kb, 0, 0:LAT])
                else:
                    pair = g // 2
                    t0, n = (0, 4) if what == "Va" else (4, 2)
                    src = ps[:, 7, 0:n * P].rearrange("p (t a b) -> p t a b", t=n, a=2)
                    i = lo(v_slots(pair, 1, t0, n), src, v_slots(pair, 0, t0, n))
                i.then_inc(misc_done, 1)

            ve.sem_inc(x_done, 1)
            ve.sem_inc(act_ready, 1)
            with ve.Fori(0, DEPTH) as l:
                ve.wait_ge(silu_done, l + 1)
                for t in DVE_ADA1[:6]:
                    ada(l, t)
                mean_square(2 * l + 1, sq_summed, l * KD + KD)
                for t in DVE_ADA1[6:]:
                    ada(l, t)
                def wi_split(c):
                    ve.wait_ge(wi_hi, l * IC + c + 1)
                    lo(wi[:, c % 2, 1], wi_raw[:, c % 2], wi[:, c % 2, 0]).then_inc(wi_ready, 1)
                wi_split(0)
                ve.wait_ge(const_in, 16 * 7)
                ada_bias(l, 0, ADA1, 2 * len(POOL_ADA1))
                coefs(l, 0)

                modulated(l, 0)
                wi_split(1)
                for c in range(2, IC):
                    wi_split(c)
                    if c == IC - 1:
                        ve.wait_ge(act_own, (l + 1) * 2 * NT)
                        ve.tensor_scalar(stat[:, :, 0:1], stat[:, :, 0:1], 1.0 / 256, EPS, ALU.mult, ALU.add)
                        ve.tensor_scalar(stat[:, :, 1:2], stat[:, :, 1:2], 1.0 / P, EPS, ALU.mult, ALU.add).then_inc(cstat_ms, 1)
                    for t in DVE_ADA2[DVE_GROUP * (c - 2):DVE_GROUP * (c - 1)]:
                        ada(l, t)
                    if c == 5:
                        ve.wait_ge(wqk_hi, 3 * l + 1)
                        lo(wq[:, :, 1, :], wq_raw[:], wq[:, :, 0, :]).then_inc(wq_ready, 1)
                ve.wait_ge(cstat_rms, 2 * l + 1)
                ve.reciprocal(stat[:, :, 0:2], stat[:, :, 0:2]).then_inc(cstat, 1)
                ve.wait_ge(cstat, 2 * l + 1)
                ve.wait_ge(small_in, (l + 1) * 160)
                for t in range(NT):
                    ve.tensor_scalar(z[:, t, 0:256], z[:, t, 0:256], stat[:, t, 0:1], None, ALU.mult)
                    ve.scalar_tensor_tensor(out=z[:, t, OFF_CKV:OFF_KR], in0=z[:, t, OFF_CKV:OFF_KR],
                                            scalar=stat[:, t, 1:2], in1=kv_g[:], op0=ALU.mult, op1=ALU.mult).then_inc(c_norm, 1)
                ada_bias(l, ADA1, NADA, PSUMS)
                coefs(l, 1)
                cached_keys(l, 0)
                misc_lo_part(l, "Ka", 0)
                for e in range(4):
                    if e == 2:
                        misc_lo_part(l, "Qa", 0)
                    ve.wait_ge(cT_hi, l * 4 + e + 1)
                    if e < 2:
                        ve.scalar_tensor_tensor(out=cqT[:, e, 1, 0:LAT], in0=ps[:, e, :], scalar=qn_g[:, l, e:e + 1],
                                                in1=f(cqT[:, e, 0, 0:LAT]), op0=ALU.mult, op1=ALU.subtract).then_inc(cT_ready, 1)
                    elif e == 2:
                        lo(ckvT[:, 1, 0:LAT], ps[:, e, :], ckvT[:, 0, 0:LAT]).then_inc(cT_ready, 1)
                    else:
                        for q in range(2):
                            ve.scalar_tensor_tensor(out=cqT[:, q, 1, LAT:T], in0=ps[:, 3, q * P:(q + 1) * P],
                                                    scalar=qn_g[:, l, q:q + 1], in1=f(cqT[:, q, 0, LAT:T]),
                                                    op0=ALU.mult, op1=ALU.subtract)
                        lo(ckvT[:, 1, 640:KEYS], ps[:, 3, 2 * P:3 * P], ckvT[:, 0, 640:KEYS]).then_inc(cT_ready, 1)
                misc_lo_part(l, "Qb", 0)
                ve.wait_ge(qm_ps, l * 2 * NT + 2 * NT)
                ve.wait_ge(vz_done, l + 1)
                for s in SCHED:
                    if s[0] == "S":
                        _, g, i = s
                        kind = HEADS[g][0]
                        u = S_AT[s]
                        bk = 2 * (u % 2)
                        ve.wait_ge(s_ready, l * UNITS + u + 1)
                        if i == 4:
                            src = ps[:, bk, 0:P]
                        elif kind == "na":
                            w = (NA_M[i][1] - NA_M[i][0] + 1) * P
                            if i == 0:
                                ve.wait_ge(bias_ready, l * 4 + g + 1)
                            ve.tensor_tensor(ps[:, bk, 0:w], ps[:, bk, 0:w], bias_h[:, g % 2, NA_OFF[i]:NA_OFF[i] + w],
                                             ALU.add).then_inc(biased, 1)
                            ve.wait_ge(biased, l * 16 + 4 * g + i + 1)
                            src = ps[:, bk, 0:w + P]
                        else:
                            src = ps[:, bk:bk + 2, 0:HALF]
                        ve.tensor_reduce(negmax[:, u:u + 1], src, AX.XY if len(src.shape) == 3 else AX.X, ALU.max,
                                         negate=True).then_inc(max_ready, 1)
                        reciprocals(ve, l, u)
                    elif s[0] in ("T", "TP"):
                        n = T_AT[s]
                        if s[0] == "TP":
                            c0, c1 = 0, 2 * P
                        else:
                            a0, a1 = na_range(s[2]) if HEADS[s[1]][0] == "na" else (0, 3)
                            c0, c1 = a0 * P, (a1 + 1) * P
                        ve.wait_ge(pT_hi, l * TS + n + 1)
                        lo(pT[:, n % 2, 1, c0:c1], ps[:, 4 + n % 2, c0:c1], pT[:, n % 2, 0, c0:c1]).then_inc(pT_ready, 1)
                    elif s[0] in ("OL", "OP"):
                        o = PAIR_TILE[s[1]]
                        part, bank, c0, c1 = (0, 6, 0, LAT) if s[0] == "OL" else (1, 7, LAT, T)
                        ve.wait_ge(o_hi, l * 2 * NP + 2 * s[1] + part + 1)
                        lo(hT[:, o, 1, c0:c1], ps[:, bank, 0:c1 - c0], hT[:, o, 0, c0:c1]).then_inc(o_ready, 1)
                    elif s[0] == "C":
                        cached_keys(l, s[1])
                    elif s[0] == "M":
                        misc_lo_part(l, *s[1:])
                    elif s[0] == "WK":
                        ve.wait_ge(wqk_hi, 3 * l + 3)
                        lo(wkv[:, 1], wkv_raw[:], wkv[:, 0])
                        lo(ckvT[:, 1, LAT:640], kc_mla[:], ckvT[:, 0, LAT:640]).then_inc(wkv_ready, 1)
                    elif s[0] == "GS":
                        t = s[1]
                        ve.wait_ge(gsq, l * NT + t + 1)
                        ve.tensor_reduce(stat[:, t, 2:10], ztmp[:].rearrange("p (h d) -> p h d", h=8), AX.X, ALU.add).then_inc(gstat, 1)
                    elif s[0] == "GR":
                        ve.wait_ge(gstat, l * NT + NT)
                        ve.tensor_scalar(stat[:, :, 2:10], stat[:, :, 2:10], 1.0 / 64, EPS, ALU.mult, ALU.add).then_inc(cstat_ms, 1)
                    elif s[0] == "V":
                        g = s[1]
                        ve.wait_ge(v_hi, l * NV + v_at(g // 2) + 1)
                        for dst, src, hi in v_sources(g, 1):
                            i = lo(dst, src, hi)
                        i.then_inc(v_ready, 1)
                    elif s[0] == "GZ":
                        t = s[1]
                        zg = z[:, t, OFF_G:G_V].rearrange("p (h d) -> p h d", h=8)
                        if t == 0:
                            ve.wait_ge(cstat_rms, 2 * l + 2)
                            ve.reciprocal(stat[:, :, 2:10], stat[:, :, 2:10]).then_inc(cstat, 1)
                            ve.wait_ge(cstat, 2 * l + 2)
                        ve.tensor_tensor(zg, zg, stat[:, t, 2:10].unsqueeze(2).broadcast_to([P, 8, 64]), ALU.mult).then_inc(dve_own, 1)
                        ve.wait_ge(dve_own, l * NT + t + 1)
                        ve.tensor_tensor(z[:, t, OFF_G:G_V], z[:, t, OFF_G:G_V], g8[:], ALU.mult).then_inc(g_norm, 1)
                for o in range(KD):
                    ve.wait_ge(wo_hi, l * KD + o + 1)
                    lo(wo[:, o % 2, 1], wo_raw[:, o % 2], wo[:, o % 2, 0]).then_inc(wo_ready, 1)
                    if o >= 1:
                        residual(l, l * XD + o, o - 1, 2 + 2 * ((o - 1) % 3), 2)
                    if o >= 4:
                        add_square(l, 2 * l + 1, o - 3)

                def gate_lo(b):
                    ve.wait_ge(gw_hi, 2 * (l * FB + b) + 1)
                    lo(gw[:, 0, 1], gw_raw[:, 0], gw[:, 0, 0]).then_inc(gate_ready, 1)
                gate_lo(0)
                add_square(l, 2 * l + 1, 5)
                residual(l, l * XD + KD, KD - 1, 2 + 2 * ((KD - 1) % 3), 2)
                add_square(l, 2 * l + 1, 6)
                add_square(l, 2 * l + 1, 7)

                mean_square(2 * l + 2, ss_done, l + 1)
                modulated(l, 1)

                def ffn_block(b, last):
                    base = (l * FB + b) * 4
                    def gated(j, hf_):
                        ve.wait_ge(sl_ready, base + 2 * j + hf_ + 1)
                        ve.wait_ge(gu_ps, base * 2 + 4 * j + 2 + hf_ + 1)
                        ve.wait_ge(act_ready, base + (hf_ + 1 if j else 0) + 1)
                        ve.tensor_tensor(mm[:, hf_], sl[:, hf_], ps[:, 4 * j + 2 + hf_, 0:HALF], ALU.mult).then_inc(mm_ready, 1)

                    def act_lo(j, hf_):
                        ve.wait_ge(act_hi, base + 2 * j + hf_ + 1)
                        cols = slice(hf_ * HALF, (hf_ + 1) * HALF)
                        lo(act[:, j, 1, cols], mm[:, hf_], act[:, j, 0, cols]).then_inc(act_ready, 1)
                    for j in range(2):
                        gated(j, 0)
                        gated(j, 1)
                        act_lo(j, 0)
                        act_lo(j, 1)
                    for o in range(KD):
                        if o == 2 and not last:
                            gate_lo(b + 1)
                        residual(l, l * XD + KD + b * KD + o + 1, o, 2 * (o % 4), 5)

                with ve.Fori(0, FB - 1) as b:
                    ffn_block(b, False)
                ffn_block(FB - 1, True)
            for k in range(1, KD):
                add_square(DEPTH, 2 * DEPTH, k)
            mean_square(DEPTH * 2 + 1, ss_done, DEPTH + 1)
            ve.wait_ge(rstd_ready, DEPTH * 2 + 1)
            for k in range(KD):
                ve.scalar_tensor_tensor(out=x[:, k], in0=x[:, k], scalar=fin_g[:, k:k + 1], in1=rstd[:],
                                        op0=ALU.mult, op1=ALU.mult).then_inc(y_ready, 1)

        @block.gpsimd
        def _(po):
            def rotate(own, n, d, view, cos, sin, tmp):
                w = d // 4
                halves = view.rearrange("p h (a b w) -> p h a b w", a=2, b=2)
                s4 = sin.rearrange("p (a b w) -> p a b w", a=2, b=2)
                t4 = tmp.rearrange("p h (a b w) -> p h a b w", a=2, b=2)
                for b in range(2):
                    po.tensor_tensor(t4[:, :, :, b, :], halves[:, :, :, 1 - b, :],
                                     s4[:, :, b, :].unsqueeze(1).broadcast_to([P, n, 2, w]), ALU.mult).then_inc(pool_own, 1)
                po.wait_ge(pool_own, own + 2)
                po.tensor_tensor(view, view, cos.unsqueeze(1).broadcast_to([P, n, d]), ALU.mult).then_inc(pool_own, 1)
                po.wait_ge(pool_own, own + 3)
                return po.tensor_tensor(view, view, tmp, ALU.add)

            OWN = 3 * 12

            po.memset(ones[:], 1.0).then_inc(ones_set, 1)

            def modulated(base, n):
                po.wait_ge(rstd_ready, n)
                for k in range(KD):
                    if k >= 2:
                        po.wait_ge(hf_ready, base + k - 1)
                        po.wait_ge(h_hi, base + k - 1)
                    po.tensor_tensor(tn[:, k % 2], x[:, k], rstd[:], ALU.mult).then_inc(tn_ready, 1)

            def window(l, h):
                v = a["rpb"][l, h, :]
                src = bass.AP(tensor=v.tensor, offset=v.offset, ap=[[15, 16], [1, 8], [1, WIN]])
                po.dma_start(win[:, 0:WIN], src).then_inc(win_in, 16)

            def ada(l, t):
                w, arrived, count, n = pool_slot(t)
                po.wait_ge(arrived, count(l))
                if n:
                    po.wait_ge(product_summed, l * PSUMS + 2 * n - 1)
                settled(po, passed_po)
                po.tensor_tensor(product[:], w, silu_c[:, 0], ALU.mult).then_inc(product_ready, 1)
                po.wait_ge(product_ready, l * PSUMS + 2 * n + 1)
                po.tensor_tensor(w, w, silu_c[:, 1], ALU.mult).then_inc(product_ready, 1)

            with po.Fori(0, DEPTH) as l:
                po.wait_ge(silu_done, l + 1)
                for t in POOL_ADA1:
                    ada(l, t)
                modulated(l * 2 * KD, 2 * l + 1)
                for t in POOL_ADA2:
                    ada(l, t)
                po.wait_ge(z_done, l * IC * NT + IC * NT)
                window(l, 0)
                po.wait_ge(wi_ready, l * IC + IC)
                settled(po, passed_po)
                zeros = V[:, 0, 0, 0, 64:P].bitcast(F32)
                po.memset(bass.AP(tensor=zeros.tensor, offset=zeros.offset, ap=[list(zeros.ap[0]), [192, 24], [1, 64]]),
                          0.0).then_inc(vz_done, 1)
                turned = 0
                for s in SCHED:
                    if s[0] == "BM":
                        h = s[1]
                        po.wait_ge(win_in, 16 * (4 * l + h + 1))
                        if h >= 2:
                            po.wait_ge(max_ready, l * UNITS + 5 * (h - 1))
                        for n in range(4):
                            m0, m1 = NA_M[n]
                            cols = (m1 - m0 + 1) * 16
                            kc0 = 16 * (m0 - n) + 16
                            w = win[:]
                            src = bass.AP(tensor=w.tensor, offset=w.offset + WIN - 1 - 15 * kc0,
                                          ap=[list(w.ap[0]), [-15, cols], [-1, ROWS]])
                            c0 = NA_OFF[n]
                            i = po.tensor_tensor(bias_h[:, h % 2, c0:c0 + cols * ROWS].rearrange("p (c r) -> p c r", r=ROWS), src,
                                                 mask[:, c0 // ROWS:c0 // ROWS + cols].unsqueeze(2).broadcast_to([P, cols, ROWS]),
                                                 ALU.add)
                        i.then_inc(bias_ready, 1)
                        if h + 1 < 4:
                            po.wait_ge(bias_ready, l * 4 + h + 1)
                            window(l, h + 1)
                    elif s[0] in ("KR", "QR"):
                        t = s[1]
                        if t == 0 and s[0] == "KR":
                            po.wait_ge(kv_out, l * 64 + 64)
                        if t == 0 and s[0] == "QR":
                            po.wait_ge(qm_done, l * 2 * NT + 2 * NT)
                        if turned:
                            po.wait_ge(q_roped, l * 8 + turned)
                        if s[0] == "KR":
                            n, view = 1, z[:, t, OFF_KR:OFF_NA].unsqueeze(1)
                        else:
                            n, view = 6, qm[:, t, :].rearrange("p (h d) -> p h d", h=6)[:, :, 64:96]
                        tmp = rstd[:, 0:32 * n].rearrange("p (h d) -> p h d", h=n)
                        rotate(l * OWN + 3 * turned, n, 32, view, rope[:, t, 0, 64:96], rope[:, t, 1, 64:96],
                               tmp).then_inc(q_roped, 1)
                        turned += 1
                    elif s[0] == "S":
                        for u in in_flight(S_AT[s], 2):
                            norm_unit(po, "pool", l, u)
                    elif s[0] == "GZ" and s[1] < 4:
                        t = s[1]
                        po.wait_ge(g_norm, l * NT + t + 1)
                        view = z[:, t, OFF_G:G_V].rearrange("p (h d) -> p h d", h=8)
                        tmp = ztmp[:].rearrange("p (h d) -> p h d", h=8)
                        if t:
                            po.wait_ge(g_roped, l * 4 + t)
                        rotate(l * OWN + 24 + 3 * t, 8, 64, view, rope[:, t, 0, 0:64], rope[:, t, 1, 0:64], tmp).then_inc(g_roped, 1)
                        po.wait_ge(g_roped, l * 4 + t + 1)
                def up_lo(b):
                    po.wait_ge(gw_hi, 2 * (l * FB + b) + 2)
                    settled(po, passed_po)
                    po.tensor_tensor(gw[:, 1, 1], gw_raw[:, 1], gw[:, 1, 0].bitcast(F32), ALU.subtract).then_inc(up_ready, 1)

                def down_lo(b):
                    po.wait_ge(dw_hi, l * FB + b + 1)
                    settled(po, passed_po)
                    po.tensor_tensor(dw[:, 1], dw_raw[:], dw[:, 0].bitcast(F32), ALU.subtract).then_inc(dw_ready, 1)

                up_lo(0)
                modulated(l * 2 * KD + KD, 2 * l + 2)
                with po.Fori(0, FB - 1) as b:
                    down_lo(b)
                    up_lo(b + 1)
                down_lo(FB - 1)



def constants():
    import numpy as np
    t = np.arange(LAT)
    col, row = (t // ROWS).astype(np.float32), (t % ROWS).astype(np.float32)

    def table(d):
        ax = d // 2
        inv = np.float32(10000.0) ** (-np.arange(0, ax, 2, dtype=np.float32) / np.float32(ax))
        ar, ac = row[:, None] * inv, col[:, None] * inv
        ang = np.concatenate([ar, ar, ac, ac], axis=-1).astype(np.float32)
        sign = np.repeat(np.array([-1, 1, -1, 1], np.float32), d // 4)
        return np.cos(ang), np.sin(ang) * sign
    (cg, sg), (cm, sm) = table(64), table(32)
    rope = np.stack([np.concatenate([cg, cm], 1), np.concatenate([sg, sm], 1)], 1).reshape(4, P, 2, 96)
    rope = np.ascontiguousarray(rope.transpose(1, 0, 2, 3)).astype(np.float32)
    parts = []
    for n in range(4):
        m0, m1 = NA_M[n]
        q = 16 * n + np.arange(P) // ROWS
        k = np.arange(16 * m0, 16 * (m1 + 1))
        start = np.clip(q - 8, 0, GRID_W - 16)[:, None]
        parts.append(np.where((k >= start) & (k < start + 16), 0.0, -1e30))
    mask = np.concatenate(parts, 1).astype(np.float32)
    return rope, mask, np.eye(P, dtype=np.float32)


def kernel(**inputs):
    import numpy as np
    import concourse.bacc as bacc
    from concourse.bass_utils import run_bass_kernel_spmd as run

    g = {k: np.asarray(v) for k, v in inputs.items()}
    rope, mask, ident = constants()
    xs = g["x_sample"][0].reshape(ROWS, GRID_W, DM).transpose(1, 0, 2).reshape(LAT, DM)
    rpb = np.pad(g["na_rpb"].transpose(0, 1, 3, 2), ((0, 0), (0, 0), (16, 16), (0, 0)))
    rpb = rpb.reshape(DEPTH, 4, 63 * 15)[:, :, ::-1]
    feat = lambda v: v.reshape(*v.shape[:-1], -1, P)
    arrays = {
        "x": np.concatenate([xs, g["x_prompt"][0]], 0).T,
        "cond": np.stack([g["c"][0], g["c_ctx"]]),
        "b_ada": feat(g["b_ada"]).transpose(2, 0, 1),
        "norm_g": np.stack([feat(g["norm_mix_g"]), feat(g["norm_ffn_g"])], 1).transpose(3, 0, 1, 2),
        "fin_g": feat(g["final_norm_g"]).T,
        "qn_g": feat(g["mla_q_norm_g"]).transpose(2, 0, 1),
        "kv_g": g["mla_kv_norm_g"],
        "g8": np.concatenate([np.tile(g["gqa_q_norm_g"], (1, 6)), np.tile(g["gqa_k_norm_g"], (1, 2))], 1),
        "rope": rope, "mask": mask, "ident": ident,
        "ckvT": g["cache_mla_ckv"][0].transpose(0, 2, 1),
        "krT": g["cache_mla_krope"][0].transpose(0, 2, 1),
        "na_kT": g["cache_na_k"][0].transpose(0, 3, 2, 1),
        "g_kT": g["cache_gqa_k"][0].transpose(0, 3, 2, 1),
        "na_v": g["cache_na_v"][0].reshape(DEPTH, P, 256),
        "g_v": g["cache_gqa_v"][0].reshape(DEPTH, P, P),
        "rpb": rpb,
        "w_adaT": g["w_ada"].transpose(0, 2, 1), "w_in": g["w_in"], "w_q_up": g["w_q_up"], "w_kv_up": g["w_kv_up"],
        "w_out": g["w_out"], "w_gate": g["w_gate"], "w_up": g["w_up"], "w_down": g["w_down"],
    }
    outs = {"o_y": (DM, T), "o_ckv": (DEPTH, P, P), "o_kr": (DEPTH, P, 32), "o_nak": (DEPTH, P, 256),
            "o_nav": (DEPTH, P, 256), "o_gk": (DEPTH, P, P), "o_gv": (DEPTH, P, P)}
    nc = bacc.Bacc("TRN2", target_bir_lowering=False, num_devices=1)
    arrays = {k: np.ascontiguousarray(v) for k, v in arrays.items()}
    a = {k: nc.dram_tensor("in_" + k, v.shape, F32, kind="ExternalInput").ap() for k, v in arrays.items()}
    o = {k: nc.dram_tensor("out_" + k, s, F32, kind="ExternalOutput").ap() for k, s in outs.items()}
    build(nc, a, o)
    r = run(nc, [{"in_" + k: v for k, v in arrays.items()}], core_ids=[0]).results[0]
    y = r["out_o_y"].T
    ys = y[:LAT].reshape(GRID_W, ROWS, DM).transpose(1, 0, 2).reshape(1, LAT, DM)
    return (np.ascontiguousarray(y[LAT:])[None], np.ascontiguousarray(ys),
            r["out_o_ckv"][None], r["out_o_kr"][None], r["out_o_nak"].reshape(1, DEPTH, P, 4, 64),
            r["out_o_nav"].reshape(1, DEPTH, P, 4, 64), r["out_o_gk"].reshape(1, DEPTH, P, 2, 64),
            r["out_o_gv"].reshape(1, DEPTH, P, 2, 64))
```
